# Optimizing a Trainium2 kernel written in Bass

```python
import math
import jax, jax.numpy as jnp
from jax import lax
import numpy as np

D_MODEL = 1024
BATCH = 1
SEQ = 512
DEPTH = 1

N_HEADS_A = 8
HEAD_DIM = 64
WIDTH_A = N_HEADS_A * HEAD_DIM
IDX_HEADS = 8
IDX_DIM = 64
TOPK_MAX = 256
N_HEADS_B = 8
WIDTH_B = N_HEADS_B * HEAD_DIM
N_BUCKETS = 32
MAX_DISTANCE = 128
PEER_HEADS = 8
N_KEYS = 128
N_EXPERTS = N_KEYS * N_KEYS
PEER_QDIM = 256
PEER_HALF = PEER_QDIM // 2
PEER_TOPK = 16
Q_BLOCK = 128
TOK_CHUNK = 128
EPS = 1e-6
IN_SPLIT_SIZES = (WIDTH_A, WIDTH_A, WIDTH_A,
                  IDX_HEADS * IDX_DIM, IDX_DIM, IDX_HEADS,
                  WIDTH_B, WIDTH_B, WIDTH_B,
                  D_MODEL, D_MODEL)
IN_WIDTH = 3 * WIDTH_A + IDX_HEADS * IDX_DIM + IDX_DIM + IDX_HEADS + 3 * WIDTH_B + 2 * D_MODEL


def rmsnorm(x, g):
    xf = x.astype(jnp.float32)
    y = xf * lax.rsqrt(jnp.mean(xf * xf, axis=-1, keepdims=True) + EPS)
    return (y * g.astype(jnp.float32)).astype(x.dtype)

def modulate(h, shift, scale):
    return h * (1 + scale[:, None, :]) + shift[:, None, :]

def t5_bucket(n):
    max_exact = N_BUCKETS // 2
    nf = jnp.maximum(n, 1).astype(jnp.float32)
    large = max_exact + (jnp.log(nf / max_exact) / math.log(MAX_DISTANCE / max_exact)
                         * (N_BUCKETS - max_exact)).astype(jnp.int32)
    large = jnp.minimum(large, N_BUCKETS - 1)
    return jnp.where(n < max_exact, n, large)

def to_blocks(a, nblk):
    b = a.shape[0]
    return a.reshape(b, nblk, Q_BLOCK, *a.shape[2:]).swapaxes(0, 1)

def dsa_attention(q, k, v, qi, ki, wi, rel_bias):
    b, s, h, dh = q.shape
    topk = min(TOPK_MAX, s // 4)
    nblk = s // Q_BLOCK
    key_pos = jnp.arange(s)
    idx_scale = (IDX_DIM ** -0.5) * (IDX_HEADS ** -0.5)

    def one_block(args):
        blk, qb, qib, wib = args
        q_pos = blk * Q_BLOCK + jnp.arange(Q_BLOCK)
        rel = jax.nn.relu(jnp.einsum('bthd,bsd->bths', qib, ki))
        score = jnp.einsum('bths,bth->bts', rel, wib).astype(jnp.float32) * idx_scale
        causal = key_pos[None, :] <= q_pos[:, None]
        score = jnp.where(causal[None], score, -jnp.inf)
        top_score, idx = lax.top_k(score, topk)
        valid = jnp.isfinite(top_score)
        kg = jax.vmap(lambda kk, ii: kk[ii])(k, idx)
        vg = jax.vmap(lambda vv, ii: vv[ii])(v, idx)
        logits = jnp.einsum('bthd,btkhd->bhtk', qb, kg).astype(jnp.float32) * (dh ** -0.5)
        bias = rel_bias[t5_bucket(q_pos[None, :, None] - idx)].astype(jnp.float32)
        logits = logits + jnp.moveaxis(bias, -1, 1)
        logits = jnp.where(valid[:, None], logits, -jnp.inf)
        p = jax.nn.softmax(logits, axis=-1).astype(v.dtype)
        return jnp.einsum('bhtk,btkhd->bthd', p, vg)

    out = lax.map(one_block, (jnp.arange(nblk), to_blocks(q, nblk), to_blocks(qi, nblk), to_blocks(wi, nblk)))
    return out.swapaxes(0, 1).reshape(b, s, h * dh)

def stick_breaking_attention(q, k, v):
    b, s, h, dh = q.shape
    nblk = s // Q_BLOCK
    key_pos = jnp.arange(s)

    def one_block(args):
        blk, qb = args
        q_pos = blk * Q_BLOCK + jnp.arange(Q_BLOCK)
        z = jnp.einsum('bthd,bshd->bhts', qb, k).astype(jnp.float32) * (dh ** -0.5)
        strict = (key_pos[None, :] < q_pos[:, None])[None, None]
        log_beta = jax.nn.log_sigmoid(z)
        log_one_minus = jnp.where(strict, log_beta - z, 0.0)
        suffix = lax.cumsum(log_one_minus, axis=3, reverse=True) - log_one_minus
        a = jnp.where(strict, jnp.exp(log_beta + suffix), 0.0).astype(v.dtype)
        return jnp.einsum('bhts,bshd->bthd', a, v)

    out = lax.map(one_block, (jnp.arange(nblk), to_blocks(q, nblk)))
    return out.swapaxes(0, 1).reshape(b, s, h * dh)

def peer_ffn(h, w_q, sub_keys, u, v):
    t, d = h.shape
    qh = (h @ w_q).reshape(t, PEER_HEADS, 2, PEER_HALF)
    s = jnp.einsum('thcd,hcnd->thcn', qh, sub_keys).astype(jnp.float32)
    s1, i1 = lax.top_k(s[:, :, 0], PEER_TOPK)
    s2, i2 = lax.top_k(s[:, :, 1], PEER_TOPK)
    cand = (s1[..., :, None] + s2[..., None, :]).reshape(t, PEER_HEADS, PEER_TOPK * PEER_TOPK)
    cand_idx = (i1[..., :, None] * N_KEYS + i2[..., None, :]).reshape(t, PEER_HEADS, PEER_TOPK * PEER_TOPK)
    top_s, pos = lax.top_k(cand, PEER_TOPK)
    eidx = jnp.take_along_axis(cand_idx, pos, axis=-1)
    g = jax.nn.softmax(top_s, axis=-1)
    nchunk = t // TOK_CHUNK

    def one_chunk(args):
        hc, ec, gc = args
        pre = jnp.einsum('cd,chkd->chk', hc, u[ec]).astype(jnp.float32)
        coef = (gc * jax.nn.gelu(pre, approximate=False)).astype(h.dtype)
        return jnp.einsum('chk,chkd->cd', coef, v[ec])

    out = lax.map(one_chunk, (h.reshape(nchunk, TOK_CHUNK, d),
                              eidx.reshape(nchunk, TOK_CHUNK, PEER_HEADS, PEER_TOPK),
                              g.reshape(nchunk, TOK_CHUNK, PEER_HEADS, PEER_TOPK)))
    return out.reshape(t, d)

def first_inputs(seed: int = 0) -> dict:
    key = jax.random.key(seed)
    ks = jax.random.split(key, 20)
    D = D_MODEL
    nrm = jax.random.normal
    x = nrm(ks[0], (BATCH, SEQ, D), jnp.float32)
    c = nrm(ks[1], (BATCH, D), jnp.float32)
    w_ada = nrm(ks[2], (DEPTH, D, 6 * D), jnp.float32) * (0.5 * D ** -0.5)
    b_ada = nrm(ks[3], (DEPTH, 6 * D), jnp.float32) * 0.01
    norm1_g = 1.0 + 0.05 * nrm(ks[4], (DEPTH, D), jnp.float32)
    norm2_g = 1.0 + 0.05 * nrm(ks[5], (DEPTH, D), jnp.float32)
    w_in = nrm(ks[6], (DEPTH, D, IN_WIDTH), jnp.float32) * D ** -0.5
    rel_bias = nrm(ks[7], (N_BUCKETS, N_HEADS_A), jnp.float32) * 0.5
    w_proj_a = nrm(ks[8], (DEPTH, WIDTH_A, D), jnp.float32) * WIDTH_A ** -0.5
    w_proj_b = nrm(ks[9], (DEPTH, WIDTH_B, D), jnp.float32) * WIDTH_B ** -0.5
    w_out = nrm(ks[10], (DEPTH, D, D), jnp.float32) * D ** -0.5
    peer_wq = nrm(ks[11], (DEPTH, D, PEER_HEADS * PEER_QDIM), jnp.float32) * D ** -0.5
    peer_sub_keys = nrm(ks[12], (DEPTH, PEER_HEADS, 2, N_KEYS, PEER_HALF), jnp.float32) * PEER_HALF ** -0.5
    peer_u = nrm(ks[13], (DEPTH, N_EXPERTS, D), jnp.float32) * D ** -0.5
    peer_v = nrm(ks[14], (DEPTH, N_EXPERTS, D), jnp.float32) * PEER_HEADS ** -0.5
    final_g = 1.0 + 0.05 * nrm(ks[15], (D,), jnp.float32)
    return {"x": x, "c": c, "w_ada": w_ada, "b_ada": b_ada, "norm1_g": norm1_g, "norm2_g": norm2_g,
            "w_in": w_in, "rel_bias": rel_bias, "w_proj_a": w_proj_a, "w_proj_b": w_proj_b,
            "w_out": w_out, "peer_wq": peer_wq, "peer_sub_keys": peer_sub_keys, "peer_u": peer_u,
            "peer_v": peer_v, "final_g": final_g}

def first_block(x, c, w_ada, b_ada, norm1_g, norm2_g, w_in, rel_bias, w_proj_a, w_proj_b, w_out,
              peer_wq, peer_sub_keys, peer_u, peer_v, final_g):
    b, s, d = x.shape
    offsets = []
    acc = 0
    for size in IN_SPLIT_SIZES[:-1]:
        acc += size
        offsets.append(acc)
    cond = jax.nn.silu(c)
    for l in range(DEPTH):
        mod = (cond @ w_ada[l] + b_ada[l]).reshape(b, 6, d)
        shift1, scale1, gate1, shift2, scale2, gate2 = [mod[:, i] for i in range(6)]

        hn = modulate(rmsnorm(x, norm1_g[l]), shift1, scale1)
        proj = hn @ w_in[l]
        qa, ka, va, qi, ki, wi, qb, kb, vb, ga, gb = jnp.split(proj, offsets, axis=-1)
        hd = (b, s, -1, HEAD_DIM)
        ya = dsa_attention(qa.reshape(hd), ka.reshape(hd), va.reshape(hd),
                           qi.reshape(b, s, IDX_HEADS, IDX_DIM), ki, wi, rel_bias)
        yb = stick_breaking_attention(qb.reshape(hd), kb.reshape(hd), vb.reshape(hd))
        merged = jax.nn.sigmoid(ga) * (ya @ w_proj_a[l]) + jax.nn.sigmoid(gb) * (yb @ w_proj_b[l])
        x = x + gate1[:, None, :] * (merged @ w_out[l])

        hn2 = modulate(rmsnorm(x, norm2_g[l]), shift2, scale2)
        f = peer_ffn(hn2.reshape(b * s, d), peer_wq[l], peer_sub_keys[l], peer_u[l], peer_v[l]).reshape(b, s, d)
        x = x + gate2[:, None, :] * f
    return rmsnorm(x, final_g)


CHUNK = 64
N_META = 16
D_MIX = D_MODEL
D_ATTN = D_MIX // 2
N_HEADS = D_ATTN // HEAD_DIM
D_POOL = D_MIX - D_ATTN
POOL_WINDOWS = (2, 4, 8, 16)
N_POOL_GROUPS = len(POOL_WINDOWS)
POOL_GROUP_DIM = D_POOL // N_POOL_GROUPS
D_IN = 3 * D_ATTN + N_HEADS + D_POOL
D_FF = ((8 * D_MODEL + 3 * 256 - 1) // (3 * 256)) * 256


def _rmsnorm(x, w):
    x32 = x.astype(jnp.float32)
    y = x32 * lax.rsqrt(jnp.mean(x32 * x32, axis=-1, keepdims=True) + EPS)
    return (y * w.astype(jnp.float32)).astype(x.dtype)

def _forgetting_attention(q, k, v, cum_logf):
    L = q.shape[2]
    scale = HEAD_DIM ** -0.5
    outs = []
    for q0 in range(0, L, Q_BLOCK):
        q1 = min(q0 + Q_BLOCK, L)
        qb = q[:, :, q0:q1]
        kp = k[:, :, :q1]
        vp = v[:, :, :q1]
        s = jnp.einsum("bhqd,bhkd->bhqk", qb, kp).astype(jnp.float32) * scale
        s = s + (cum_logf[:, :, q0:q1, None] - cum_logf[:, :, None, :q1])
        t_idx = jnp.arange(q0, q1)[:, None]
        s_idx = jnp.arange(q1)[None, :]
        s = jnp.where(s_idx <= t_idx, s, -jnp.inf)
        p = jax.nn.softmax(s, axis=-1).astype(v.dtype)
        outs.append(jnp.einsum("bhqk,bhkd->bhqd", p, vp))
    return jnp.concatenate(outs, axis=2)

def _trailing_mean_minus_self(u, window):
    L = u.shape[1]
    cs = jnp.concatenate([jnp.zeros_like(u[:, :1]), jnp.cumsum(u, axis=1)], axis=1)
    t = jnp.arange(L)
    lo = jnp.maximum(t + 1 - window, 0)
    total = cs[:, 1:] - cs[:, lo]
    count = (t + 1 - lo).astype(jnp.float32)[None, :, None]
    return total / count - u

def _layer(h, norm1_w, w_in, b_fgate, q_norm_w, k_norm_w, w_pool, pool_scale,
           w_out, norm2_w, w_gate, w_up, w_down):
    B, L, _ = h.shape
    n1 = _rmsnorm(h, norm1_w)
    proj = n1 @ w_in.astype(h.dtype)
    q, k, v, fg, u = jnp.split(
        proj, [D_ATTN, 2 * D_ATTN, 3 * D_ATTN, 3 * D_ATTN + N_HEADS], axis=-1)

    q = _rmsnorm(q.reshape(B, L, N_HEADS, HEAD_DIM), q_norm_w).transpose(0, 2, 1, 3)
    k = _rmsnorm(k.reshape(B, L, N_HEADS, HEAD_DIM), k_norm_w).transpose(0, 2, 1, 3)
    v = v.reshape(B, L, N_HEADS, HEAD_DIM).transpose(0, 2, 1, 3)
    log_f = jax.nn.log_sigmoid((fg + b_fgate.astype(fg.dtype)).astype(jnp.float32))
    cum_logf = jnp.cumsum(log_f.transpose(0, 2, 1), axis=-1)
    a_out = _forgetting_attention(q, k, v, cum_logf)
    a_out = a_out.transpose(0, 2, 1, 3).reshape(B, L, D_ATTN)

    u32 = u.astype(jnp.float32)
    pooled = jnp.stack(
        [_trailing_mean_minus_self(u32[..., g * POOL_GROUP_DIM:(g + 1) * POOL_GROUP_DIM], w)
         for g, w in enumerate(POOL_WINDOWS)], axis=2).astype(h.dtype)
    p_out = jnp.einsum("blgc,gcd->blgd", pooled, w_pool.astype(h.dtype)).reshape(B, L, D_POOL)
    p_out = p_out * pool_scale.astype(h.dtype)

    mix = jnp.concatenate([a_out, p_out], axis=-1) @ w_out.astype(h.dtype)
    h = h + mix

    n2 = _rmsnorm(h, norm2_w)
    ffn = (jax.nn.silu(n2 @ w_gate.astype(h.dtype)) * (n2 @ w_up.astype(h.dtype))) @ w_down.astype(h.dtype)
    return h + ffn

def second_inputs(seed: int = 0) -> dict:
    key = jax.random.key(seed)
    ks = jax.random.split(key, 16)
    x = jax.random.normal(ks[0], (BATCH, SEQ, D_MODEL), jnp.float32)
    meta_tokens = jax.random.normal(ks[1], (N_META, D_MODEL), jnp.float32)
    norm1_w = 1.0 + 0.05 * jax.random.normal(ks[2], (DEPTH, D_MODEL), jnp.float32)
    w_in = jax.random.normal(ks[3], (DEPTH, D_MODEL, D_IN), jnp.float32) * D_MODEL ** -0.5
    w_in = w_in.at[:, :, 3 * D_ATTN:3 * D_ATTN + N_HEADS].multiply(0.1)
    b_fgate = 2.0 + 2.0 * jax.random.uniform(ks[4], (DEPTH, N_HEADS), jnp.float32)
    q_norm_w = 1.0 + 0.05 * jax.random.normal(ks[5], (DEPTH, HEAD_DIM), jnp.float32)
    k_norm_w = 1.0 + 0.05 * jax.random.normal(ks[6], (DEPTH, HEAD_DIM), jnp.float32)
    w_pool = jax.random.normal(ks[7], (DEPTH, N_POOL_GROUPS, POOL_GROUP_DIM, POOL_GROUP_DIM),
                               jnp.float32) * POOL_GROUP_DIM ** -0.5
    pool_scale = 1.0 + 0.1 * jax.random.normal(ks[8], (DEPTH, D_POOL), jnp.float32)
    w_out = jax.random.normal(ks[9], (DEPTH, D_MIX, D_MODEL), jnp.float32) * D_MIX ** -0.5
    norm2_w = 1.0 + 0.05 * jax.random.normal(ks[10], (DEPTH, D_MODEL), jnp.float32)
    w_gate = jax.random.normal(ks[11], (DEPTH, D_MODEL, D_FF), jnp.float32) * D_MODEL ** -0.5
    w_up = jax.random.normal(ks[12], (DEPTH, D_MODEL, D_FF), jnp.float32) * D_MODEL ** -0.5
    w_down = jax.random.normal(ks[13], (DEPTH, D_FF, D_MODEL), jnp.float32) * D_FF ** -0.5
    return {"x": x, "meta_tokens": meta_tokens, "norm1_w": norm1_w, "w_in": w_in,
            "b_fgate": b_fgate, "q_norm_w": q_norm_w, "k_norm_w": k_norm_w,
            "w_pool": w_pool, "pool_scale": pool_scale, "w_out": w_out,
            "norm2_w": norm2_w, "w_gate": w_gate, "w_up": w_up, "w_down": w_down}

def second_block(x, meta_tokens, norm1_w, w_in, b_fgate, q_norm_w, k_norm_w, w_pool,
              pool_scale, w_out, norm2_w, w_gate, w_up, w_down):
    B = x.shape[0]
    meta = jnp.broadcast_to(meta_tokens.astype(x.dtype)[None], (B, N_META, D_MODEL))
    h = jnp.concatenate([meta, x], axis=1)
    for layer in range(DEPTH):
        h = _layer(h, norm1_w[layer], w_in[layer], b_fgate[layer], q_norm_w[layer],
                   k_norm_w[layer], w_pool[layer], pool_scale[layer], w_out[layer],
                   norm2_w[layer], w_gate[layer], w_up[layer], w_down[layer])
    return h[:, N_META:]


def setup_inputs(seed=0):
    out = dict(first_inputs(seed))
    for name, value in second_inputs(seed + 1).items():
        if name != "x":
            out[name + "_2"] = value
    return out


def reference(
    x, c, w_ada, b_ada, norm1_g, norm2_g, w_in, rel_bias, w_proj_a, w_proj_b, w_out, peer_wq,
    peer_sub_keys, peer_u, peer_v, final_g, meta_tokens_2, norm1_w_2, w_in_2, b_fgate_2,
    q_norm_w_2, k_norm_w_2, w_pool_2, pool_scale_2, w_out_2, norm2_w_2, w_gate_2, w_up_2,
    w_down_2,
):
    x = first_block(
        x, c, w_ada, b_ada, norm1_g, norm2_g, w_in, rel_bias, w_proj_a, w_proj_b, w_out,
        peer_wq, peer_sub_keys, peer_u, peer_v, final_g,
    )
    return second_block(
        x, meta_tokens_2, norm1_w_2, w_in_2, b_fgate_2, q_norm_w_2, k_norm_w_2, w_pool_2,
        pool_scale_2, w_out_2, norm2_w_2, w_gate_2, w_up_2, w_down_2,
    )


_drawn_inputs = setup_inputs


def setup_inputs(seed=0):
    import zlib

    import numpy as np

    out = dict(_drawn_inputs(seed))
    spreads = {}
    factors = {'b_ada': 5.187,
     'norm1_g': 4.415,
     'norm2_g': 3.623,
     'rel_bias': 3.854,
     'q_norm_w_2': 6.209,
     'k_norm_w_2': 8.0}
    for name, (base, spread) in spreads.items():
        noise = np.random.default_rng([zlib.crc32(name.encode()), seed]).standard_normal(out[name].shape)
        drawn = base * np.exp(spread * noise) if base else spread * noise
        out[name] = __import__('jax').numpy.asarray(drawn.astype(out[name].dtype))
    for name, factor in factors.items():
        out[name] = (out[name] * factor).astype(out[name].dtype)
    return out
```

```python
import concourse.bass as bass
from concourse import mybir
from contextlib import ExitStack, contextmanager

P = 128
D = 1024
KT = D // P
T = 512
TT = T // P
META = 16
L2 = META + T
NH, DH = 8, 64
HP = NH // 2
TOPK = 128
BUCKETS = 32
REL = T + P - 1
PH, NK, PK = 8, 128, 16
ADA = 6 * D // P
FF = 2816 // P
EPS = 1e-6
GATED, TAKEN = -1e30, -3e38
SLOTS = 4
G, GS = 2, 4
GROUPS = PK // G
BEST_AFTER = 2
IDX_SCALE = 64 ** -0.5 * 8 ** -0.5

B_ADA, G1, G2, GF, N1, N2, QN, PS, BF = 0, 48, 56, 64, 72, 80, 88, 90, 94
SMALL = 96

S_QK, S_KI, S_WI, S_V, S_GATE = 0, 20, 21, 22, 30
S_PROJ, S_OUT, S_WQ = 46, 54, 62
S_IN2, S_V2, S_FG, S_POOL, S_OUT2, S_UP, S_DOWN = 78, 90, 94, 95, 96, 104, 148
TILES = 172


V_QK, V_KI, V_WI, V_PROJ, V_OUT, V_IN2, V_V2, V_POOL, V_OUT2, V_UP = 0, 20, 21, 22, 30, 38, 50, 54, 55, 63
A_V, A_GATE, A_WQ = 0, 8, 24

SQ0, MS = [0, 8, 16, 24, 40], [0, 1, 2, 3, 12]


class Signal:
    CREDIT = 4

    def __init__(self, sem):
        self.sem = sem

    def ready(self, n):
        return n + 1 + self.CREDIT

    def free(self, n, depth):
        return n + 1 + self.CREDIT - depth


class Steps:

    def __init__(self, eng, sem):
        self.eng, self.sem, self.n, self.shift = eng, sem, 0, 0

    def __call__(self, instruction):
        instruction.then_inc(self.sem, 1)
        self.n += 1

    def wait(self):
        self.eng.wait_ge(self.sem, self.shift + self.n)

    @contextmanager
    def loop(self, count, per):
        with self.eng.Fori(0, count) as i:
            base, shift = self.n, self.shift
            self.shift = shift + i * per
            yield i
            assert self.n - base == per, (self.n - base, per)
        self.n, self.shift = base + per * count, shift


def program(nc, xT, metaT, cond, w_ada, small, onehot, rel_bias, w_stream, sub_keys, experts, outT):
    f32, u32 = mybir.dt.float32, mybir.dt.uint32
    ALU, ACT, AX = mybir.AluOpType, mybir.ActivationFunctionType, mybir.AxisListType.X
    rel_dram = nc.dram_tensor("rel_rows", (NH, REL + 1), f32, kind="Internal").ap()

    ctx = ExitStack()
    with ctx:
        def sb(name, shape, dtype=f32):
            return ctx.enter_context(nc.sbuf_tensor(name, shape, dtype))

        def sem(name):
            return ctx.enter_context(nc.semaphore(name))

        x = sb("x", [P, KT, L2])
        hn = sb("hn", [P, KT, L2])
        ring = sb("ring", [P, SLOTS, D])
        vec = sb("vec", [P, SMALL])
        mod = sb("mod", [P, ADA])
        gain1 = sb("gain1", [P, KT])
        gain2 = sb("gain2", [P, KT])
        ident = sb("ident", [P, P])
        ones = sb("ones", [P, P])
        neg_ones = sb("neg_ones", [P, P])
        neg_tri = sb("neg_tri", [P, P])
        half_ones = sb("half_ones", [P, P])
        causal = sb("causal", [P, P])
        strict = sb("strict", [P, P])
        sq = sb("sq", [P, 2, L2])
        rstd = sb("rstd", [P, L2])
        col = sb("col", [P, 16])
        rel_sb = sb("rel_sb", [BUCKETS, NH])

        ARENA = 36300
        arena = sb("arena", [P, ARENA])
        used = [0]

        def take(*shape):
            n = 1
            for s in shape:
                n *= s
            a = arena[:, used[0]:used[0] + n]
            used[0] += n
            assert used[0] <= ARENA, used[0]
            if len(shape) == 2:
                a = a.rearrange("p (a b) -> p a b", b=shape[1])
            if len(shape) == 3:
                a = a.rearrange("p (a b c) -> p a b c", b=shape[1], c=shape[2])
            return a

        qk = take(20, T)
        QI, KA, QA, KB, QB = 0, 4, 8, 12, 16
        ki = take(T)
        wi = take(TT, NH)
        v = take(TT, 2 * NH * DH)
        gates = take(16, T)
        y = take(8, T)
        mask = [take(P * (i + 1)) for i in range(TT)]
        stage = [take(T) for _ in range(2)]
        stage_v = take(TT, P)
        work = used[0]
        bias = take(NH, T)
        logit = [take(T) for _ in range(2)]
        probT = [take(TT, P) for _ in range(2)]
        onehot_sb = bias[:, 0:2, :].rearrange("p a b -> p (a b)")[0:BUCKETS, 0:REL]
        used[0] = work
        used[0] += NH * T
        relu_all = take(2 * T)
        relu = [relu_all[:, 0:T], relu_all[:, T:2 * T]]
        score = take(T)
        rel_row = relu_all[0:NH, 0:REL]
        used[0] = work
        stage_h = [take(T) for _ in range(2)]
        sp = [take(T - P * i) for i in range(TT)]
        az = [take(T - P * i) for i in range(TT)]
        used[0] = 20 * T + T + TT * NH + TT * 2 * NH * DH + 16 * T
        ada = take(SLOTS, D)
        cvec = take(D)
        used[0] = work + NH * T + 2 * T
        junk_ada = take(D)
        used[0] = 0
        sc = take(TT, 16, NK)
        keys = take(16, NK)
        qh = [take(T) for _ in range(2)]
        h_tok = take(TT, D)
        h_cur = take(D)
        rows = take(GS, G, 2 * D)
        acc = take(D)
        diag = take(GS, G * P)
        eidx = sb("eidx", [P, 2, P], u32)
        eslot = sb("eslot", [P, GS, G], u32)
        wgt = take(2, P)
        pre = take(GS, G)
        coef = take(GS, G)
        half = take(2, NK)
        top = take(2, PK)
        topf = take(2, PK)
        cand = take(PK, PK)
        best = take(PK)
        posf = take(2, PK)
        hot = take(2, PK * PK)
        iota16 = sb("iota16", [P, PK])
        epart = take(2, PK)
        topi = sb("topi", [P, 2, PK], u32)
        pos = sb("pos", [P, PK], u32)
        pos2 = sb("pos2", [P, 2, PK], u32)
        used[0] = 0
        big = take(12, L2)
        v2 = take(TT + 1, NH * DH)
        lf = take(L2)
        lf2 = take(L2)
        cum = take(L2)
        cum_tok = take(TT, NH)
        cum_row = take(NH, L2)
        mix = take(8, T)
        stage2 = [take(L2) for _ in range(2)]
        stage2_v = take(TT + 1, P)
        logit2 = [take(L2) for _ in range(2)]
        probT2 = [take(TT + 1, P) for _ in range(2)]
        pool_a = take(L2)
        pool_b = take(L2)
        pooled = take(4, T)
        used[0] = 0
        act_ff = take(FF, T)
        silu = [take(T) for _ in range(2)]
        outb = take(KT, T)

        psum = ctx.enter_context(nc.psum_tensor("psum", [P, 8 * 512], f32))

        def bank(b, width=512, start=0):
            return psum[:, b * 512 + start:b * 512 + start + width]

        def seam(b, width=L2):
            return psum[:, (b + 1) * 512 - META:(b + 1) * 512 - META + width]

        zs_all = [bank(2), bank(3, 384), bank(4, 256), bank(3, 128, 384)]
        us_all = [bank(5), bank(7), bank(5), bank(7)]

        ring_ready = [sem(f"ring_ready{i}") for i in range(SLOTS)]
        x_loaded, vec_loaded, meta_loaded, cond_loaded = (sem(n) for n in (
            "x_loaded", "vec_loaded", "meta_loaded", "cond_loaded"))
        onehot_loaded, rel_stored, bias_loaded, keys_loaded = (sem(n) for n in (
            "onehot_loaded", "rel_stored", "bias_loaded", "keys_loaded"))
        ada_ready = [sem(f"ada_ready{i}") for i in range(SLOTS)]
        rows_ready = [sem(f"rows_ready{i}") for i in range(GS)]
        out_stored = sem("out_stored")
        consts_done = sem("consts_done")

        signals = {"pe": [], "act": [], "dve": [], "pool": []}

        def signal(engine, name):
            s = Signal(sem(name))
            signals[engine].append(s)
            return s

        tile_done = signal("pe", "tile_done")
        ada_used = signal("dve", "ada_used")
        cond_done = signal("act", "cond_done")
        sq_ready = signal("act", "sq_ready")
        sq_used = signal("pe", "sq_used")
        root_ready = signal("act", "root_ready")
        ms_ready = signal("dve", "ms_ready")
        hn_ready = signal("dve", "hn_ready")
        x_ready = signal("dve", "x_ready")
        dense_dve = signal("dve", "dense_dve")
        dense_act = signal("act", "dense_act")
        rel_done = signal("pe", "rel_done")
        rel_copied = signal("dve", "rel_copied")
        idx_done = signal("pe", "idx_done")
        relu_done = signal("act", "relu_done")
        relu_used = signal("dve", "relu_used")
        score_done = signal("dve", "score_done")
        score_gated = signal("pool", "score_gated")
        staged = signal("dve", "staged")
        s_done = signal("pe", "s_done")
        s_taken = signal("dve", "s_taken")
        exp_done = signal("act", "exp_done")
        p_done = signal("dve", "p_done")
        t_done = signal("pe", "t_done")
        t_taken = signal("act", "t_taken")
        pv_done = signal("pe", "pv_done")
        y_taken = signal("dve", "y_taken")
        z_done = signal("pe", "z_done")
        soft_done = signal("act", "soft_done")
        sp_done = signal("dve", "sp_done")
        sp_gated = signal("pool", "sp_gated")
        u_done = signal("pe", "u_done")
        half_zeroed = signal("pool", "half_zeroed")
        a_done = signal("act", "a_done")
        yb_done = signal("pe", "yb_done")
        yb_taken = signal("dve", "yb_taken")
        gates_done = signal("act", "gates_done")
        key_done = signal("pe", "key_done")
        key_taken = signal("act", "key_taken")
        htok_done = signal("pe", "htok_done")
        htok_taken = signal("act", "htok_taken")
        idx_ready = signal("dve", "idx_ready")
        eslot_done = signal("pool", "eslot_done")
        best_done = signal("dve", "best_done")
        best_exp = signal("act", "best_exp")
        pre_done = signal("dve", "pre_done")
        gelu_done = signal("act", "gelu_done")
        coef_done = signal("dve", "coef_done")
        diag_done = signal("act", "diag_done")
        rows_used = signal("pe", "rows_used")
        acc_done = signal("act", "acc_done")
        f_done = signal("pe", "f_done")
        f_taken = signal("dve", "f_taken")
        fg_done = signal("dve", "fg_done")
        fg_exp = signal("act", "fg_exp")
        cum_done = signal("dve", "cum_done")
        cumt_done = signal("pe", "cumt_done")
        cumr_done = signal("pe", "cumr_done")
        cumr_taken = signal("act", "cumr_taken")
        pooled_done = signal("dve", "pooled_done")
        up_silu = signal("act", "up_silu")
        o_ready = signal("dve", "o_ready")
        cum_pick = [ident[0:NH, h:h + 1].to_broadcast([NH, P]) for h in range(NH)]
        own = {e: sem(f"{e}_step") for e in ("act", "dve", "pool")}
        held = {e: sem(f"{e}_held") for e in ("act", "dve", "pool", "pe")}

        def start(eng, name):
            for s in signals[name]:
                eng.sem_inc(s.sem, Signal.CREDIT)

        def tell(eng, steps, s):
            steps.wait()
            eng.sem_inc(s.sem, 1)

        block = ctx.enter_context(nc.Block())

        @block.sync
        def _(sp_eng):
            eng = sp_eng
            eng.dma_start(x[:, :, META:], xT.rearrange("(k p) t -> p k t", p=P)).then_inc(x_loaded, 16)
            eng.dma_start(vec[:], small).then_inc(vec_loaded, 16)
            for j in range(SLOTS):
                eng.dma_start(ring[:, j, :], w_stream[j]).then_inc(ring_ready[j], 16)
            eng.dma_start(x[:, :, 0:META], metaT.rearrange("(k p) t -> p k t", p=P))\
               .then_inc(meta_loaded, 16)
            with eng.Fori(0, TILES // SLOTS - 1) as q:
                for j in range(SLOTS):
                    eng.wait_ge(tile_done.sem, tile_done.ready(q * SLOTS + j))
                    eng.dma_start(ring[:, j, :], w_stream[(q + 1) * SLOTS + j]).then_inc(ring_ready[j], 16)
            for m in range(KT):
                eng.wait_ge(o_ready.sem, o_ready.ready(m))
                eng.dma_start(outT[m * P:(m + 1) * P, :], outb[:, m, :]).then_inc(out_stored, 16)
            eng.wait_ge(out_stored, 16 * KT)

        @block.tensor
        def _(pe):
            mm = nc.tensor.matmul
            start(pe, "pe")

            def tile(t0, j, q=0, per=0):
                n = t0 + j
                pe.wait_ge(ring_ready[n % SLOTS], 16 * (n // SLOTS + 1) + q * (16 * per // SLOTS))
                return ring[:, n % SLOTS, :].rearrange("p (k m) -> p k m", m=P)

            def norm(c, with_meta):
                for k in range(KT):
                    pe.wait_ge(sq_ready.sem, sq_ready.ready(SQ0[c] + k))
                    if k == 0 and c:
                        pe.wait_ge(ms_ready.sem, ms_ready.ready(MS[c] - 1))
                    if with_meta:
                        mm(seam(2, META), ones[:], sq[:, k % 2, 0:META], start=k == 0, stop=k == KT - 1)
                    mm(bank(3), ones[:], sq[:, k % 2, META:], start=k == 0, stop=k == KT - 1)\
                        .then_inc(sq_used.sem, 1)

            def dense(out, w, rhs):
                for k in range(w.shape[1]):
                    last = mm(out, w[:, k, :], rhs[:, k, :], start=k == 0, stop=k == w.shape[1] - 1)
                return last

            pe.wait_ge(consts_done, 1)
            pe.wait_ge(onehot_loaded, 32)
            for a in range(2):
                w = min(512, REL - a * 512)
                last = mm(bank(4 + a, w)[0:NH, :], rel_sb[:], onehot_sb[:, a * 512:a * 512 + w], start=True, stop=True)
            last.then_inc(rel_done.sem, 1)
            norm(0, False)
            rhs = hn[:, :, META:]
            pe.wait_ge(hn_ready.sem, hn_ready.ready(0))
            with pe.Fori(0, 5) as q:
                for j in range(4):
                    w = tile(S_QK, j, q, 4)
                    pe.wait_ge(dense_dve.sem, dense_dve.free(q * 4 + j, 2))
                    dense(bank(j % 2), w, rhs).then_inc(tile_done.sem, 1)
            w = tile(S_KI, 0)
            pe.wait_ge(dense_dve.sem, dense_dve.free(V_KI, 2))
            dense(bank(0), w, rhs).then_inc(tile_done.sem, 1)
            w = tile(S_WI, 0)
            pe.wait_ge(dense_dve.sem, dense_dve.free(V_WI, 2))
            for i in range(TT):
                for k in range(KT):
                    last = mm(bank(1, NH, i * NH), hn[:, k, META + i * P:META + (i + 1) * P], w[:, k, 0:NH],
                              start=k == 0, stop=k == KT - 1)
            last.then_inc(tile_done.sem, 1)
            pe.wait_ge(dense_dve.sem, dense_dve.ready(V_KI))
            n = 0
            for i in range(1, TT):
                for h in range(NH):
                    pe.wait_ge(relu_done.sem, relu_done.free(n, 2))
                    r = slice(64 * (h % 2), 64 * (h % 2) + 64)
                    mm(bank(4 + n % 2, P * (i + 1)), qk[r, QI + h // 2, i * P:(i + 1) * P],
                       ki[r, 0:P * (i + 1)], start=True, stop=True).then_inc(idx_done.sem, 1)
                    n += 1

            pe.wait_ge(dense_dve.sem, dense_dve.ready(V_WI))
            with pe.Fori(0, 2) as q:
                for j in range(4):
                    w = tile(S_V, j, q, 4)
                    pe.wait_ge(dense_act.sem, dense_act.free(A_V + q * 4 + j, 2))
                    for i in range(TT):
                        for k in range(KT):
                            last = mm(bank(j % 2, P, i * P), hn[:, k, META + i * P:META + (i + 1) * P],
                                      w[:, k, :], start=k == 0, stop=k == KT - 1)
                    last.then_inc(tile_done.sem, 1)

            units = [(e, i) for e in range(2) for i in range(TT)]
            U = len(units)

            pe.wait_ge(relu_done.sem, relu_done.ready(23))
            with pe.Fori(0, HP) as q:
                pe.wait_ge(staged.sem, staged.ready(q))
                for u in range(U + 1):
                    if u < U:
                        e, i = units[u]
                        r = slice(64 * e, 64 * e + 64)
                        pe.wait_ge(s_taken.sem, s_taken.free(q * U + u, 2))
                        mm(bank(2 + u % 2, P * (i + 1)), stage[0][r, i * P:(i + 1) * P],
                           stage[1][r, 0:P * (i + 1)], start=True, stop=True).then_inc(s_done.sem, 1)
                    if u % 2 == 1:
                        w = tile(S_GATE, u // 2, q, 4)
                        pe.wait_ge(dense_act.sem, dense_act.free(A_GATE + q * 4 + u // 2, 2))
                        dense(bank(u // 2 % 2), w, rhs).then_inc(tile_done.sem, 1)
                    if u >= 1:
                        w = u - 1
                        e, i = units[w]
                        pe.wait_ge(p_done.sem, p_done.ready(q * U + w))
                        pe.wait_ge(t_taken.sem, t_taken.free(q * U + w, 2))
                        for j in range(i + 1):
                            last = nc.tensor.transpose(bank(4 + w % 2, P, j * P),
                                                       logit[w % 2][:, j * P:(j + 1) * P], ident[:])
                        last.then_inc(t_done.sem, 1)
                        if w == 0:
                            pe.wait_ge(y_taken.sem, y_taken.free(q, 1))
                        pe.wait_ge(t_taken.sem, t_taken.ready(q * U + w))
                        for j in range(i + 1):
                            last = mm(bank(6, P, i * P)[64 * e:64 * e + 64, :], stage_v[:, j, 64 * e:64 * e + 64],
                                      probT[w % 2][:, j, :], start=j == 0, stop=j == i)
                        last.then_inc(pv_done.sem, 1)

            pe.wait_ge(y_taken.sem, y_taken.ready(HP - 1))
            with pe.Fori(0, HP) as q:
                pe.wait_ge(staged.sem, staged.ready(HP + q))
                for e in range(2):
                    pe.wait_ge(sp_done.sem, sp_done.free((q * 2 + e) * TT, 1))
                    for i in reversed(range(TT)):
                        mm(zs_all[i], stage[0][:, i * P:(i + 1) * P], stage_h[e][:, i * P:T],
                           start=True, stop=True).then_inc(z_done.sem, 1)
                    for n, i in enumerate(reversed(range(TT))):
                        item = (q * 2 + e) * TT + n
                        pe.wait_ge(sp_gated.sem, sp_gated.ready(item))
                        pe.wait_ge(a_done.sem, a_done.free(item, 2))
                        mm(us_all[n][:, 0:T - i * P], stage[0][:, i * P:(i + 1) * P], stage_h[e][:, i * P:T],
                           start=True, stop=False)
                        mm(us_all[n][:, 0:P], ident[:], strict[:], start=False, stop=False)
                        for j in range(i, TT):
                            last = mm(us_all[n][:, (j - i) * P:T - i * P], neg_tri[:] if j == i else neg_ones[:],
                                      sp[j], start=False, stop=j == TT - 1)
                        last.then_inc(u_done.sem, 1)
                    pe.wait_ge(a_done.sem, a_done.ready((q * 2 + e) * TT + TT - 1))
                    if e == 0:
                        pe.wait_ge(yb_taken.sem, yb_taken.free(q, 1))
                    for i in range(TT):
                        last = mm(bank(6, T - i * P, i * P)[64 * e:64 * e + 64, :],
                                  stage_v[:, i, 64 * e:64 * e + 64], az[i], start=i == 0, stop=i == TT - 1)
                    last.then_inc(yb_done.sem, 1)

            pe.wait_ge(yb_taken.sem, yb_taken.ready(HP - 1))
            pe.wait_ge(dense_act.sem, dense_act.ready(A_WQ - 1))
            with pe.Fori(0, 2) as q:
                for j in range(4):
                    w = tile(S_PROJ, j, q, 4)
                    pe.wait_ge(dense_dve.sem, dense_dve.free(V_PROJ + q * 4 + j, 2))
                    dense(bank(2 * (j % 2)), w[:, 0:4, :], y[:, 0:4, :])
                    dense(bank(2 * (j % 2) + 1), w[:, 4:8, :], y[:, 4:8, :]).then_inc(tile_done.sem, 1)
            pe.wait_ge(dense_dve.sem, dense_dve.ready(V_OUT - 1))
            with pe.Fori(0, 2) as q:
                for j in range(4):
                    w = tile(S_OUT, j, q, 4)
                    pe.wait_ge(dense_dve.sem, dense_dve.free(V_OUT + q * 4 + j, 2))
                    dense(bank(j % 2), w, gates[:, 0:KT, :]).then_inc(tile_done.sem, 1)

            norm(1, False)
            pe.wait_ge(hn_ready.sem, hn_ready.ready(1))
            for n in range(TT):
                pe.wait_ge(htok_taken.sem, htok_taken.free(n, 2))
                for k in range(KT):
                    last = nc.tensor.transpose(bank(4 + 2 * (n % 2), P, k * P), hn[:, k, META + n * P:META + (n + 1) * P],
                                               ident[:])
                last.then_inc(htok_done.sem, 1)
            pe.wait_ge(keys_loaded, 16)
            with pe.Fori(0, 4) as q:
                for j in range(4):
                    w = tile(S_WQ, j, q, 4)
                    pe.wait_ge(dense_act.sem, dense_act.free(A_WQ + q * 4 + j, 2))
                    dense(bank(j % 2), w, rhs).then_inc(tile_done.sem, 1)
                    pe.wait_ge(dense_act.sem, dense_act.ready(A_WQ + q * 4 + j))
                    pe.wait_ge(key_taken.sem, key_taken.free(q * 4 + j, 2))
                    for i in range(TT):
                        last = mm(bank(2 + j % 2, P, i * P), qh[j % 2][:, i * P:(i + 1) * P],
                                  keys[:, q * 4 + j, :], start=True, stop=True)
                    last.then_inc(key_done.sem, 1)
            def v_rows(n, g, first, last_one):
                s = g % GS
                pe.wait_ge(diag_done.sem, diag_done.ready(n + g))
                for c in range(G):
                    for a in range(2):
                        last = mm(bank(2 + a), diag[:, s, c * P:(c + 1) * P], rows[:, s, c, D + a * 512:D + (a + 1) * 512],
                                  start=first and c == 0, stop=last_one and c == G - 1)
                last.then_inc(rows_used.sem, 1)

            with pe.Fori(0, TT) as n:
                tile_groups = n * (PH * GROUPS)
                pe.wait_ge(acc_done.sem, acc_done.free(n, 1))
                for g in range(GROUPS):
                    v_rows(tile_groups, g, g == 0, False)
                with pe.Fori(1, PH - 1) as h:
                    for g in range(GROUPS):
                        v_rows(tile_groups + h * GROUPS, g, False, False)
                for g in range(GROUPS):
                    v_rows(tile_groups + (PH - 1) * GROUPS, g, False, g == GROUPS - 1)
                pe.wait_ge(acc_done.sem, acc_done.ready(n))
                for k in range(KT):
                    last = nc.tensor.transpose(bank(4, P, k * P), acc[:, k * P:(k + 1) * P], ident[:])
                last.then_inc(f_done.sem, 1)
            norm(2, False)
            norm(3, True)
            pe.wait_ge(hn_ready.sem, hn_ready.ready(3))

            meta = hn[:, :, 0:META]
            with pe.Fori(0, 3) as q:
                for j in range(4):
                    w = tile(S_IN2, j, q, 4)
                    pe.wait_ge(dense_dve.sem, dense_dve.free(V_IN2 + q * 4 + j, 2))
                    dense(seam(4 + 2 * (j % 2), META), w, meta)
                    dense(bank(5 + 2 * (j % 2)), w, rhs).then_inc(tile_done.sem, 1)
            pe.wait_ge(dense_dve.sem, dense_dve.ready(V_V2 - 1))
            for j in range(4):
                w = tile(S_V2, j)
                pe.wait_ge(dense_dve.sem, dense_dve.free(V_V2 + j, 2))
                for k in range(KT):
                    mm(bank(4 + j % 2, P)[0:META, :], hn[:, k, 0:META], w[:, k, :], start=k == 0, stop=k == KT - 1)
                for i in range(TT):
                    for k in range(KT):
                        last = mm(bank(j % 2, P, i * P), hn[:, k, META + i * P:META + (i + 1) * P],
                                  w[:, k, :], start=k == 0, stop=k == KT - 1)
                last.then_inc(tile_done.sem, 1)
            w = tile(S_FG, 0)
            for k in range(KT):
                mm(seam(6, META)[0:NH, :], w[:, k, 0:NH], meta[:, k, :], start=k == 0, stop=k == KT - 1)
            for k in range(KT):
                last = mm(bank(7)[0:NH, :], w[:, k, 0:NH], rhs[:, k, :], start=k == 0, stop=k == KT - 1)
            last.then_inc(tile_done.sem, 1)
            for n in range(8):
                pe.wait_ge(sq_ready.sem, sq_ready.ready(4 * KT + n))
                pe.wait_ge(ms_ready.sem, ms_ready.ready(3 + n))
                mm(seam(2, META), half_ones[:], sq[:, n % 2, 0:META], start=True, stop=True)
                mm(bank(3), half_ones[:], sq[:, n % 2, META:], start=True, stop=True).then_inc(sq_used.sem, 1)
            pe.wait_ge(cum_done.sem, cum_done.ready(0))
            for i in range(TT):
                last = nc.tensor.transpose(bank(0, NH, i * NH), cum[0:NH, META + i * P:META + (i + 1) * P],
                                           ident[0:NH, 0:NH])
            last.then_inc(cumt_done.sem, 1)
            pe.wait_ge(ms_ready.sem, ms_ready.ready(11))
            for h in range(NH):
                pe.wait_ge(cumr_taken.sem, cumr_taken.free(h, 1))
                mm(seam(4, META), cum_pick[h], cum[0:NH, 0:META], start=True, stop=True)
                mm(bank(5), cum_pick[h], cum[0:NH, META:], start=True, stop=True).then_inc(cumr_done.sem, 1)
            pe.wait_ge(cumr_taken.sem, cumr_taken.ready(NH - 1))
            with pe.Fori(0, HP) as q:
                pe.wait_ge(staged.sem, staged.ready(2 * HP + q))
                for u in range(U + 1):
                    if u < U:
                        e, i = units[u]
                        r = slice(64 * e, 64 * e + 64)
                        pe.wait_ge(s_taken.sem, s_taken.free(HP * U + q * U + u, 2))
                        lhsT = stage2[0][r, META + i * P:META + (i + 1) * P]
                        mm(seam(2 + 2 * (u % 2), META), lhsT, stage2[1][r, 0:META], start=True, stop=True)
                        mm(bank(3 + 2 * (u % 2), P * (i + 1)), lhsT, stage2[1][r, META:META + P * (i + 1)],
                           start=True, stop=True).then_inc(s_done.sem, 1)
                    if u >= 1:
                        w = u - 1
                        e, i = units[w]
                        item = HP * U + q * U + w
                        pe.wait_ge(p_done.sem, p_done.ready(item))
                        pe.wait_ge(t_taken.sem, t_taken.free(item, 2))
                        nc.tensor.transpose(bank(0, P, (w % 2) * P), logit2[w % 2][:, 0:P], ident[:])
                        for j in range(i + 1):
                            last = nc.tensor.transpose(bank(6 + w % 2, P, j * P),
                                                       logit2[w % 2][:, META + j * P:META + (j + 1) * P], ident[:])
                        last.then_inc(t_done.sem, 1)
                        if w == 0:
                            pe.wait_ge(y_taken.sem, y_taken.free(HP + q, 1))
                        pe.wait_ge(t_taken.sem, t_taken.ready(item))
                        out = bank(1, P, i * P)[64 * e:64 * e + 64, :]
                        mm(out, stage2_v[:, TT, 64 * e:64 * e + 64], probT2[w % 2][:, TT, :],
                           start=True, stop=False)
                        for j in range(i + 1):
                            last = mm(out, stage2_v[:, j, 64 * e:64 * e + 64],
                                      probT2[w % 2][:, j, :], start=False, stop=j == i)
                        last.then_inc(pv_done.sem, 1)
            w = tile(S_POOL, 0)
            pe.wait_ge(pooled_done.sem, pooled_done.ready(0))
            pe.wait_ge(y_taken.sem, y_taken.ready(2 * HP - 1))
            for g in range(4):
                last = mm(bank(2 + g), w[:, g, :], pooled[:, g, :], start=True, stop=True)
            last.then_inc(tile_done.sem, 1)
            pe.wait_ge(dense_dve.sem, dense_dve.ready(V_POOL))
            with pe.Fori(0, 2) as q:
                for j in range(4):
                    w = tile(S_OUT2, j, q, 4)
                    pe.wait_ge(dense_dve.sem, dense_dve.free(V_OUT2 + q * 4 + j, 2))
                    dense(bank(j % 2), w, mix).then_inc(tile_done.sem, 1)
            norm(4, False)
            pe.wait_ge(hn_ready.sem, hn_ready.ready(4))
            with pe.Fori(0, FF // 2) as q:
                for j in range(4):
                    w = tile(S_UP, j, q, 4)
                    if j % 2 == 0:
                        pe.wait_ge(dense_dve.sem, dense_dve.free(V_UP + q * 2 + j // 2, 2))
                    dense(bank(j), w, rhs).then_inc(tile_done.sem, 1)
            pe.wait_ge(dense_dve.sem, dense_dve.ready(V_UP + FF - 1))
            with pe.Fori(0, 2) as q:
                for m in range(4):
                    pe.wait_ge(o_ready.sem, o_ready.free(q * 4 + m, 2))
                    for c in range(3):
                        w = tile(S_DOWN, 3 * m + c, q, 12)
                        for k in range(min(8, FF - 8 * c)):
                            kk = 8 * c + k
                            last = mm(bank(m % 2), w[:, k, :], act_ff[:, kk, :], start=kk == 0, stop=kk == FF - 1)
                        last.then_inc(tile_done.sem, 1)

        @block.scalar
        def _(act):
            op = nc.scalar.activation
            start(act, "act")
            steps = Steps(act, own["act"])

            def hold():
                act.sem_inc(held["act"], 1)

            act.dma_start(cvec[:], cond.to_broadcast([P, D])).then_inc(cond_loaded, 16)
            act.dma_start(rel_sb[:], rel_bias).then_inc(onehot_loaded, 16)
            act.dma_start(onehot_sb, onehot).then_inc(onehot_loaded, 16)
            act.wait_ge(cond_loaded, 16)
            op(cvec[:], cvec[:], ACT.Silu).then_inc(cond_done.sem, 1)

            def norm(c, first):
                for k in range(KT):
                    act.wait_ge(sq_used.sem, sq_used.free(SQ0[c] + k, 2))
                    op(sq[:, k % 2, first:], x[:, k, first:], ACT.Square).then_inc(sq_ready.sem, 1)
                act.wait_ge(ms_ready.sem, ms_ready.ready(MS[c]))
                op(rstd[:, first:], rstd[:, first:], ACT.Sqrt).then_inc(root_ready.sem, 1)

            act.wait_ge(x_loaded, 16)
            norm(0, META)
            act.wait_ge(rel_stored, 16)
            n = 0
            for i in range(1, TT):
                for h in range(NH):
                    act.wait_ge(idx_done.sem, idx_done.ready(n))
                    act.wait_ge(relu_used.sem, relu_used.free(n, 2))
                    op(relu[n % 2][:, 0:P * (i + 1)], bank(4 + n % 2, P * (i + 1)), ACT.Relu)\
                        .then_inc(relu_done.sem, 1)
                    n += 1

            with act.Fori(0, 2) as q:
                for j in range(4):
                    act.wait_ge(tile_done.sem, tile_done.ready(S_V + q * 4 + j))
                    hold()
                    op(v[:, :, bass.ds((q * 4 + j) * P, P)], bank(j % 2).rearrange("p (a b) -> p a b", b=P),
                       ACT.Copy).then_inc(dense_act.sem, 1)

            units = [(e, i) for e in range(2) for i in range(TT)]
            U = len(units)

            def gate(q, j):
                act.wait_ge(tile_done.sem, tile_done.ready(S_GATE + q * 4 + j))
                hold()
                op(gates[:, q * 4 + j, :], bank(j % 2), ACT.Copy).then_inc(dense_act.sem, 1)

            def softmax_pair(base, lg, width, copy, between=None):
                for u in range(U + 1):
                    if u < U:
                        w = width(units[u][1])
                        act.wait_ge(s_taken.sem, s_taken.ready(base + u))
                        op(lg[u % 2][:, 0:w], lg[u % 2][:, 0:w], ACT.Exp, bias=col[:, 2 + u % 2:3 + u % 2],
                           accum_out=col[:, 4 + u % 2:5 + u % 2]).then_inc(exp_done.sem, 1)
                    if between and u % 2 == 1:
                        between(u // 2)
                    if u >= 1:
                        act.wait_ge(t_done.sem, t_done.ready(base + u - 1))
                        act.wait_ge(pv_done.sem, pv_done.free(base + u - 1, 2))
                        copy(u - 1, units[u - 1][1])

            def copy_a(u, i):
                op(probT[u % 2][:, 0:i + 1, :], bank(4 + u % 2, P * (i + 1)).rearrange("p (a b) -> p a b", b=P),
                   ACT.Copy).then_inc(t_taken.sem, 1)

            with act.Fori(0, HP) as q:
                softmax_pair(q * U, logit, lambda i: P * (i + 1), copy_a, lambda j: gate(q, j))
            with steps.loop(HP, 16) as q:
                for e in range(2):
                    act.wait_ge(yb_done.sem, yb_done.free(q * 2 + e, 1))
                    item = (q * 2 + e) * TT
                    act.wait_ge(z_done.sem, z_done.ready(item + TT - 1))
                    for i in reversed(range(TT)):
                        steps(op(az[i], zs_all[i], ACT.Abs))
                    steps.wait()
                    for i in reversed(range(TT)):
                        steps(op(az[i], az[i], ACT.Exp, scale=-1.0))
                    steps.wait()
                    for i in reversed(range(TT)):
                        op(az[i], az[i], ACT.Ln, bias=1.0).then_inc(soft_done.sem, 1)
                    for n, i in enumerate(reversed(range(TT))):
                        act.wait_ge(u_done.sem, u_done.ready(item + n))
                        op(az[i], us_all[n][:, 0:T - i * P], ACT.Exp).then_inc(a_done.sem, 1)
            for m in (0, 8, 4, 12):
                op(gates[:, m:m + 4, :], gates[:, m:m + 4, :], ACT.Sigmoid).then_inc(gates_done.sem, 1)
            act.wait_ge(x_ready.sem, x_ready.ready(0))
            norm(1, META)
            for n in range(TT):
                act.wait_ge(htok_done.sem, htok_done.ready(n))
                op(h_tok[:, n, :], psum[:, (4 + 2 * (n % 2)) * 512:(6 + 2 * (n % 2)) * 512], ACT.Copy)\
                    .then_inc(htok_taken.sem, 1)
            with act.Fori(0, 4) as q:
                for j in range(4):
                    act.wait_ge(tile_done.sem, tile_done.ready(S_WQ + q * 4 + j))
                    act.wait_ge(key_done.sem, key_done.free(q * 4 + j, 2))
                    op(qh[j % 2][:], bank(j % 2), ACT.Copy).then_inc(dense_act.sem, 1)
                    act.wait_ge(key_done.sem, key_done.ready(q * 4 + j))
                    hold()
                    op(sc[:, :, q * 4 + j, :], bank(2 + j % 2).rearrange("p (a b) -> p a b", b=P), ACT.Copy)\
                        .then_inc(key_taken.sem, 1)

            def best_weights(n):
                act.wait_ge(best_done.sem, best_done.ready(n))
                op(best[:], best[:], ACT.Exp, bias=col[:, 8:9], accum_out=col[:, 9:10])\
                    .then_inc(best_exp.sem, 1)

            def diagonals(n, g):
                s = g % GS
                act.wait_ge(coef_done.sem, coef_done.ready(n + g))
                for c in range(G):
                    ins = op(diag[:, s, c * P:(c + 1) * P], ident[:], ACT.Copy, scale=coef[:, s, c:c + 1])
                    if c == G - 1:
                        steps.wait()
                        ins.then_inc(diag_done.sem, 1)
                    else:
                        steps(ins)

            def gelus(n, best_n=None):
                for g in range(GROUPS):
                    act.wait_ge(pre_done.sem, pre_done.ready(n + g))
                    op(pre[:, g % GS, :], pre[:, g % GS, :], ACT.Gelu).then_inc(gelu_done.sem, 1)
                    diagonals(n, g)
                    if g == BEST_AFTER and best_n is not None:
                        best_weights(best_n)

            def sum_out(j):
                act.wait_ge(rows_used.sem, rows_used.ready(j * (PH * GROUPS) + (PH * GROUPS - 1)))
                act.wait_ge(f_done.sem, f_done.free(j, 1))
                op(acc[:], psum[:, 2 * 512:4 * 512], ACT.Copy).then_inc(acc_done.sem, 1)

            with act.Fori(0, PH) as h:
                best_weights(h)
            with steps.loop(TT - 1, PH * GROUPS * (G - 1)) as j:
                with steps.loop(PH, GROUPS * (G - 1)) as h:
                    n = j * (PH * GROUPS) + h * GROUPS
                    gelus(n, j * PH + h + PH)
                sum_out(j)
            with steps.loop(PH, GROUPS * (G - 1)) as h:
                gelus(h * GROUPS + (TT - 1) * PH * GROUPS)
            sum_out(TT - 1)
            act.wait_ge(x_ready.sem, x_ready.ready(1))
            norm(2, META)
            act.wait_ge(x_ready.sem, x_ready.ready(2))
            act.wait_ge(meta_loaded, 16)
            norm(3, 0)
            for n in range(8):
                act.wait_ge(dense_dve.sem, dense_dve.ready(V_IN2 + n))
                act.wait_ge(sq_used.sem, sq_used.free(4 * KT + n, 2))
                op(sq[:, n % 2, :], big[:, n, :], ACT.Square).then_inc(sq_ready.sem, 1)
                act.wait_ge(ms_ready.sem, ms_ready.ready(4 + n))
                op(rstd[:], rstd[:], ACT.Sqrt).then_inc(root_ready.sem, 1)
            act.wait_ge(fg_done.sem, fg_done.ready(0))
            steps(op(lf2[0:NH, :], lf2[0:NH, :], ACT.Exp, scale=-1.0))
            steps.wait()
            op(lf2[0:NH, :], lf2[0:NH, :], ACT.Ln, bias=1.0).then_inc(fg_exp.sem, 1)
            for h in range(NH):
                act.wait_ge(cumr_done.sem, cumr_done.ready(h))
                op(cum_row[:, h, :], seam(4), ACT.Copy, scale=-1.0).then_inc(cumr_taken.sem, 1)

            def copy_2(u, i):
                steps(op(probT2[u % 2][:, TT, :], bank(0, P, (u % 2) * P), ACT.Copy))
                steps(op(probT2[u % 2][:, 0:i + 1, :],
                         bank(6 + u % 2, P * (i + 1)).rearrange("p (a b) -> p a b", b=P), ACT.Copy))
                steps.wait()
                act.sem_inc(t_taken.sem, 1)

            with steps.loop(HP, 2 * U) as q:
                softmax_pair(HP * U + q * U, logit2, lambda i: META + P * (i + 1), copy_2)
            act.wait_ge(x_ready.sem, x_ready.ready(3))
            norm(4, META)
            with act.Fori(0, FF // 2) as q:
                for j in range(2):
                    act.wait_ge(tile_done.sem, tile_done.ready(S_UP + q * 4 + 2 * j))
                    act.wait_ge(dense_dve.sem, dense_dve.free(V_UP + q * 2 + j, 2))
                    op(silu[j][:], bank(2 * j), ACT.Silu).then_inc(up_silu.sem, 1)

        @block.gpsimd
        def _(pool):
            start(pool, "pool")
            steps = Steps(pool, own["pool"])
            select = nc.gpsimd.affine_select

            for a, value in ((ident, 0.0), (ones, 1.0), (neg_ones, -1.0), (neg_tri, -1.0),
                             (half_ones, 0.0), (causal, 0.0), (strict, 0.0)):
                steps(nc.gpsimd.memset(a[:], value))
            steps(nc.gpsimd.iota(iota16[:], pattern=[[1, PK]], base=0, channel_multiplier=0,
                                 allow_small_or_imprecise_dtypes=True))
            steps.wait()
            steps(select(out=ident[:], in_=ident[:], compare_op=ALU.not_equal, fill=1.0, base=0,
                         pattern=[[-1, P]], channel_multiplier=1))
            steps(select(out=neg_tri[:], in_=neg_tri[:], compare_op=ALU.is_ge, fill=0.0, base=0,
                         pattern=[[-1, P]], channel_multiplier=1))
            steps(select(out=causal[:], in_=causal[:], compare_op=ALU.is_ge, fill=GATED, base=0,
                         pattern=[[-1, P]], channel_multiplier=1))
            steps(select(out=strict[:], in_=strict[:], compare_op=ALU.is_gt, fill=GATED, base=0,
                         pattern=[[1, P]], channel_multiplier=-1))
            for e in range(2):
                steps.wait()
                steps(nc.gpsimd.memset(half_ones[64 * e:64 * e + 64, 64 * e:64 * e + 64], 1.0))
            steps.wait()
            pool.sem_inc(consts_done, 1)
            with pool.Fori(0, ADA // SLOTS) as q:
                for j in range(SLOTS):
                    pool.wait_ge(ada_used.sem, ada_used.free(q * SLOTS + j, SLOTS))
                    pool.sem_inc(held["pool"], 1)
                    nc.gpsimd.dma_start(ada[:, j, :], w_ada[q * SLOTS + j]).then_inc(ada_ready[j], 16)
            pool.wait_ge(rel_copied.sem, rel_copied.ready(0))
            nc.gpsimd.dma_start(rel_dram[:, 0:REL], rel_row).then_inc(rel_stored, 16)
            pool.wait_ge(rel_stored, 16)
            pool.wait_ge(ada_used.sem, ada_used.ready(ADA - 1))
            nc.gpsimd.dma_start(y[:], bass.AP(tensor=rel_dram.tensor, offset=rel_dram.offset,
                                                 ap=[[1, P], [REL + 1, NH], [1, T]])).then_inc(bias_loaded, 16)
            for i in range(1, TT):
                pool.wait_ge(score_done.sem, score_done.ready(i - 1))
                d = score[:, i * P:(i + 1) * P]
                select(out=d, in_=d, compare_op=ALU.is_ge, fill=GATED, base=0, pattern=[[-1, P]],
                       channel_multiplier=1).then_inc(score_gated.sem, 1)
            pool.wait_ge(y_taken.sem, y_taken.ready(HP - 1))
            for e in range(2):
                steps.wait()
                steps(nc.gpsimd.memset(stage_h[e][64 * (1 - e):64 * (1 - e) + 64, :], 0.0))
            tell(pool, steps, half_zeroed)
            with pool.Fori(0, HP) as q:
                for e in range(2):
                    for n, i in enumerate(reversed(range(TT))):
                        pool.wait_ge(sp_done.sem, sp_done.ready((q * 2 + e) * TT + n))
                        pool.sem_inc(held["pool"], 1)
                        d = sp[i][:, 0:P]
                        select(out=d, in_=d, compare_op=ALU.is_gt, fill=0.0, base=0, pattern=[[1, P]],
                               channel_multiplier=-1).then_inc(sp_gated.sem, 1)
            pool.wait_ge(yb_taken.sem, yb_taken.ready(HP - 1))
            nc.gpsimd.dma_start(keys[:], sub_keys).then_inc(keys_loaded, 16)
            def gathers(n, h):
                for g in range(GROUPS):
                    s = g % GS
                    pool.wait_ge(rows_used.sem, rows_used.free(n + g, GS))
                    pool.sem_inc(held["pool"], 1)
                    steps(nc.gpsimd.tensor_copy(eslot[:, s, :], eidx[:, 0, bass.ds(h * PK + g * G, G)]))
                    steps.wait()
                    pool.sem_inc(held["pool"], 1)
                    for c in range(G):
                        nc.gpsimd.indirect_dma_start(
                            rows[:, s, c, :], None, experts,
                            bass.IndirectOffsetOnAxis(ap=eslot[:, s, c:c + 1], axis=0)).then_inc(rows_ready[s], 16)

            with steps.loop(TT, PH * GROUPS) as j:
                pool.wait_ge(idx_ready.sem, idx_ready.ready(j))
                pool.sem_inc(held["pool"], 1)
                with steps.loop(PH, GROUPS) as h:
                    gathers(j * PH * GROUPS + h * GROUPS, h)

        @block.vector
        def _(dve):
            V = nc.vector
            start(dve, "dve")
            steps = Steps(dve, own["dve"])

            def hold():
                dve.sem_inc(held["dve"], 1)

            def sync():
                steps.wait()
                hold()

            def stt(out, a, s, b, op0, op1):
                return V.scalar_tensor_tensor(out=out, in0=a, scalar=s, in1=b, op0=op0, op1=op1)

            def ttr(out, a, b, op0, op1, accum):
                return V.tensor_tensor_reduce(out=out, in0=a, in1=b, scale=1.0,
                                              scalar=0.0 if op1 == ALU.add else TAKEN,
                                              op0=op0, op1=op1, accum_out=accum)

            def ada_tiles(q, js, n0, per=SLOTS):
                for j in js:
                    dve.wait_ge(ada_ready[j], 16 * (n0 // SLOTS + 1) + q * (16 * per // SLOTS))
                    sync()
                    steps(ttr(junk_ada, ada[:, j, :],
                              cvec[:], ALU.mult, ALU.add, col[:, j:j + 1]))
                    steps.wait()
                    dve.sem_inc(ada_used.sem, 1)

            def ada_store(q, n0, per=SLOTS):
                sync()
                steps(V.tensor_tensor(mod[:, bass.ds(q * per + n0, SLOTS)], col[:, 0:SLOTS],
                                      vec[:, bass.ds(q * per + (B_ADA + n0), SLOTS)], ALU.add))

            dve.wait_ge(rel_done.sem, rel_done.ready(0))
            steps(V.tensor_copy(rel_row, bank(4, REL)[0:NH, :]))
            tell(dve, steps, rel_copied)
            dve.wait_ge(cond_done.sem, cond_done.ready(0))
            dve.wait_ge(vec_loaded, 16)
            with steps.loop(4, SLOTS + 1) as q:
                ada_tiles(q, range(SLOTS), 0)
                ada_store(q, 0)
            steps.wait()
            steps(stt(gain1[:], mod[:, 8:16], 1.0, vec[:, G1:G1 + KT], ALU.add, ALU.mult))
            steps.wait()

            def norm(c, first, gain, shift=None, dst=hn):
                dve.wait_ge(sq_used.sem, sq_used.ready(SQ0[c] + KT - 1))
                sums = seam(2) if first == 0 else bank(3)
                steps(V.tensor_scalar(rstd[:, first:], sums, 1.0 / D, EPS, ALU.mult, ALU.add))
                tell(dve, steps, ms_ready)
                dve.wait_ge(root_ready.sem, root_ready.ready(MS[c]))
                steps(V.reciprocal(rstd[:, first:], rstd[:, first:]))
                steps.wait()
                for k in range(KT):
                    steps(stt(dst[:, k, first:], x[:, k, first:], gain[:, k:k + 1], rstd[:, first:],
                              ALU.mult, ALU.mult))
                if shift is not None:
                    steps.wait()
                    for k in range(KT):
                        steps(V.tensor_scalar(dst[:, k, first:], dst[:, k, first:], shift[:, k:k + 1], None, ALU.add))
                tell(dve, steps, hn_ready)

            norm(0, META, gain1, mod[:, 0:KT])
            def qk_out(q, j):
                dve.wait_ge(tile_done.sem, tile_done.ready(S_QK + q * 4 + j))
                steps(V.tensor_scalar(qk[:, q * 4 + j, :], bank(j % 2), 1.0, None, ALU.mult))
                tell(dve, steps, dense_dve)

            with steps.loop(4, 4 + 2 * (SLOTS + 1)) as q:
                for half_q in range(2):
                    for j in range(2):
                        qk_out(q, 2 * half_q + j)
                        ada_tiles(q, [2 * j, 2 * j + 1], 16 + 4 * half_q, 8)
                    ada_store(q, 16 + 4 * half_q, 8)
            for j in range(4):
                qk_out(4, j)
            dve.wait_ge(tile_done.sem, tile_done.ready(S_KI))
            steps(V.tensor_copy(ki[:], bank(0)))
            tell(dve, steps, dense_dve)
            dve.wait_ge(tile_done.sem, tile_done.ready(S_WI))
            steps(V.tensor_copy(wi[:], bank(1, TT * NH).rearrange("p (a b) -> p a b", b=NH)))
            tell(dve, steps, dense_dve)
            steps(V.tensor_scalar(qk[:, QB:QB + 4, :], qk[:, QB:QB + 4, :], 0.125, None, ALU.mult))
            steps.wait()
            steps(stt(gain2[:], mod[:, 32:40], 1.0, vec[:, G2:G2 + KT], ALU.add, ALU.mult))

            steps(V.tensor_copy(mask[0], causal[:]))
            n = 0
            for i in range(1, TT):
                w = P * (i + 1)
                for h in range(NH):
                    dve.wait_ge(relu_done.sem, relu_done.ready(n))
                    if h == 0:
                        steps(V.tensor_scalar(score[:, 0:w], relu[n % 2][:, 0:w], wi[:, i, h:h + 1], None, ALU.mult))
                    else:
                        steps(stt(score[:, 0:w], relu[n % 2][:, 0:w], wi[:, i, h:h + 1], score[:, 0:w],
                                  ALU.mult, ALU.add))
                    tell(dve, steps, relu_used)
                    n += 1
                steps(V.tensor_scalar(score[:, 0:w], score[:, 0:w], IDX_SCALE, None, ALU.mult))
                tell(dve, steps, score_done)
                dve.wait_ge(score_gated.sem, score_gated.ready(i - 1))
                for r in range(TOPK // 8):
                    steps(V.max(col[:, 0:8], score[:, 0:w]))
                    steps.wait()
                    steps(V.match_replace(score[:, 0:w], col[:, 0:8], score[:, 0:w], TAKEN))
                    steps.wait()
                steps(V.tensor_scalar(mask[i], score[:, 0:w], 0.5 * TAKEN, GATED, ALU.is_gt, ALU.mult))
                steps.wait()

            units = [(e, i) for e in range(2) for i in range(TT)]
            U = len(units)

            def finish_unit(base, u, lg, w):
                dve.wait_ge(exp_done.sem, exp_done.ready(base + u))
                steps(V.reciprocal(col[:, 6 + u % 2:7 + u % 2], col[:, 4 + u % 2:5 + u % 2]))
                steps.wait()
                steps(V.tensor_scalar(lg[u % 2][:, 0:w], lg[u % 2][:, 0:w], col[:, 6 + u % 2:7 + u % 2],
                                      None, ALU.mult))
                tell(dve, steps, p_done)

            dve.wait_ge(dense_act.sem, dense_act.ready(A_GATE - 1))
            dve.wait_ge(bias_loaded, 16)
            steps(V.tensor_copy(bias[:], y[:, :, ::-1]))
            with steps.loop(HP, 3 + 5 * U + 1) as q:
                dve.wait_ge(s_done.sem, s_done.free(q * U, 1))
                dve.wait_ge(pv_done.sem, pv_done.free(q * U, 1))
                hold()
                steps(V.tensor_copy(stage[0], qk[:, q + QA, :]))
                steps(V.tensor_copy(stage[1], qk[:, q + KA, :]))
                steps(V.tensor_copy(stage_v[:], v[:, :, bass.ds(q * P, P)]))
                tell(dve, steps, staged)
                for u in range(U + 1):
                    if u < U:
                        e, i = units[u]
                        w = P * (i + 1)
                        lg = logit[u % 2][:, 0:w]
                        dve.wait_ge(s_done.sem, s_done.ready(q * U + u))
                        dve.wait_ge(t_done.sem, t_done.free(q * U + u, 2))
                        hold()
                        steps(stt(lg, bank(2 + u % 2, w), 0.125, bias[:, q * 2 + e, T - w:T], ALU.mult, ALU.add))
                        sync()
                        steps(ttr(lg, lg, mask[i], ALU.add, ALU.max, col[:, u % 2:u % 2 + 1]))
                        steps.wait()
                        steps(V.tensor_scalar(col[:, 2 + u % 2:3 + u % 2], col[:, u % 2:u % 2 + 1], -1.0, None, ALU.mult))
                        tell(dve, steps, s_taken)
                    if u >= 1:
                        finish_unit(q * U, u - 1, logit, P * (units[u - 1][1] + 1))
                dve.wait_ge(pv_done.sem, pv_done.ready(q * U + U - 1))
                hold()
                steps(V.tensor_copy(y[:, q, :], bank(6)))
                tell(dve, steps, y_taken)

            dve.wait_ge(half_zeroed.sem, half_zeroed.ready(0))
            with steps.loop(HP, 4 + 2 * TT + 1) as q:
                dve.wait_ge(yb_done.sem, yb_done.free(q * 2, 1))
                hold()
                steps(V.tensor_copy(stage[0], qk[:, q + KB, :]))
                for e in range(2):
                    steps(V.tensor_copy(stage_h[e][64 * e:64 * e + 64, :], qk[64 * e:64 * e + 64, q + QB, :]))
                steps(V.tensor_copy(stage_v[:], v[:, :, bass.ds(q * P + NH * DH, P)]))
                tell(dve, steps, staged)
                for e in range(2):
                    item = (q * 2 + e) * TT
                    dve.wait_ge(u_done.sem, u_done.free(item, 1))
                    for n, i in enumerate(reversed(range(TT))):
                        dve.wait_ge(soft_done.sem, soft_done.ready(item + n))
                        steps(stt(sp[i], zs_all[i], 0.0, az[i], ALU.max, ALU.add))
                        tell(dve, steps, sp_done)
                dve.wait_ge(yb_done.sem, yb_done.ready(q * 2 + 1))
                hold()
                steps(V.tensor_copy(y[:, q + 4, :], bank(6)))
                tell(dve, steps, yb_taken)

            with steps.loop(2, 4 * 3) as q:
                for j in range(4):
                    m = q * 4 + j
                    b = 2 * (j % 2)
                    dve.wait_ge(gates_done.sem, gates_done.ready(q * 2 + 1))
                    dve.wait_ge(tile_done.sem, tile_done.ready(S_PROJ + m))
                    steps(V.tensor_tensor(gates[:, m, :], gates[:, m, :], bank(b), ALU.mult))
                    steps(V.tensor_tensor(gates[:, m + 8, :], gates[:, m + 8, :], bank(b + 1), ALU.mult))
                    steps.wait()
                    steps(V.tensor_tensor(gates[:, m, :], gates[:, m, :], gates[:, m + 8, :], ALU.add))
                    tell(dve, steps, dense_dve)
            with steps.loop(2, 4) as q:
                for j in range(4):
                    m = q * 4 + j
                    dve.wait_ge(tile_done.sem, tile_done.ready(S_OUT + m))
                    steps(stt(x[:, m, META:], bank(j % 2), mod[:, bass.ds(q * 4 + (16 + j), 1)], x[:, m, META:],
                              ALU.mult, ALU.add))
                    tell(dve, steps, dense_dve)
            tell(dve, steps, x_ready)
            norm(1, META, gain2, mod[:, 24:32])

            def bc(a, dims, axis):
                return a.unsqueeze(axis).to_broadcast(dims)

            def choose(j, h, n):
                steps(V.tensor_copy(half[:], sc[:, j, bass.ds(h * 2, 2), :]))
                sync()
                for c in range(2):
                    steps(V.max(top[:, c, 0:8], half[:, c, :]))
                sync()
                for c in range(2):
                    steps(V.max_index(topi[:, c, 0:8], top[:, c, 0:8], half[:, c, :]))
                sync()
                for c in range(2):
                    steps(V.match_replace(half[:, c, :], top[:, c, 0:8], half[:, c, :], TAKEN))
                sync()
                for c in range(2):
                    steps(V.max(top[:, c, 8:16], half[:, c, :]))
                sync()
                for c in range(2):
                    steps(V.max_index(topi[:, c, 8:16], top[:, c, 8:16], half[:, c, :]))
                yield
                steps(V.tensor_tensor(cand[:], bc(top[:, 0, :], [P, PK, PK], 2), bc(top[:, 1, :], [P, PK, PK], 1), ALU.add))
                sync()
                steps(V.tensor_copy(topf[:], topi[:]))
                flat = cand[:].rearrange("p a b -> p (a b)")
                steps(V.max(best[:, 0:8], flat))
                sync()
                steps(V.max_index(pos[:, 0:8], best[:, 0:8], flat))
                steps(V.tensor_scalar(col[:, 8:9], best[:, 0:1], -1.0, None, ALU.mult))
                sync()
                yield
                steps(V.match_replace(flat, best[:, 0:8], flat, TAKEN))
                sync()
                steps(V.max(best[:, 8:16], flat))
                sync()
                steps(V.max_index(pos[:, 8:16], best[:, 8:16], flat))
                tell(dve, steps, best_done)
                yield
                steps(V.tensor_single_scalar(pos2[:, 0, :], pos[:], 4, ALU.logical_shift_right))
                steps(V.tensor_single_scalar(pos2[:, 1, :], pos[:], 15, ALU.bitwise_and))
                sync()
                steps(V.tensor_copy(posf[:], pos2[:]))
                sync()
                for c in range(2):
                    hc = hot[:, c, :].rearrange("p (a b) -> p a b", b=PK)
                    steps(V.tensor_tensor(hc, bc(posf[:, c, :], [P, PK, PK], 2), bc(iota16[:], [P, PK, PK], 1), ALU.is_equal))
                sync()
                yield
                for c in range(2):
                    hc = hot[:, c, :].rearrange("p (a b) -> p a b", b=PK)
                    steps(V.tensor_tensor(hc, hc, bc(topf[:, c, :], [P, PK, PK], 1), ALU.mult))
                sync()
                for c in range(2):
                    hc = hot[:, c, :].rearrange("p (a b) -> p a b", b=PK)
                    steps(V.tensor_reduce(epart[:, c, :], hc, AX, ALU.add))
                sync()
                steps(stt(eidx[:, 1, bass.ds(h * PK, PK)], epart[:, 0, :], float(NK), epart[:, 1, :], ALU.mult, ALU.add))
                dve.wait_ge(best_exp.sem, best_exp.ready(n))
                hold()
                steps(V.reciprocal(col[:, 10:11], col[:, 9:10]))
                sync()
                steps(V.tensor_scalar(wgt[:, 1, bass.ds(h * PK, PK)], best[:], col[:, 10:11], None, ALU.mult))
            CHOOSE = 1 + 2 + 4 + 2 + 3 + 2 + 3 + 1 + 1 + 2 + 1 + 6 + 1 + 1 + 1

            junks = [hn[:].rearrange("p a b -> p (a b)")[:, c * D:(c + 1) * D] for c in range(G)]

            def dots(n, slot_count, g):
                s = g % GS
                dve.wait_ge(rows_ready[s], slot_count)
                sync()
                for c in range(G):
                    steps(ttr(junks[c], rows[:, s, c, 0:D], h_cur[:], ALU.mult, ALU.add, pre[:, s, c:c + 1]))
                tell(dve, steps, pre_done)

            def weights(n, h, g):
                s = g % GS
                dve.wait_ge(gelu_done.sem, gelu_done.ready(n))
                hold()
                steps(V.tensor_tensor(coef[:, s, :], pre[:, s, :], wgt[:, 0, bass.ds(h * PK + g * G, G)], ALU.mult))
                tell(dve, steps, coef_done)
            GROUP = G + 1

            def experts_of_head(j, h, also_next):
                base = j * (PH * GROUPS) + h * GROUPS
                parts = choose(j + 1, h, j * PH + h + PH) if also_next else iter(())
                for g in range(GROUPS):
                    dots(base + g, j * (PH * GROUPS // GS * 16 * G) + h * (GROUPS // GS * 16 * G)
                         + (g // GS + 1) * 16 * G, g)
                    weights(base + g, h, g)
                    next(parts, None)

            def begin_tile(j):
                sync()
                steps(V.tensor_copy(eidx[:, 0, :], eidx[:, 1, :]))
                steps(V.tensor_copy(wgt[:, 0, :], wgt[:, 1, :]))
                steps(V.tensor_copy(h_cur[:], h_tok[:, j, :]))
                tell(dve, steps, idx_ready)

            def tile_of_tokens(j, also_next):
                with steps.loop(PH, GROUPS * GROUP + (CHOOSE if also_next else 0)) as h:
                    experts_of_head(j, h, also_next)
                if also_next:
                    begin_tile(j + 1)
                dve.wait_ge(f_done.sem, f_done.ready(j))
                hold()
                for k in range(KT):
                    xs = x[:, k, bass.ds(j * P + META, P)]
                    steps(stt(xs, bank(4, P, k * P), mod[:, 40 + k:41 + k], xs, ALU.mult, ALU.add))

            dve.wait_ge(key_taken.sem, key_taken.ready(15))
            dve.wait_ge(htok_taken.sem, htok_taken.ready(TT - 1))
            with steps.loop(PH, CHOOSE) as h:
                for _ in choose(0, h, h):
                    pass
            begin_tile(0)
            with steps.loop(TT - 1, 3 + PH * (GROUPS * GROUP + CHOOSE) + KT) as j:
                tile_of_tokens(j, True)
            tile_of_tokens(TT - 1, False)
            tell(dve, steps, x_ready)
            norm(2, META, vec[:, GF:GF + KT], dst=x)
            tell(dve, steps, x_ready)
            norm(3, 0, vec[:, N1:N1 + KT])

            with steps.loop(3, 4) as q:
                for j in range(4):
                    dve.wait_ge(tile_done.sem, tile_done.ready(S_IN2 + q * 4 + j))
                    steps(V.tensor_scalar(big[:, q * 4 + j, :], seam(4 + 2 * (j % 2)), 1.0, None, ALU.mult))
                    tell(dve, steps, dense_dve)
            steps(V.memset(v2[:, TT, :], 0.0))
            steps.wait()
            for j in range(4):
                dve.wait_ge(tile_done.sem, tile_done.ready(S_V2 + j))
                steps(V.tensor_copy(v2[:, 0:TT, j * P:(j + 1) * P], bank(j % 2).rearrange("p (a b) -> p a b", b=P)))
                steps(V.tensor_copy(v2[0:META, TT, j * P:(j + 1) * P], bank(4 + j % 2, P)[0:META, :]))
                tell(dve, steps, dense_dve)
            dve.wait_ge(tile_done.sem, tile_done.ready(S_FG))
            steps(V.tensor_scalar(lf[0:NH, :], seam(6)[0:NH, :], vec[0:NH, BF:BF + 1], None, ALU.add))
            steps.wait()
            steps(stt(lf2[0:NH, :], lf[0:NH, :], -1.0, lf[0:NH, :], ALU.mult, ALU.max))
            tell(dve, steps, fg_done)
            for n in range(8):
                dve.wait_ge(sq_used.sem, sq_used.ready(4 * KT + n))
                steps.wait()
                steps(V.tensor_scalar(rstd[:], seam(2), 1.0 / DH, EPS, ALU.mult, ALU.add))
                tell(dve, steps, ms_ready)
                dve.wait_ge(root_ready.sem, root_ready.ready(4 + n))
                steps(V.reciprocal(rstd[:], rstd[:]))
                steps.wait()
                c = QN + n // 4
                steps(stt(big[:, n, :], big[:, n, :], vec[:, c:c + 1], rstd[:], ALU.mult, ALU.mult))
            steps.wait()
            steps(V.tensor_scalar(big[:, 0:4, :], big[:, 0:4, :], 0.125, None, ALU.mult))
            dve.wait_ge(fg_exp.sem, fg_exp.ready(0))
            steps(stt(lf[0:NH, :], lf[0:NH, :], 0.0, lf2[0:NH, :], ALU.min, ALU.subtract))
            steps.wait()
            steps(V.tensor_tensor_scan(cum[0:NH, :], ones[0:NH, 0:1].to_broadcast([NH, L2]), lf[0:NH, :], 0.0,
                                       ALU.mult, ALU.add))
            tell(dve, steps, cum_done)
            dve.wait_ge(cumt_done.sem, cumt_done.ready(0))
            steps(V.tensor_copy(cum_tok[:], bank(0, TT * NH).rearrange("p (a b) -> p a b", b=NH)))
            for g in range(4):
                u = big[:, 8 + g, :]
                src, lo = u, 0
                for a in range(g + 1):
                    dst = (pool_a, pool_b)[a % 2]
                    lo += 1 << a
                    steps.wait()
                    steps(V.tensor_tensor(dst[:, lo:], src[:, lo:], src[:, lo - (1 << a):L2 - (1 << a)], ALU.add))
                    src = dst
                steps.wait()
                steps(stt(pooled[:, g, :], src[:, META:], 1.0 / (2 << g), u[:, META:], ALU.mult, ALU.subtract))
            tell(dve, steps, pooled_done)
            dve.wait_ge(cumr_taken.sem, cumr_taken.ready(NH - 1))
            with steps.loop(HP, 3 + 5 * U + 1) as q:
                base = q * U + HP * U
                dve.wait_ge(s_done.sem, s_done.free(base, 1))
                dve.wait_ge(pv_done.sem, pv_done.free(base, 1))
                hold()
                steps(V.tensor_copy(stage2[0], big[:, q, :]))
                steps(V.tensor_copy(stage2[1], big[:, q + 4, :]))
                steps(V.tensor_copy(stage2_v[:], v2[:, :, bass.ds(q * P, P)]))
                tell(dve, steps, staged)
                for u in range(U + 1):
                    if u < U:
                        e, i = units[u]
                        w = META + P * (i + 1)
                        lg = logit2[u % 2][:, 0:w]
                        dve.wait_ge(s_done.sem, s_done.ready(base + u))
                        dve.wait_ge(t_done.sem, t_done.free(base + u, 2))
                        hold()
                        steps(stt(lg, seam(2 + 2 * (u % 2), w), cum_tok[:, i, bass.ds(q * 2 + e, 1)],
                                  cum_row[:, q * 2 + e, 0:w], ALU.add, ALU.add))
                        steps.wait()
                        steps(V.tensor_tensor(lg[:, w - P:w], lg[:, w - P:w], causal[:], ALU.add))
                        sync()
                        steps(V.tensor_reduce(col[:, 2 + u % 2:3 + u % 2], lg, AX, ALU.max, negate=True))
                        tell(dve, steps, s_taken)
                    if u >= 1:
                        finish_unit(base, u - 1, logit2, META + P * (units[u - 1][1] + 1))
                dve.wait_ge(pv_done.sem, pv_done.ready(base + U - 1))
                hold()
                steps(V.tensor_copy(mix[:, q, :], bank(1)))
                tell(dve, steps, y_taken)
            dve.wait_ge(tile_done.sem, tile_done.ready(S_POOL))
            for g in range(4):
                steps(V.tensor_scalar(mix[:, 4 + g, :], bank(2 + g), vec[:, PS + g:PS + g + 1], None, ALU.mult))
            tell(dve, steps, dense_dve)
            with steps.loop(2, 4) as q:
                for j in range(4):
                    m = q * 4 + j
                    dve.wait_ge(tile_done.sem, tile_done.ready(S_OUT2 + m))
                    steps(V.tensor_tensor(x[:, m, META:], bank(j % 2), x[:, m, META:], ALU.add))
                    tell(dve, steps, dense_dve)
            tell(dve, steps, x_ready)
            norm(4, META, vec[:, N2:N2 + KT])
            with steps.loop(FF // 2, 2) as q:
                for j in range(2):
                    dve.wait_ge(tile_done.sem, tile_done.ready(S_UP + q * 4 + 2 * j + 1))
                    dve.wait_ge(up_silu.sem, up_silu.ready(q * 2 + j))
                    steps(V.tensor_tensor(act_ff[:, q * 2 + j, :], silu[j][:], bank(2 * j + 1), ALU.mult))
                    tell(dve, steps, dense_dve)
            with steps.loop(2, 4) as q:
                for m in range(4):
                    dve.wait_ge(tile_done.sem, tile_done.ready(S_DOWN + q * 12 + 3 * m + 2))
                    steps(V.tensor_tensor(outb[:, q * 4 + m, :], bank(m % 2), x[:, q * 4 + m, META:], ALU.add))
                    tell(dve, steps, o_ready)


def tiles(w):
    k, m = w.shape
    return w.reshape(k // P, P, m // P, P).transpose(2, 1, 0, 3).reshape(m // P, P, k)


def columns(vector):
    return vector.reshape(-1, P).T


def kernel(**inputs):
    import numpy as np
    import concourse.bacc as bacc
    from concourse.bass_utils import run_bass_kernel_spmd

    a = {n: np.asarray(v) for n, v in inputs.items()}
    w_in = a["w_in"][0]
    cut = np.split(w_in, np.cumsum([512, 512, 512, 512, 64, 8, 512, 512, 512, 1024]), axis=1)
    qa, ka, va, qi, ki, wi, qb, kb, vb, ga, gb = cut
    w_in2 = a["w_in_2"][0]
    q2, k2, v2, fg, u2 = np.split(w_in2, np.cumsum([512, 512, 512, 8]), axis=1)
    pad = lambda w, m: np.concatenate([w, np.zeros((w.shape[0], m - w.shape[1]), w.dtype)], axis=1)
    both = np.concatenate([a["w_proj_a"][0], a["w_proj_b"][0]], axis=0)
    gate, up = tiles(a["w_gate_2"][0]), tiles(a["w_up_2"][0])
    down = tiles(a["w_down_2"][0])
    down = np.concatenate([down, np.zeros((KT, P, (24 - FF) * P), down.dtype)], axis=2)
    down = down.reshape(KT, P, 3, D).transpose(0, 2, 1, 3).reshape(3 * KT, P, D)
    pools = pad(a["w_pool_2"][0].transpose(1, 0, 2).reshape(P, 4 * P), D)[None]
    stream = np.concatenate([
        tiles(np.concatenate([qi, ka, qa, kb, qb], axis=1)), tiles(np.concatenate([ki, ki], axis=1)),
        tiles(pad(wi, P)), tiles(np.concatenate([va, vb, ga, gb], axis=1)), tiles(both),
        tiles(a["w_out"][0]), tiles(a["peer_wq"][0]), tiles(np.concatenate([q2, k2, u2, v2], axis=1)),
        tiles(pad(fg, P)), pools, tiles(a["w_out_2"][0]),
        np.stack([gate, up], axis=1).reshape(2 * FF, P, D), down], axis=0)
    assert stream.shape[0] == TILES, stream.shape
    twice = lambda w: np.concatenate([w, w])
    small = np.concatenate([
        columns(a["b_ada"][0]), columns(a["norm1_g"][0]), columns(a["norm2_g"][0]), columns(a["final_g"]),
        columns(a["norm1_w_2"][0]), columns(a["norm2_w_2"][0]), columns(twice(a["q_norm_w_2"][0])),
        columns(twice(a["k_norm_w_2"][0])), columns(a["pool_scale_2"][0]),
        np.concatenate([a["b_fgate_2"][0], np.zeros(P - NH, w_in.dtype)])[:, None],
        np.zeros((P, 1), w_in.dtype)], axis=1)
    dist = np.arange(REL) - (P - 1)
    far = BUCKETS // 2 + (np.log(np.maximum(dist, 1).astype(np.float32) / (BUCKETS // 2))
                          / np.float32(np.log(128 / (BUCKETS // 2))) * (BUCKETS // 2)).astype(np.int32)
    bucket = np.where(dist < BUCKETS // 2, np.maximum(dist, 0), np.minimum(far, BUCKETS - 1))
    onehot = (np.arange(BUCKETS)[:, None] == bucket[None]).astype(np.float32)
    arrays = {
        "xT": a["x"][0].T, "metaT": a["meta_tokens_2"].T, "cond": a["c"],
        "w_ada": a["w_ada"][0].T.reshape(ADA, P, D), "small": small, "onehot": onehot,
        "rel_bias": a["rel_bias"], "w_stream": stream,
        "sub_keys": a["peer_sub_keys"][0].reshape(2 * PH, NK, P).transpose(2, 0, 1),
        "experts": np.concatenate([a["peer_u"][0], a["peer_v"][0]], axis=1),
    }
    arrays = {n: np.ascontiguousarray(v) for n, v in arrays.items()}
    nc = bacc.Bacc("TRN2", target_bir_lowering=False, num_devices=1)
    args = [nc.dram_tensor(n, v.shape, mybir.dt.from_np(v.dtype), kind="ExternalInput").ap()
            for n, v in arrays.items()]
    out = nc.dram_tensor("outT", (D, T), mybir.dt.float32, kind="ExternalOutput").ap()
    program(nc, *args, out)
    r = run_bass_kernel_spmd(nc, [arrays], core_ids=[0])
    return np.ascontiguousarray(r.results[0]["outT"].T)[None]
```

```python
import concourse.bass as bass
from concourse import mybir
from contextlib import ExitStack, contextmanager

P = 128
D = 1024
KT = D // P
T = 512
TT = T // P
META = 16
L2 = META + T
NH, DH = 8, 64
HP = NH // 2
TOPK = 128
BUCKETS = 32
REL = T + P - 1
PH, NK, PK = 8, 128, 16
ADA = 6 * D // P
FF = 2816 // P
EPS = 1e-6
GATED, TAKEN = -1e30, -3e38
SLOTS = 4
HIGHS = 2
G, GS = 2, 4
GROUPS = PK // G
BEST_AFTER = 2
IDX_SCALE = 64 ** -0.5 * 8 ** -0.5

B_ADA, G1, G2, GF, N1, N2, QN, PS, BF = 0, 48, 56, 64, 72, 80, 88, 90, 94
SMALL = 96

S_QK, S_KI, S_WI, S_V, S_GATE = 0, 20, 21, 22, 30
S_PROJ, S_OUT, S_WQ = 46, 54, 62
S_IN2, S_V2, S_FG, S_POOL, S_OUT2, S_UP, S_DOWN = 78, 90, 94, 95, 96, 104, 148
TILES = 172


V_QK, V_KI, V_WI, V_PROJ, V_OUT, V_IN2, V_V2, V_POOL, V_OUT2, V_UP = 0, 20, 21, 22, 30, 38, 50, 52, 53, 61
A_V, A_GATE, A_WQ = 0, 4, 20

SQ0, MS = [0, 8, 16, 24, 40], [0, 1, 2, 3, 12]


class Signal:
    CREDIT = 4

    def __init__(self, sem):
        self.sem = sem

    def ready(self, n):
        return n + 1 + self.CREDIT

    def free(self, n, depth):
        return n + 1 + self.CREDIT - depth


class Steps:

    def __init__(self, eng, sem):
        self.eng, self.sem, self.n, self.shift = eng, sem, 0, 0

    def __call__(self, instruction):
        instruction.then_inc(self.sem, 1)
        self.n += 1

    def wait(self):
        self.eng.wait_ge(self.sem, self.shift + self.n)

    @contextmanager
    def loop(self, count, per):
        with self.eng.Fori(0, count) as i:
            base, shift = self.n, self.shift
            self.shift = shift + i * per
            yield i
            assert self.n - base == per, (self.n - base, per)
        self.n, self.shift = base + per * count, shift


def program(nc, xT, metaT, cond, w_ada, small, onehot, rel_bias, w_stream, sub_keys, experts, outT):
    f32, u32, f32r = mybir.dt.float32, mybir.dt.uint32, mybir.dt.float32r
    ALU, ACT, AX = mybir.AluOpType, mybir.ActivationFunctionType, mybir.AxisListType.X
    rel_dram = nc.dram_tensor("rel_rows", (NH, REL + 1), f32, kind="Internal").ap()

    ctx = ExitStack()
    with ctx:
        def sb(name, shape, dtype=f32):
            return ctx.enter_context(nc.sbuf_tensor(name, shape, dtype))

        place = {}

        def sb_placed(name, shape, dtype=f32):
            place[name] = -(-nc.sbuf_base // 32) * 32
            return sb(name, shape, dtype)

        def over(name, shape, other, dtype=f32r, start=0):
            return nc.alloc_sbuf_tensor_at(name, shape, dtype, offset=place[other] + 4 * start)

        def sem(name):
            return ctx.enter_context(nc.semaphore(name))

        x = sb("x", [P, KT, L2])
        hn = sb_placed("hn", [P, KT, L2])
        hn_low = over("hn_low", [P, KT, L2], "hn")
        hn_high = sb_placed("hn_high", [P, KT, L2], f32r)
        ring = sb_placed("ring", [P, SLOTS, D])
        ring_low = over("ring_low", [P, SLOTS, D], "ring")
        w_high = sb("w_high", [P, HIGHS, D], f32r)
        vec = sb("vec", [P, SMALL])
        mod = sb("mod", [P, ADA])
        gain1 = sb("gain1", [P, KT])
        gain2 = sb("gain2", [P, KT])
        ident = sb("ident", [P, P])
        ones = sb("ones", [P, P])
        neg_ones = sb("neg_ones", [P, P])
        neg_tri = sb("neg_tri", [P, P])
        ident_r = sb("ident_r", [P, P], f32r)
        half_ones = sb("half_ones", [P, P])
        causal = sb("causal", [P, P])
        strict = sb("strict", [P, P])
        sq = sb("sq", [P, 2, L2])
        rstd = sb("rstd", [P, L2])
        col = sb("col", [P, 16])
        rel_sb = sb("rel_sb", [BUCKETS, NH])

        ARENA = 31100
        arena = sb_placed("arena", [P, ARENA])
        used = [0]

        def take(*shape):
            n = 1
            for s in shape:
                n *= s
            a = arena[:, used[0]:used[0] + n]
            used[0] += n
            assert used[0] <= ARENA, used[0]
            if len(shape) == 2:
                a = a.rearrange("p (a b) -> p a b", b=shape[1])
            if len(shape) == 3:
                a = a.rearrange("p (a b c) -> p a b c", b=shape[1], c=shape[2])
            return a

        def take_rounded(name, *shape):
            a = over(name, [P, *shape], "arena", start=used[0])
            take(*shape)
            return a

        qk = take(20, T)
        QI, KA, QA, KB, QB = 0, 4, 8, 12, 16
        ki = take(T)
        wi = take(TT, NH)
        v = take(TT, 2 * NH * DH)
        gates_at = used[0]
        gates = take(16, T)
        masks_at = used[0]
        mask = [take(P * (i + 1)) for i in range(TT)]
        probT = [take(TT, P) for _ in range(2)]
        stage = [take(T) for _ in range(2)]
        stage_v = take(TT, P)
        work = used[0]
        bias = take(NH, T)
        y = bias
        y_low = over("y_low", [P, NH, T], "arena", start=work)
        logit = [sq[:, c, 0:T] for c in range(2)]
        used[0] = work
        relu_all = take(2 * T)
        relu = [relu_all[:, 0:T], relu_all[:, T:2 * T]]
        score = take(T)
        onehot_sb = take(1024)[0:BUCKETS, 0:REL]
        rel_row = relu_all[0:NH, 0:REL]
        used[0] = work + 3 * T
        v_high = take_rounded("v_high", 2, D)
        used[0] = 0
        y_high = [take_rounded("ya_high", HP, T)]
        stage_h = [take(T) for _ in range(2)]
        sp = [take(T - P * i) for i in range(TT)]
        az = [take(T - P * i) for i in range(TT)]
        assert used[0] <= 12 * T
        used[0] = 4 * T
        merged_high = take_rounded("merged_high", KT, T)
        merged_low = over("merged_low", [P, KT, T], "arena", start=gates_at)
        used[0] = masks_at
        y_high.append(take_rounded("yb_high", HP, T))
        used[0] = gates_at
        ada = take(SLOTS, D)
        cvec = take(D)
        junk_ada = take(D)
        bias_rows = gates[:, 0:NH, :]
        used[0] = 0
        sc = take(TT, 16, NK)
        h_tok = take(TT, D)
        keys = take(16, NK)
        qh = [take(T) for _ in range(2)]
        used[0] -= 16 * NK + 2 * T
        rows = take(GS, G, 2 * D)
        spare = over("spare", [P, 3 * D], "hn_high", f32)
        h_cur = spare[:, 0:D]
        acc = spare[:, D:2 * D]
        diag = spare[:, 2 * D:3 * D].rearrange("p (a b) -> p a b", b=G * P)
        eidx = sb("eidx", [P, 2, P], u32)
        eslot = sb("eslot", [P, GS, G], u32)
        wgt = take(2, P)
        pre = take(GS, G)
        coef = take(GS, G)
        half = take(2, NK)
        top = take(2, PK)
        topf = take(2, PK)
        cand = take(PK, PK)
        best = take(PK)
        posf = take(2, PK)
        hot = take(2, PK * PK)
        iota16 = sb("iota16", [P, PK])
        epart = take(2, PK)
        topi = sb("topi", [P, 2, PK], u32)
        pos = sb("pos", [P, PK], u32)
        pos2 = sb("pos2", [P, 2, PK], u32)
        used[0] = 0
        big = take(12, L2)
        v2 = take(TT + 1, NH * DH)
        lf = take(L2)
        lf2 = take(L2)
        cum = take(L2)
        cum_tok = take(TT, NH)
        cum_row = take(NH, L2)
        mix_low = over("mix_low", [P, 8, T], "arena", start=used[0])
        mix = take(8, T)
        v2_high = over("v2_high", [P, 2, D], "arena", start=used[0])
        mix_high = take_rounded("mix_high", 8, T)
        stage2 = [take(L2) for _ in range(2)]
        stage2_v = take(TT + 1, P)
        logit2 = [take(L2) for _ in range(2)]
        probT2 = [take(TT + 1, P) for _ in range(2)]
        pool_a = take(L2)
        pool_b = take(L2)
        pooled_low = over("pooled_low", [P, 4, T], "arena", start=used[0])
        pooled = take(4, T)
        pooled_high = mix_high[:, 4:8, :]
        used[0] = 0
        act_low = over("act_low", [P, FF, T], "arena", start=used[0])
        act_ff = take(FF, T)
        act_high = take_rounded("act_high", FF, T)
        silu = [take(T) for _ in range(2)]
        outb = take(KT, T)

        psum = ctx.enter_context(nc.psum_tensor("psum", [P, 8 * 512], f32))

        def bank(b, width=512, start=0):
            return psum[:, b * 512 + start:b * 512 + start + width]

        def seam(b, width=L2):
            return psum[:, (b + 1) * 512 - META:(b + 1) * 512 - META + width]

        zs_all = [bank(2), bank(3, 384), bank(4, 256), bank(3, 128, 384)]
        us_all = [bank(5), bank(7), bank(5), bank(7)]

        ring_ready = [sem(f"ring_ready{i}") for i in range(SLOTS)]
        x_loaded, vec_loaded, meta_loaded, cond_loaded = (sem(n) for n in (
            "x_loaded", "vec_loaded", "meta_loaded", "cond_loaded"))
        onehot_loaded, rel_stored, bias_loaded, keys_loaded = (sem(n) for n in (
            "onehot_loaded", "rel_stored", "bias_loaded", "keys_loaded"))
        ada_ready = [sem(f"ada_ready{i}") for i in range(SLOTS)]
        rows_ready = [sem(f"rows_ready{i}") for i in range(GS)]
        out_stored = sem("out_stored")
        consts_done = sem("consts_done")

        signals = {"pe": [], "act": [], "dve": [], "pool": []}

        def signal(engine, name):
            s = Signal(sem(name))
            signals[engine].append(s)
            return s

        tile_done = signal("pe", "tile_done")
        ada_used = signal("dve", "ada_used")
        cond_done = signal("act", "cond_done")
        w_split = signal("pool", "w_split")
        normed = signal("dve", "normed")
        high_ready = signal("act", "high_ready")
        sq_ready = signal("act", "sq_ready")
        sq_used = signal("pe", "sq_used")
        root_ready = signal("act", "root_ready")
        ms_ready = signal("dve", "ms_ready")
        hn_ready = signal("dve", "hn_ready")
        x_ready = signal("dve", "x_ready")
        dense_dve = signal("dve", "dense_dve")
        dense_act = signal("act", "dense_act")
        rel_done = signal("pe", "rel_done")
        rel_copied = signal("dve", "rel_copied")
        idx_done = signal("pe", "idx_done")
        relu_done = signal("act", "relu_done")
        relu_used = signal("dve", "relu_used")
        staged = signal("dve", "staged")
        s_done = signal("pe", "s_done")
        s_taken = signal("dve", "s_taken")
        exp_done = signal("act", "exp_done")
        p_done = signal("dve", "p_done")
        t_done = signal("pe", "t_done")
        t_taken = signal("act", "t_taken")
        pv_done = signal("pe", "pv_done")
        y_taken = signal("dve", "y_taken")
        z_done = signal("pe", "z_done")
        soft_done = signal("act", "soft_done")
        sp_done = signal("dve", "sp_done")
        sp_gated = signal("pool", "sp_gated")
        u_done = signal("pe", "u_done")
        half_zeroed = signal("pool", "half_zeroed")
        a_done = signal("act", "a_done")
        yb_done = signal("pe", "yb_done")
        yb_taken = signal("dve", "yb_taken")
        gates_done = signal("act", "gates_done")
        key_done = signal("pe", "key_done")
        key_taken = signal("act", "key_taken")
        htok_done = signal("pe", "htok_done")
        htok_taken = signal("act", "htok_taken")
        idx_ready = signal("dve", "idx_ready")
        eslot_done = signal("pool", "eslot_done")
        best_done = signal("dve", "best_done")
        best_exp = signal("act", "best_exp")
        pre_done = signal("dve", "pre_done")
        gelu_done = signal("act", "gelu_done")
        coef_done = signal("dve", "coef_done")
        diag_done = signal("act", "diag_done")
        rows_used = signal("pe", "rows_used")
        acc_done = signal("act", "acc_done")
        f_done = signal("pe", "f_done")
        f_taken = signal("dve", "f_taken")
        fg_done = signal("dve", "fg_done")
        fg_exp = signal("act", "fg_exp")
        cum_done = signal("dve", "cum_done")
        cumt_done = signal("pe", "cumt_done")
        cumr_done = signal("pe", "cumr_done")
        cumr_taken = signal("act", "cumr_taken")
        pooled_done = signal("dve", "pooled_done")
        up_silu = signal("act", "up_silu")
        o_ready = signal("dve", "o_ready")
        cum_pick = [ident[0:NH, h:h + 1].to_broadcast([NH, P]) for h in range(NH)]
        own = {e: sem(f"{e}_step") for e in ("act", "dve", "pool")}
        held = {e: sem(f"{e}_held") for e in ("act", "dve", "pool", "pe")}

        def start(eng, name):
            for s in signals[name]:
                eng.sem_inc(s.sem, Signal.CREDIT)

        def tell(eng, steps, s):
            steps.wait()
            eng.sem_inc(s.sem, 1)

        block = ctx.enter_context(nc.Block())

        @block.sync
        def _(sp_eng):
            eng = sp_eng
            def ada_load(j, n0, q=0, per=0):
                if n0 >= SLOTS:
                    eng.wait_ge(ada_used.sem, ada_used.free(n0 + q * per, SLOTS))
                eng.dma_start(ada[:, j, :], w_ada[n0 + q * per]).then_inc(ada_ready[j], 16)

            def refill(q, j):
                eng.wait_ge(tile_done.sem, tile_done.ready(q * SLOTS + j))
                eng.dma_start(ring[:, j, :], w_stream[(q + 1) * SLOTS + j]).then_inc(ring_ready[j], 16)

            for j in range(SLOTS):
                ada_load(j, j)
            eng.dma_start(x[:, :, META:], xT.rearrange("(k p) t -> p k t", p=P)).then_inc(x_loaded, 16)
            eng.dma_start(vec[:], small).then_inc(vec_loaded, 16)
            with eng.Fori(0, 2) as q:
                for j in range(SLOTS):
                    ada_load(j, SLOTS + j, q, SLOTS)
            for j in range(SLOTS):
                eng.dma_start(ring[:, j, :], w_stream[j]).then_inc(ring_ready[j], 16)
            for n in range(3 * SLOTS, 5 * SLOTS):
                ada_load(n % SLOTS, n)
            eng.dma_start(x[:, :, 0:META], metaT.rearrange("(k p) t -> p k t", p=P))\
               .then_inc(meta_loaded, 16)
            with eng.Fori(0, 3) as q:
                for j in range(SLOTS):
                    refill(q, j)
                    for c in range(2):
                        ada_load((2 * j + c) % SLOTS, 5 * SLOTS + 2 * j + c, q, 2 * SLOTS)
            for j in range(SLOTS):
                refill(3, j)
                for n in range(11 * SLOTS + 2 * j, min(11 * SLOTS + 2 * j + 2, ADA)):
                    ada_load(n % SLOTS, n)
            with eng.Fori(4, TILES // SLOTS - 1) as q:
                for j in range(SLOTS):
                    refill(q, j)
            for m in range(KT):
                eng.wait_ge(o_ready.sem, o_ready.ready(m))
                eng.dma_start(outT[m * P:(m + 1) * P, :], outb[:, m, :]).then_inc(out_stored, 16)
            eng.wait_ge(out_stored, 16 * KT)

        @block.tensor
        def _(pe):
            mm = nc.tensor.matmul
            start(pe, "pe")

            def tile(t0, j, q=0, per=0):
                n = t0 + j
                pe.wait_ge(w_split.sem, w_split.ready(n + q * per))
                return (w_high[:, n % HIGHS, :].rearrange("p (k m) -> p k m", m=P),
                        ring_low[:, n % SLOTS, :].rearrange("p (k m) -> p k m", m=P))

            def part(a, *index):
                return tuple(half[index] for half in a)

            def product(out, a, b, start, stop):
                mm(out, a[0], b[0], start=start, stop=False)
                mm(out, a[0], b[1], start=False, stop=False)
                return mm(out, a[1], b[0], start=False, stop=stop)

            def norm(c, with_meta):
                for k in range(KT):
                    pe.wait_ge(sq_ready.sem, sq_ready.ready(SQ0[c] + k))
                    if k == 0 and c:
                        pe.wait_ge(ms_ready.sem, ms_ready.ready(MS[c] - 1))
                    if with_meta:
                        mm(seam(2, META), ones[:], sq[:, k % 2, 0:META], start=k == 0, stop=k == KT - 1)
                    mm(bank(3), ones[:], sq[:, k % 2, META:], start=k == 0, stop=k == KT - 1)\
                        .then_inc(sq_used.sem, 1)

            def dense(out, w, rhs):
                for k in range(KT):
                    last = product(out, part(w, ALL, k), part(rhs, ALL, k), k == 0, k == KT - 1)
                return last

            def by_token(out, w, tokens):
                for k in range(KT):
                    last = product(out, part(hn_parts, ALL, k, tokens), part(w, ALL, k), k == 0, k == KT - 1)
                return last

            def tile_pair(t0, high, q=0, per=0):
                pe.wait_ge(w_split.sem, w_split.ready(t0 + 1 + q * per))
                low = ring_low[:, t0 % SLOTS:t0 % SLOTS + 2, :]
                return tuple(a.rearrange("p c (k m) -> p k c m", m=P) for a in (high[:], low))

            def pair_by_token(b, w):
                for i in range(TT):
                    last = by_token(bank(b + i // 2, 2 * P, i % 2 * 2 * P), w, slice(META + i * P, META + (i + 1) * P))
                last.then_inc(tile_done.sem, 2)

            ALL = slice(None)
            hn_parts = (hn_high, hn_low)

            pe.wait_ge(consts_done, 1)
            pe.wait_ge(onehot_loaded, 32)
            for a in range(2):
                w = min(512, REL - a * 512)
                last = mm(bank(4 + a, w)[0:NH, :], rel_sb[:], onehot_sb[:, a * 512:a * 512 + w], start=True, stop=True)
            last.then_inc(rel_done.sem, 1)
            norm(0, False)
            rhs = part(hn_parts, ALL, ALL, slice(META, L2))
            pe.wait_ge(hn_ready.sem, hn_ready.ready(0))
            with pe.Fori(0, 5) as q:
                for j in range(4):
                    w = tile(S_QK, j, q, 4)
                    pe.wait_ge(dense_dve.sem, dense_dve.free(q * 4 + j, 2))
                    dense(bank(j % 2), w, rhs).then_inc(tile_done.sem, 1)
            w = tile(S_KI, 0)
            pe.wait_ge(dense_dve.sem, dense_dve.free(V_KI, 2))
            dense(bank(0), w, rhs).then_inc(tile_done.sem, 1)
            w = tile(S_WI, 0)
            pe.wait_ge(dense_dve.sem, dense_dve.free(V_WI, 2))
            w = part(w, ALL, ALL, slice(0, NH))
            for i in range(TT):
                last = by_token(bank(1, NH, i * NH), w, slice(META + i * P, META + (i + 1) * P))
            last.then_inc(tile_done.sem, 1)
            pe.wait_ge(dense_dve.sem, dense_dve.ready(V_KI))
            n = 0
            for i in range(1, TT):
                for h in range(NH):
                    pe.wait_ge(relu_done.sem, relu_done.free(n, 2))
                    r = slice(64 * (h % 2), 64 * (h % 2) + 64)
                    mm(bank(4 + n % 2, P * (i + 1)), qk[r, QI + h // 2, i * P:(i + 1) * P],
                       ki[r, 0:P * (i + 1)], start=True, stop=True).then_inc(idx_done.sem, 1)
                    n += 1

            pe.wait_ge(dense_dve.sem, dense_dve.ready(V_WI))
            with pe.Fori(0, 2) as q:
                for c, high in enumerate((w_high, v_high)):
                    w = tile_pair(S_V + 2 * c, high, q, 4)
                    pe.wait_ge(dense_act.sem, dense_act.free(A_V + q * 2 + c, 2))
                    pair_by_token(2 * c, w)

            units = [(e, i) for e in range(2) for i in range(TT)]
            U = len(units)

            pe.wait_ge(relu_done.sem, relu_done.ready(23))
            with pe.Fori(0, HP) as q:
                pe.wait_ge(staged.sem, staged.ready(q))
                for u in range(U + 1):
                    if u < U:
                        e, i = units[u]
                        r = slice(64 * e, 64 * e + 64)
                        pe.wait_ge(s_taken.sem, s_taken.free(q * U + u, 2))
                        mm(bank(2 + u % 2, P * (i + 1)), stage[0][r, i * P:(i + 1) * P],
                           stage[1][r, 0:P * (i + 1)], start=True, stop=True).then_inc(s_done.sem, 1)
                    if u % 2 == 1:
                        w = tile(S_GATE, u // 2, q, 4)
                        pe.wait_ge(dense_act.sem, dense_act.free(A_GATE + q * 4 + u // 2, 2))
                        dense(bank(u // 2 % 2), w, rhs).then_inc(tile_done.sem, 1)
                    if u >= 1:
                        w = u - 1
                        e, i = units[w]
                        pe.wait_ge(p_done.sem, p_done.ready(q * U + w))
                        pe.wait_ge(t_taken.sem, t_taken.free(q * U + w, 2))
                        for j in range(i + 1):
                            last = nc.tensor.transpose(bank(4 + w % 2, P, j * P),
                                                       logit[w % 2][:, j * P:(j + 1) * P], ident[:])
                        last.then_inc(t_done.sem, 1)
                        if w == 0:
                            pe.wait_ge(y_taken.sem, y_taken.free(q, 1))
                        pe.wait_ge(t_taken.sem, t_taken.ready(q * U + w))
                        for j in range(i + 1):
                            last = mm(bank(6, P, i * P)[64 * e:64 * e + 64, :], stage_v[:, j, 64 * e:64 * e + 64],
                                      probT[w % 2][:, j, :], start=j == 0, stop=j == i)
                        last.then_inc(pv_done.sem, 1)

            pe.wait_ge(y_taken.sem, y_taken.ready(HP - 1))
            with pe.Fori(0, HP) as q:
                pe.wait_ge(staged.sem, staged.ready(HP + q))
                for e in range(2):
                    pe.wait_ge(sp_done.sem, sp_done.free((q * 2 + e) * TT, 1))
                    for i in reversed(range(TT)):
                        mm(zs_all[i], stage[0][:, i * P:(i + 1) * P], stage_h[e][:, i * P:T],
                           start=True, stop=True).then_inc(z_done.sem, 1)
                    for n, i in enumerate(reversed(range(TT))):
                        item = (q * 2 + e) * TT + n
                        pe.wait_ge(sp_gated.sem, sp_gated.ready(item))
                        pe.wait_ge(a_done.sem, a_done.free(item, 2))
                        mm(us_all[n][:, 0:T - i * P], stage[0][:, i * P:(i + 1) * P], stage_h[e][:, i * P:T],
                           start=True, stop=False)
                        mm(us_all[n][:, 0:P], ident[:], strict[:], start=False, stop=False)
                        for j in range(i, TT):
                            last = mm(us_all[n][:, (j - i) * P:T - i * P], neg_tri[:] if j == i else neg_ones[:],
                                      sp[j], start=False, stop=j == TT - 1)
                        last.then_inc(u_done.sem, 1)
                    pe.wait_ge(a_done.sem, a_done.ready((q * 2 + e) * TT + TT - 1))
                    if e == 0:
                        pe.wait_ge(yb_taken.sem, yb_taken.free(q, 1))
                    for i in range(TT):
                        last = mm(bank(6, T - i * P, i * P)[64 * e:64 * e + 64, :],
                                  stage_v[:, i, 64 * e:64 * e + 64], az[i], start=i == 0, stop=i == TT - 1)
                    last.then_inc(yb_done.sem, 1)

            pe.wait_ge(yb_taken.sem, yb_taken.ready(HP - 1))
            pe.wait_ge(dense_act.sem, dense_act.ready(A_WQ - 1))
            with pe.Fori(0, 2) as q:
                for j in range(4):
                    w = tile(S_PROJ, j, q, 4)
                    pe.wait_ge(dense_dve.sem, dense_dve.free(V_PROJ + q * 4 + j, 2))
                    for e in range(2):
                        for k in range(HP):
                            last = product(bank(2 * (j % 2) + e), part(w, ALL, HP * e + k),
                                           (y_high[e][:, k, :], y_low[:, HP * e + k, :]), k == 0, k == HP - 1)
                    last.then_inc(tile_done.sem, 1)
            pe.wait_ge(dense_dve.sem, dense_dve.ready(V_OUT - 1))
            with pe.Fori(0, 2) as q:
                for j in range(4):
                    w = tile(S_OUT, j, q, 4)
                    pe.wait_ge(dense_dve.sem, dense_dve.free(V_OUT + q * 4 + j, 2))
                    dense(bank(j % 2), w, (merged_high, merged_low)).then_inc(tile_done.sem, 1)

            norm(1, False)
            pe.wait_ge(hn_ready.sem, hn_ready.ready(1))
            for n in range(TT):
                pe.wait_ge(htok_taken.sem, htok_taken.free(n, 2))
                tokens = slice(META + n * P, META + (n + 1) * P)
                for k in range(KT):
                    out = bank(4 + 2 * (n % 2), P, k * P)
                    mm(out, hn_high[:, k, tokens], ident_r[:], start=True, stop=False)
                    last = mm(out, hn_low[:, k, tokens], ident_r[:], start=False, stop=True)
                last.then_inc(htok_done.sem, 1)
            pe.wait_ge(keys_loaded, 16)
            with pe.Fori(0, 4) as q:
                for j in range(4):
                    w = tile(S_WQ, j, q, 4)
                    pe.wait_ge(dense_act.sem, dense_act.free(A_WQ + q * 4 + j, 2))
                    dense(bank(j % 2), w, rhs).then_inc(tile_done.sem, 1)
                    pe.wait_ge(dense_act.sem, dense_act.ready(A_WQ + q * 4 + j))
                    pe.wait_ge(key_taken.sem, key_taken.free(q * 4 + j, 2))
                    for i in range(TT):
                        last = mm(bank(2 + j % 2, P, i * P), qh[j % 2][:, i * P:(i + 1) * P],
                                  keys[:, q * 4 + j, :], start=True, stop=True)
                    last.then_inc(key_done.sem, 1)
            def v_rows(n, g, first, last_one):
                s = g % GS
                pe.wait_ge(diag_done.sem, diag_done.ready(n + g))
                for c in range(G):
                    for a in range(2):
                        last = mm(bank(2 + a), diag[:, s, c * P:(c + 1) * P], rows[:, s, c, D + a * 512:D + (a + 1) * 512],
                                  start=first and c == 0, stop=last_one and c == G - 1)
                last.then_inc(rows_used.sem, 1)

            with pe.Fori(0, TT) as n:
                tile_groups = n * (PH * GROUPS)
                pe.wait_ge(acc_done.sem, acc_done.free(n, 1))
                for g in range(GROUPS):
                    v_rows(tile_groups, g, g == 0, False)
                with pe.Fori(1, PH - 1) as h:
                    for g in range(GROUPS):
                        v_rows(tile_groups + h * GROUPS, g, False, False)
                for g in range(GROUPS):
                    v_rows(tile_groups + (PH - 1) * GROUPS, g, False, g == GROUPS - 1)
                pe.wait_ge(acc_done.sem, acc_done.ready(n))
                for k in range(KT):
                    last = nc.tensor.transpose(bank(4, P, k * P), acc[:, k * P:(k + 1) * P], ident[:])
                last.then_inc(f_done.sem, 1)
            norm(2, False)
            norm(3, True)
            pe.wait_ge(hn_ready.sem, hn_ready.ready(2))

            meta = part(hn_parts, ALL, ALL, slice(0, META))
            with pe.Fori(0, 3) as q:
                for j in range(4):
                    w = tile(S_IN2, j, q, 4)
                    pe.wait_ge(dense_dve.sem, dense_dve.free(V_IN2 + q * 4 + j, 2))
                    dense(seam(4 + 2 * (j % 2), META), w, meta)
                    dense(bank(5 + 2 * (j % 2)), w, rhs).then_inc(tile_done.sem, 1)
            pe.wait_ge(dense_dve.sem, dense_dve.ready(V_V2 - 1))
            for c, high in enumerate((w_high, v2_high)):
                w = tile_pair(S_V2 + 2 * c, high)
                by_token(bank(4 + c, 2 * P)[0:META, :], w, slice(0, META))
                pair_by_token(2 * c, w)
            w = tile(S_FG, 0)
            w = part(w, ALL, ALL, slice(0, NH))
            dense(seam(6, META)[0:NH, :], w, meta)
            last = dense(bank(7)[0:NH, :], w, rhs)
            last.then_inc(tile_done.sem, 1)
            pe.wait_ge(dense_dve.sem, dense_dve.ready(V_POOL - 1))
            for n in range(8):
                pe.wait_ge(sq_ready.sem, sq_ready.ready(4 * KT + n))
                pe.wait_ge(ms_ready.sem, ms_ready.ready(3 + n))
                mm(seam(2, META), half_ones[:], sq[:, n % 2, 0:META], start=True, stop=True)
                mm(bank(3), half_ones[:], sq[:, n % 2, META:], start=True, stop=True).then_inc(sq_used.sem, 1)
            pe.wait_ge(cum_done.sem, cum_done.ready(0))
            for i in range(TT):
                last = nc.tensor.transpose(bank(0, NH, i * NH), cum[0:NH, META + i * P:META + (i + 1) * P],
                                           ident[0:NH, 0:NH])
            last.then_inc(cumt_done.sem, 1)
            pe.wait_ge(ms_ready.sem, ms_ready.ready(11))
            for h in range(NH):
                pe.wait_ge(cumr_taken.sem, cumr_taken.free(h, 1))
                mm(seam(4, META), cum_pick[h], cum[0:NH, 0:META], start=True, stop=True)
                mm(bank(5), cum_pick[h], cum[0:NH, META:], start=True, stop=True).then_inc(cumr_done.sem, 1)
            pe.wait_ge(cumr_taken.sem, cumr_taken.ready(NH - 1))
            with pe.Fori(0, HP) as q:
                pe.wait_ge(staged.sem, staged.ready(2 * HP + q))
                for u in range(U + 1):
                    if u < U:
                        e, i = units[u]
                        r = slice(64 * e, 64 * e + 64)
                        pe.wait_ge(s_taken.sem, s_taken.free(HP * U + q * U + u, 2))
                        lhsT = stage2[0][r, META + i * P:META + (i + 1) * P]
                        mm(seam(2 + 2 * (u % 2), META), lhsT, stage2[1][r, 0:META], start=True, stop=True)
                        mm(bank(3 + 2 * (u % 2), P * (i + 1)), lhsT, stage2[1][r, META:META + P * (i + 1)],
                           start=True, stop=True).then_inc(s_done.sem, 1)
                    if u >= 1:
                        w = u - 1
                        e, i = units[w]
                        item = HP * U + q * U + w
                        pe.wait_ge(p_done.sem, p_done.ready(item))
                        pe.wait_ge(t_taken.sem, t_taken.free(item, 2))
                        nc.tensor.transpose(bank(0, P, (w % 2) * P), logit2[w % 2][:, 0:P], ident[:])
                        for j in range(i + 1):
                            last = nc.tensor.transpose(bank(6 + w % 2, P, j * P),
                                                       logit2[w % 2][:, META + j * P:META + (j + 1) * P], ident[:])
                        last.then_inc(t_done.sem, 1)
                        if w == 0:
                            pe.wait_ge(y_taken.sem, y_taken.free(HP + q, 1))
                        pe.wait_ge(t_taken.sem, t_taken.ready(item))
                        out = bank(1, P, i * P)[64 * e:64 * e + 64, :]
                        mm(out, stage2_v[:, TT, 64 * e:64 * e + 64], probT2[w % 2][:, TT, :],
                           start=True, stop=False)
                        for j in range(i + 1):
                            last = mm(out, stage2_v[:, j, 64 * e:64 * e + 64],
                                      probT2[w % 2][:, j, :], start=False, stop=j == i)
                        last.then_inc(pv_done.sem, 1)
            w = tile(S_POOL, 0)
            pe.wait_ge(pooled_done.sem, pooled_done.ready(0))
            pe.wait_ge(y_taken.sem, y_taken.ready(2 * HP - 1))
            for g in range(4):
                last = product(bank(2 + g), part(w, ALL, g), (pooled_high[:, g, :], pooled_low[:, g, :]), True, True)
            last.then_inc(tile_done.sem, 1)
            pe.wait_ge(dense_dve.sem, dense_dve.ready(V_POOL))
            with pe.Fori(0, 2) as q:
                for j in range(4):
                    w = tile(S_OUT2, j, q, 4)
                    pe.wait_ge(dense_dve.sem, dense_dve.free(V_OUT2 + q * 4 + j, 2))
                    dense(bank(j % 2), w, (mix_high, mix_low)).then_inc(tile_done.sem, 1)
            norm(4, False)
            pe.wait_ge(hn_ready.sem, hn_ready.ready(3))
            with pe.Fori(0, FF // 2) as q:
                for j in range(4):
                    w = tile(S_UP, j, q, 4)
                    if j % 2 == 0:
                        pe.wait_ge(dense_dve.sem, dense_dve.free(V_UP + q * 2 + j // 2, 2))
                    dense(bank(j), w, rhs).then_inc(tile_done.sem, 1)
            pe.wait_ge(dense_dve.sem, dense_dve.ready(V_UP + FF - 1))
            with pe.Fori(0, 2) as q:
                for m in range(4):
                    pe.wait_ge(o_ready.sem, o_ready.free(q * 4 + m, 2))
                    for c in range(3):
                        w = tile(S_DOWN, 3 * m + c, q, 12)
                        for k in range(min(8, FF - 8 * c)):
                            kk = 8 * c + k
                            last = product(bank(m % 2), part(w, ALL, k), (act_high[:, kk, :], act_low[:, kk, :]),
                                           kk == 0, kk == FF - 1)
                        last.then_inc(tile_done.sem, 1)

        @block.scalar
        def _(act):
            op = nc.scalar.activation
            start(act, "act")
            steps = Steps(act, own["act"])

            def hold():
                act.sem_inc(held["act"], 1)

            act.dma_start(cvec[:], cond.to_broadcast([P, D])).then_inc(cond_loaded, 16)
            act.dma_start(rel_sb[:], rel_bias).then_inc(onehot_loaded, 16)
            act.dma_start(onehot_sb, onehot).then_inc(onehot_loaded, 16)
            act.wait_ge(cond_loaded, 16)
            op(cvec[:], cvec[:], ACT.Silu).then_inc(cond_done.sem, 1)

            def high_parts(c, first, shift=None):
                for k in range(KT):
                    act.wait_ge(normed.sem, normed.ready(c * KT + k))
                    if shift is None:
                        ins = op(hn_high[:, k, first:], hn[:, k, first:], ACT.Copy)
                    else:
                        ins = op(hn_high[:, k, first:], hn[:, k, first:], ACT.Identity, bias=shift[:, k:k + 1])
                    ins.then_inc(high_ready.sem, 1)

            def norm(c, first):
                for k in range(KT):
                    act.wait_ge(sq_used.sem, sq_used.free(SQ0[c] + k, 2))
                    op(sq[:, k % 2, first:], x[:, k, first:], ACT.Square).then_inc(sq_ready.sem, 1)
                act.wait_ge(ms_ready.sem, ms_ready.ready(MS[c]))
                op(rstd[:, first:], rstd[:, first:], ACT.Sqrt).then_inc(root_ready.sem, 1)

            act.wait_ge(x_loaded, 16)
            norm(0, META)
            high_parts(0, META, mod[:, 0:KT])
            act.wait_ge(rel_stored, 16)
            n = 0
            for i in range(1, TT):
                for h in range(NH):
                    act.wait_ge(idx_done.sem, idx_done.ready(n))
                    act.wait_ge(relu_used.sem, relu_used.free(n, 2))
                    op(relu[n % 2][:, 0:P * (i + 1)], bank(4 + n % 2, P * (i + 1)), ACT.Relu)\
                        .then_inc(relu_done.sem, 1)
                    n += 1

            with act.Fori(0, 2) as q:
                for c in range(2):
                    act.wait_ge(tile_done.sem, tile_done.ready(S_V + q * 4 + 2 * c + 1))
                    hold()
                    op(v[:, :, bass.ds((q * 2 + c) * 2 * P, 2 * P)],
                       bank(2 * c, 1024).rearrange("p (a b) -> p a b", b=2 * P), ACT.Copy).then_inc(dense_act.sem, 1)

            units = [(e, i) for e in range(2) for i in range(TT)]
            U = len(units)

            def gate(q, j):
                act.wait_ge(tile_done.sem, tile_done.ready(S_GATE + q * 4 + j))
                hold()
                op(gates[:, q * 4 + j, :], bank(j % 2), ACT.Copy).then_inc(dense_act.sem, 1)

            def softmax_pair(base, lg, width, copy, between=None):
                for u in range(U + 1):
                    if u < U:
                        w = width(units[u][1])
                        act.wait_ge(s_taken.sem, s_taken.ready(base + u))
                        op(lg[u % 2][:, 0:w], lg[u % 2][:, 0:w], ACT.Exp, bias=col[:, 2 + u % 2:3 + u % 2],
                           accum_out=col[:, 4 + u % 2:5 + u % 2]).then_inc(exp_done.sem, 1)
                    if between and u % 2 == 1:
                        between(u // 2)
                    if u >= 1:
                        act.wait_ge(t_done.sem, t_done.ready(base + u - 1))
                        act.wait_ge(pv_done.sem, pv_done.free(base + u - 1, 2))
                        copy(u - 1, units[u - 1][1])

            def copy_a(u, i):
                op(probT[u % 2][:, 0:i + 1, :], bank(4 + u % 2, P * (i + 1)).rearrange("p (a b) -> p a b", b=P),
                   ACT.Copy).then_inc(t_taken.sem, 1)

            with act.Fori(0, HP) as q:
                softmax_pair(q * U, logit, lambda i: P * (i + 1), copy_a, lambda j: gate(q, j))
            with steps.loop(HP, 16) as q:
                for e in range(2):
                    act.wait_ge(yb_done.sem, yb_done.free(q * 2 + e, 1))
                    item = (q * 2 + e) * TT
                    act.wait_ge(z_done.sem, z_done.ready(item + TT - 1))
                    for i in reversed(range(TT)):
                        steps(op(az[i], zs_all[i], ACT.Abs))
                    steps.wait()
                    for i in reversed(range(TT)):
                        steps(op(az[i], az[i], ACT.Exp, scale=-1.0))
                    steps.wait()
                    for i in reversed(range(TT)):
                        op(az[i], az[i], ACT.Ln, bias=1.0).then_inc(soft_done.sem, 1)
                    for n, i in enumerate(reversed(range(TT))):
                        act.wait_ge(u_done.sem, u_done.ready(item + n))
                        op(az[i], us_all[n][:, 0:T - i * P], ACT.Exp).then_inc(a_done.sem, 1)
            for m in (0, 8, 4, 12):
                op(gates[:, m:m + 4, :], gates[:, m:m + 4, :], ACT.Sigmoid).then_inc(gates_done.sem, 1)
            act.wait_ge(x_ready.sem, x_ready.ready(0))
            norm(1, META)
            high_parts(1, META, mod[:, 24:32])
            for n in range(TT):
                act.wait_ge(htok_done.sem, htok_done.ready(n))
                op(h_tok[:, n, :], psum[:, (4 + 2 * (n % 2)) * 512:(6 + 2 * (n % 2)) * 512], ACT.Copy)\
                    .then_inc(htok_taken.sem, 1)
            with act.Fori(0, 4) as q:
                for j in range(4):
                    act.wait_ge(tile_done.sem, tile_done.ready(S_WQ + q * 4 + j))
                    act.wait_ge(key_done.sem, key_done.free(q * 4 + j, 2))
                    op(qh[j % 2][:], bank(j % 2), ACT.Copy).then_inc(dense_act.sem, 1)
                    act.wait_ge(key_done.sem, key_done.ready(q * 4 + j))
                    hold()
                    op(sc[:, :, q * 4 + j, :], bank(2 + j % 2).rearrange("p (a b) -> p a b", b=P), ACT.Copy)\
                        .then_inc(key_taken.sem, 1)

            def best_weights(n):
                act.wait_ge(best_done.sem, best_done.ready(n))
                op(best[:], best[:], ACT.Exp, bias=col[:, 8:9], accum_out=col[:, 9:10])\
                    .then_inc(best_exp.sem, 1)

            def diagonals(n, g):
                s = g % GS
                act.wait_ge(coef_done.sem, coef_done.ready(n + g))
                for c in range(G):
                    ins = op(diag[:, s, c * P:(c + 1) * P], ident[:], ACT.Copy, scale=coef[:, s, c:c + 1])
                    if c == G - 1:
                        steps.wait()
                        ins.then_inc(diag_done.sem, 1)
                    else:
                        steps(ins)

            def gelus(n, best_n=None):
                for g in range(GROUPS):
                    act.wait_ge(pre_done.sem, pre_done.ready(n + g))
                    op(pre[:, g % GS, :], pre[:, g % GS, :], ACT.Gelu).then_inc(gelu_done.sem, 1)
                    diagonals(n, g)
                    if g == BEST_AFTER and best_n is not None:
                        best_weights(best_n)

            def sum_out(j):
                act.wait_ge(rows_used.sem, rows_used.ready(j * (PH * GROUPS) + (PH * GROUPS - 1)))
                act.wait_ge(f_done.sem, f_done.free(j, 1))
                op(acc[:], psum[:, 2 * 512:4 * 512], ACT.Copy).then_inc(acc_done.sem, 1)

            with act.Fori(0, PH) as h:
                best_weights(h)
            with steps.loop(TT - 1, PH * GROUPS * (G - 1)) as j:
                with steps.loop(PH, GROUPS * (G - 1)) as h:
                    n = j * (PH * GROUPS) + h * GROUPS
                    gelus(n, j * PH + h + PH)
                sum_out(j)
            with steps.loop(PH, GROUPS * (G - 1)) as h:
                gelus(h * GROUPS + (TT - 1) * PH * GROUPS)
            sum_out(TT - 1)
            act.wait_ge(x_ready.sem, x_ready.ready(1))
            norm(2, META)
            act.wait_ge(x_ready.sem, x_ready.ready(2))
            act.wait_ge(meta_loaded, 16)
            norm(3, 0)
            high_parts(2, 0)
            for n in range(8):
                act.wait_ge(dense_dve.sem, dense_dve.ready(V_IN2 + n))
                act.wait_ge(sq_used.sem, sq_used.free(4 * KT + n, 2))
                op(sq[:, n % 2, :], big[:, n, :], ACT.Square).then_inc(sq_ready.sem, 1)
                act.wait_ge(ms_ready.sem, ms_ready.ready(4 + n))
                op(rstd[:], rstd[:], ACT.Sqrt).then_inc(root_ready.sem, 1)
            act.wait_ge(fg_done.sem, fg_done.ready(0))
            steps(op(lf2[0:NH, :], lf2[0:NH, :], ACT.Exp, scale=-1.0))
            steps.wait()
            op(lf2[0:NH, :], lf2[0:NH, :], ACT.Ln, bias=1.0).then_inc(fg_exp.sem, 1)
            for h in range(NH):
                act.wait_ge(cumr_done.sem, cumr_done.ready(h))
                op(cum_row[:, h, :], seam(4), ACT.Copy, scale=-1.0).then_inc(cumr_taken.sem, 1)

            def copy_2(u, i):
                steps(op(probT2[u % 2][:, TT, :], bank(0, P, (u % 2) * P), ACT.Copy))
                steps(op(probT2[u % 2][:, 0:i + 1, :],
                         bank(6 + u % 2, P * (i + 1)).rearrange("p (a b) -> p a b", b=P), ACT.Copy))
                steps.wait()
                act.sem_inc(t_taken.sem, 1)

            with steps.loop(HP, 2 * U) as q:
                softmax_pair(HP * U + q * U, logit2, lambda i: META + P * (i + 1), copy_2)
            act.wait_ge(x_ready.sem, x_ready.ready(3))
            norm(4, META)
            high_parts(3, META)
            with act.Fori(0, FF // 2) as q:
                for j in range(2):
                    act.wait_ge(tile_done.sem, tile_done.ready(S_UP + q * 4 + 2 * j))
                    act.wait_ge(dense_dve.sem, dense_dve.free(V_UP + q * 2 + j, 2))
                    op(silu[j][:], bank(2 * j), ACT.Silu).then_inc(up_silu.sem, 1)

        @block.gpsimd
        def _(pool):
            start(pool, "pool")
            steps = Steps(pool, own["pool"])
            select = nc.gpsimd.affine_select

            for a, value in ((ident, 0.0), (ones, 1.0), (neg_ones, -1.0), (neg_tri, -1.0),
                             (half_ones, 0.0), (causal, 0.0), (strict, 0.0)):
                steps(nc.gpsimd.memset(a[:], value))
            steps(nc.gpsimd.iota(iota16[:], pattern=[[1, PK]], base=0, channel_multiplier=0,
                                 allow_small_or_imprecise_dtypes=True))
            steps.wait()
            steps(select(out=ident[:], in_=ident[:], compare_op=ALU.not_equal, fill=1.0, base=0,
                         pattern=[[-1, P]], channel_multiplier=1))
            steps(select(out=neg_tri[:], in_=neg_tri[:], compare_op=ALU.is_ge, fill=0.0, base=0,
                         pattern=[[-1, P]], channel_multiplier=1))
            steps(select(out=causal[:], in_=causal[:], compare_op=ALU.is_ge, fill=GATED, base=0,
                         pattern=[[-1, P]], channel_multiplier=1))
            steps(select(out=strict[:], in_=strict[:], compare_op=ALU.is_gt, fill=GATED, base=0,
                         pattern=[[1, P]], channel_multiplier=-1))
            steps.wait()
            steps(nc.gpsimd.tensor_tensor(ident_r[:], ident[:], ones[:], ALU.mult))
            for e in range(2):
                steps.wait()
                steps(nc.gpsimd.memset(half_ones[64 * e:64 * e + 64, 64 * e:64 * e + 64], 1.0))
            steps.wait()
            pool.sem_inc(consts_done, 1)

            def split_tile(n, q=0, per=0, high=None, depth=HIGHS):
                pool.wait_ge(ring_ready[n % SLOTS], 16 * (n // SLOTS + 1) + q * (16 * per // SLOTS))
                pool.wait_ge(tile_done.sem, tile_done.free(n + q * per, depth))
                pool.sem_inc(held["pool"], 1)
                if high is None:
                    high = w_high[:, n % HIGHS, :]
                raw, low = ring[:, n % SLOTS, :], ring_low[:, n % SLOTS, :]
                steps(nc.gpsimd.tensor_tensor(high.rearrange("p (a b) -> p a b", b=P),
                                              raw.rearrange("p (a b) -> p a b", b=P),
                                              ones[:].unsqueeze(1).to_broadcast([P, KT, P]), ALU.mult))
                steps.wait()
                steps(nc.gpsimd.tensor_tensor(low, raw, high.bitcast(f32), ALU.subtract))
                tell(pool, steps, w_split)

            def split(first, last):
                with steps.loop((last - first) // SLOTS, 2 * SLOTS) as q:
                    for j in range(SLOTS):
                        split_tile(first + j, q, SLOTS)

            def split_pairs(first, rounds, second_high):
                pool.wait_ge(tile_done.sem, tile_done.ready(first - 1))
                with steps.loop(rounds, 2 * SLOTS) as q:
                    for j in range(SLOTS):
                        split_tile(first + j, q, SLOTS, second_high[:, j - 2, :] if j >= 2 else None, SLOTS)
                for n in range(first + rounds * SLOTS, first + rounds * SLOTS + 2):
                    split_tile(n, depth=SLOTS)

            pool.wait_ge(rel_copied.sem, rel_copied.ready(0))
            nc.gpsimd.dma_start(rel_dram[:, 0:REL], rel_row).then_inc(rel_stored, 16)
            pool.wait_ge(rel_stored, 16)
            split(S_QK, S_KI)
            pool.wait_ge(ada_used.sem, ada_used.ready(ADA - 1))
            nc.gpsimd.dma_start(bias_rows, bass.AP(tensor=rel_dram.tensor, offset=rel_dram.offset,
                                                 ap=[[1, P], [REL + 1, NH], [1, T]])).then_inc(bias_loaded, 16)
            for n in range(S_KI, S_V):
                split_tile(n)
            split_pairs(S_V, 2, v_high)
            split(S_GATE + 2, 48)
            pool.wait_ge(y_taken.sem, y_taken.ready(HP - 1))
            for e in range(2):
                steps.wait()
                steps(nc.gpsimd.memset(stage_h[e][64 * (1 - e):64 * (1 - e) + 64, :], 0.0))
            tell(pool, steps, half_zeroed)
            with pool.Fori(0, HP) as q:
                for e in range(2):
                    for n, i in enumerate(reversed(range(TT))):
                        pool.wait_ge(sp_done.sem, sp_done.ready((q * 2 + e) * TT + n))
                        pool.sem_inc(held["pool"], 1)
                        d = sp[i][:, 0:P]
                        select(out=d, in_=d, compare_op=ALU.is_gt, fill=0.0, base=0, pattern=[[1, P]],
                               channel_multiplier=-1).then_inc(sp_gated.sem, 1)
            pool.wait_ge(yb_taken.sem, yb_taken.ready(HP - 1))
            nc.gpsimd.dma_start(keys[:], sub_keys).then_inc(keys_loaded, 16)
            split(48, 80)
            def gathers(n, h):
                for g in range(GROUPS):
                    s = g % GS
                    pool.wait_ge(rows_used.sem, rows_used.free(n + g, GS))
                    pool.sem_inc(held["pool"], 1)
                    steps(nc.gpsimd.tensor_copy(eslot[:, s, :], eidx[:, 0, bass.ds(h * PK + g * G, G)]))
                    steps.wait()
                    pool.sem_inc(held["pool"], 1)
                    for c in range(G):
                        nc.gpsimd.indirect_dma_start(
                            rows[:, s, c, :], None, experts,
                            bass.IndirectOffsetOnAxis(ap=eslot[:, s, c:c + 1], axis=0)).then_inc(rows_ready[s], 16)

            with steps.loop(TT, PH * GROUPS) as j:
                pool.wait_ge(idx_ready.sem, idx_ready.ready(j))
                pool.sem_inc(held["pool"], 1)
                with steps.loop(PH, GROUPS) as h:
                    gathers(j * PH * GROUPS + h * GROUPS, h)
            split(80, S_V2 - 2)
            for n in range(S_V2 - 2, S_V2):
                split_tile(n)
            split_pairs(S_V2, 1, v2_high)
            split(S_OUT2, TILES)

        @block.vector
        def _(dve):
            V = nc.vector
            start(dve, "dve")
            steps = Steps(dve, own["dve"])

            def hold():
                dve.sem_inc(held["dve"], 1)

            def sync():
                steps.wait()
                hold()

            def stt(out, a, s, b, op0, op1):
                return V.scalar_tensor_tensor(out=out, in0=a, scalar=s, in1=b, op0=op0, op1=op1)

            def ttr(out, a, b, op0, op1, accum):
                return V.tensor_tensor_reduce(out=out, in0=a, in1=b, scale=1.0,
                                              scalar=0.0 if op1 == ALU.add else TAKEN,
                                              op0=op0, op1=op1, accum_out=accum)

            def ada_tiles(q, js, n0, per=SLOTS):
                for j in js:
                    dve.wait_ge(ada_ready[j], 16 * (n0 // SLOTS + 1) + q * (16 * per // SLOTS))
                    sync()
                    steps(ttr(junk_ada, ada[:, j, :],
                              cvec[:], ALU.mult, ALU.add, col[:, j:j + 1]))
                    steps.wait()
                    dve.sem_inc(ada_used.sem, 1)

            def ada_store(q, n0, per=SLOTS):
                sync()
                steps(V.tensor_tensor(mod[:, bass.ds(q * per + n0, SLOTS)], col[:, 0:SLOTS],
                                      vec[:, bass.ds(q * per + (B_ADA + n0), SLOTS)], ALU.add))

            dve.wait_ge(rel_done.sem, rel_done.ready(0))
            steps(V.tensor_copy(rel_row, bank(4, REL)[0:NH, :]))
            tell(dve, steps, rel_copied)
            dve.wait_ge(cond_done.sem, cond_done.ready(0))
            dve.wait_ge(vec_loaded, 16)
            with steps.loop(4, SLOTS + 1) as q:
                ada_tiles(q, range(SLOTS), 0)
                ada_store(q, 0)
            steps.wait()
            steps(stt(gain1[:], mod[:, 8:16], 1.0, vec[:, G1:G1 + KT], ALU.add, ALU.mult))
            steps.wait()

            def norm(c, first, gain, parts, shift=None, dst=hn):
                dve.wait_ge(sq_used.sem, sq_used.ready(SQ0[c] + KT - 1))
                sums = seam(2) if first == 0 else bank(3)
                steps(V.tensor_scalar(rstd[:, first:], sums, 1.0 / D, EPS, ALU.mult, ALU.add))
                tell(dve, steps, ms_ready)
                dve.wait_ge(root_ready.sem, root_ready.ready(MS[c]))
                steps(V.reciprocal(rstd[:, first:], rstd[:, first:]))
                steps.wait()
                for k in range(KT):
                    steps(stt(dst[:, k, first:], x[:, k, first:], gain[:, k:k + 1], rstd[:, first:],
                              ALU.mult, ALU.mult))
                    if parts is not None:
                        tell(dve, steps, normed)
                if parts is None:
                    return
                for k in range(KT):
                    dve.wait_ge(high_ready.sem, high_ready.ready(parts * KT + k))
                    high = hn_high[:, k, first:].bitcast(f32)
                    if shift is None:
                        steps(V.tensor_tensor(hn_low[:, k, first:], hn[:, k, first:], high, ALU.subtract))
                    else:
                        steps(stt(hn_low[:, k, first:], hn[:, k, first:], shift[:, k:k + 1], high,
                                  ALU.add, ALU.subtract))
                tell(dve, steps, hn_ready)

            def low_part(low, raw, high):
                steps(V.tensor_copy(high, raw))
                steps.wait()
                steps(V.tensor_tensor(low, raw, high.bitcast(f32), ALU.subtract))

            norm(0, META, gain1, 0, mod[:, 0:KT])
            def qk_out(q, j):
                dve.wait_ge(tile_done.sem, tile_done.ready(S_QK + q * 4 + j))
                steps(V.tensor_scalar(qk[:, q * 4 + j, :], bank(j % 2), 1.0, None, ALU.mult))
                tell(dve, steps, dense_dve)

            with steps.loop(4, 4 + 2 * (SLOTS + 1)) as q:
                for half_q in range(2):
                    for j in range(2):
                        qk_out(q, 2 * half_q + j)
                        ada_tiles(q, [2 * j, 2 * j + 1], 16 + 4 * half_q, 8)
                    ada_store(q, 16 + 4 * half_q, 8)
            for j in range(4):
                qk_out(4, j)
            dve.wait_ge(tile_done.sem, tile_done.ready(S_KI))
            steps(V.tensor_copy(ki[:], bank(0)))
            tell(dve, steps, dense_dve)
            dve.wait_ge(tile_done.sem, tile_done.ready(S_WI))
            steps(V.tensor_copy(wi[:], bank(1, TT * NH).rearrange("p (a b) -> p a b", b=NH)))
            tell(dve, steps, dense_dve)
            steps(V.tensor_scalar(qk[:, QB:QB + 4, :], qk[:, QB:QB + 4, :], 0.125, None, ALU.mult))
            steps.wait()
            steps(stt(gain2[:], mod[:, 32:40], 1.0, vec[:, G2:G2 + KT], ALU.add, ALU.mult))

            steps(V.tensor_copy(mask[0], causal[:]))
            n = 0
            for i in range(1, TT):
                w = P * (i + 1)
                for h in range(NH):
                    dve.wait_ge(relu_done.sem, relu_done.ready(n))
                    if h == 0:
                        steps(V.tensor_scalar(score[:, 0:w], relu[n % 2][:, 0:w], wi[:, i, h:h + 1], None, ALU.mult))
                    else:
                        steps(stt(score[:, 0:w], relu[n % 2][:, 0:w], wi[:, i, h:h + 1], score[:, 0:w],
                                  ALU.mult, ALU.add))
                    tell(dve, steps, relu_used)
                    n += 1
                steps(V.tensor_scalar(score[:, 0:w], score[:, 0:w], IDX_SCALE, None, ALU.mult))
                steps.wait()
                steps(V.tensor_tensor(score[:, w - P:w], score[:, w - P:w], causal[:], ALU.add))
                steps.wait()
                for r in range(TOPK // 8):
                    steps(V.max(col[:, 0:8], score[:, 0:w]))
                    steps.wait()
                    steps(V.match_replace(score[:, 0:w], col[:, 0:8], score[:, 0:w], TAKEN))
                    steps.wait()
                steps(V.tensor_scalar(mask[i], score[:, 0:w], 0.5 * TAKEN, GATED, ALU.is_gt, ALU.mult))
                steps.wait()

            units = [(e, i) for e in range(2) for i in range(TT)]
            U = len(units)

            def finish_unit(base, u, lg, w):
                dve.wait_ge(exp_done.sem, exp_done.ready(base + u))
                steps(V.reciprocal(col[:, 6 + u % 2:7 + u % 2], col[:, 4 + u % 2:5 + u % 2]))
                steps.wait()
                steps(V.tensor_scalar(lg[u % 2][:, 0:w], lg[u % 2][:, 0:w], col[:, 6 + u % 2:7 + u % 2],
                                      None, ALU.mult))
                tell(dve, steps, p_done)

            dve.wait_ge(dense_act.sem, dense_act.ready(A_GATE - 1))
            dve.wait_ge(bias_loaded, 16)
            steps(V.tensor_copy(bias[:], bias_rows[:, :, ::-1]))
            with steps.loop(HP, 3 + 5 * U + 2) as q:
                dve.wait_ge(s_done.sem, s_done.free(q * U, 1))
                dve.wait_ge(pv_done.sem, pv_done.free(q * U, 1))
                hold()
                steps(V.tensor_copy(stage[0], qk[:, q + QA, :]))
                steps(V.tensor_copy(stage[1], qk[:, q + KA, :]))
                steps(V.tensor_copy(stage_v[:], v[:, :, bass.ds(q * P, P)]))
                tell(dve, steps, staged)
                for u in range(U + 1):
                    if u < U:
                        e, i = units[u]
                        w = P * (i + 1)
                        lg = logit[u % 2][:, 0:w]
                        dve.wait_ge(s_done.sem, s_done.ready(q * U + u))
                        dve.wait_ge(t_done.sem, t_done.free(q * U + u, 2))
                        hold()
                        steps(stt(lg, bank(2 + u % 2, w), 0.125, bias[:, q * 2 + e, T - w:T], ALU.mult, ALU.add))
                        sync()
                        steps(ttr(lg, lg, mask[i], ALU.add, ALU.max, col[:, u % 2:u % 2 + 1]))
                        steps.wait()
                        steps(V.tensor_scalar(col[:, 2 + u % 2:3 + u % 2], col[:, u % 2:u % 2 + 1], -1.0, None, ALU.mult))
                        tell(dve, steps, s_taken)
                    if u >= 1:
                        finish_unit(q * U, u - 1, logit, P * (units[u - 1][1] + 1))
                dve.wait_ge(pv_done.sem, pv_done.ready(q * U + U - 1))
                hold()
                low_part(y_low[:, q, :], bank(6), y_high[0][:, q, :])
                tell(dve, steps, y_taken)

            dve.wait_ge(half_zeroed.sem, half_zeroed.ready(0))
            with steps.loop(HP, 4 + 2 * TT + 2) as q:
                dve.wait_ge(yb_done.sem, yb_done.free(q * 2, 1))
                hold()
                steps(V.tensor_copy(stage[0], qk[:, q + KB, :]))
                for e in range(2):
                    steps(V.tensor_copy(stage_h[e][64 * e:64 * e + 64, :], qk[64 * e:64 * e + 64, q + QB, :]))
                steps(V.tensor_copy(stage_v[:], v[:, :, bass.ds(q * P + NH * DH, P)]))
                tell(dve, steps, staged)
                for e in range(2):
                    item = (q * 2 + e) * TT
                    dve.wait_ge(u_done.sem, u_done.free(item, 1))
                    for n, i in enumerate(reversed(range(TT))):
                        dve.wait_ge(soft_done.sem, soft_done.ready(item + n))
                        steps(stt(sp[i], zs_all[i], 0.0, az[i], ALU.max, ALU.add))
                        tell(dve, steps, sp_done)
                dve.wait_ge(yb_done.sem, yb_done.ready(q * 2 + 1))
                hold()
                low_part(y_low[:, q + HP, :], bank(6), y_high[1][:, q, :])
                tell(dve, steps, yb_taken)

            with steps.loop(2, 4 * 5) as q:
                for j in range(4):
                    m = q * 4 + j
                    b = 2 * (j % 2)
                    dve.wait_ge(gates_done.sem, gates_done.ready(q * 2 + 1))
                    dve.wait_ge(tile_done.sem, tile_done.ready(S_PROJ + m))
                    steps(V.tensor_tensor(gates[:, m, :], gates[:, m, :], bank(b), ALU.mult))
                    steps(V.tensor_tensor(gates[:, m + 8, :], gates[:, m + 8, :], bank(b + 1), ALU.mult))
                    steps.wait()
                    steps(V.tensor_tensor(gates[:, m, :], gates[:, m, :], gates[:, m + 8, :], ALU.add))
                    steps.wait()
                    low_part(merged_low[:, m, :], gates[:, m, :], merged_high[:, m, :])
                    tell(dve, steps, dense_dve)
            with steps.loop(2, 4) as q:
                for j in range(4):
                    m = q * 4 + j
                    dve.wait_ge(tile_done.sem, tile_done.ready(S_OUT + m))
                    steps(stt(x[:, m, META:], bank(j % 2), mod[:, bass.ds(q * 4 + (16 + j), 1)], x[:, m, META:],
                              ALU.mult, ALU.add))
                    tell(dve, steps, dense_dve)
            tell(dve, steps, x_ready)
            norm(1, META, gain2, 1, mod[:, 24:32])

            def bc(a, dims, axis):
                return a.unsqueeze(axis).to_broadcast(dims)

            def choose(j, h, n):
                steps(V.tensor_copy(half[:], sc[:, j, bass.ds(h * 2, 2), :]))
                sync()
                for c in range(2):
                    steps(V.max(top[:, c, 0:8], half[:, c, :]))
                sync()
                for c in range(2):
                    steps(V.max_index(topi[:, c, 0:8], top[:, c, 0:8], half[:, c, :]))
                sync()
                for c in range(2):
                    steps(V.match_replace(half[:, c, :], top[:, c, 0:8], half[:, c, :], TAKEN))
                sync()
                for c in range(2):
                    steps(V.max(top[:, c, 8:16], half[:, c, :]))
                sync()
                for c in range(2):
                    steps(V.max_index(topi[:, c, 8:16], top[:, c, 8:16], half[:, c, :]))
                yield
                steps(V.tensor_tensor(cand[:], bc(top[:, 0, :], [P, PK, PK], 2), bc(top[:, 1, :], [P, PK, PK], 1), ALU.add))
                sync()
                steps(V.tensor_copy(topf[:], topi[:]))
                flat = cand[:].rearrange("p a b -> p (a b)")
                steps(V.max(best[:, 0:8], flat))
                sync()
                steps(V.max_index(pos[:, 0:8], best[:, 0:8], flat))
                steps(V.tensor_scalar(col[:, 8:9], best[:, 0:1], -1.0, None, ALU.mult))
                sync()
                yield
                steps(V.match_replace(flat, best[:, 0:8], flat, TAKEN))
                sync()
                steps(V.max(best[:, 8:16], flat))
                sync()
                steps(V.max_index(pos[:, 8:16], best[:, 8:16], flat))
                tell(dve, steps, best_done)
                yield
                steps(V.tensor_single_scalar(pos2[:, 0, :], pos[:], 4, ALU.logical_shift_right))
                steps(V.tensor_single_scalar(pos2[:, 1, :], pos[:], 15, ALU.bitwise_and))
                sync()
                steps(V.tensor_copy(posf[:], pos2[:]))
                sync()
                for c in range(2):
                    hc = hot[:, c, :].rearrange("p (a b) -> p a b", b=PK)
                    steps(V.tensor_tensor(hc, bc(posf[:, c, :], [P, PK, PK], 2), bc(iota16[:], [P, PK, PK], 1), ALU.is_equal))
                sync()
                yield
                for c in range(2):
                    hc = hot[:, c, :].rearrange("p (a b) -> p a b", b=PK)
                    steps(V.tensor_tensor(hc, hc, bc(topf[:, c, :], [P, PK, PK], 1), ALU.mult))
                sync()
                for c in range(2):
                    hc = hot[:, c, :].rearrange("p (a b) -> p a b", b=PK)
                    steps(V.tensor_reduce(epart[:, c, :], hc, AX, ALU.add))
                sync()
                steps(stt(eidx[:, 1, bass.ds(h * PK, PK)], epart[:, 0, :], float(NK), epart[:, 1, :], ALU.mult, ALU.add))
                dve.wait_ge(best_exp.sem, best_exp.ready(n))
                hold()
                steps(V.reciprocal(col[:, 10:11], col[:, 9:10]))
                sync()
                steps(V.tensor_scalar(wgt[:, 1, bass.ds(h * PK, PK)], best[:], col[:, 10:11], None, ALU.mult))
            CHOOSE = 1 + 2 + 4 + 2 + 3 + 2 + 3 + 1 + 1 + 2 + 1 + 6 + 1 + 1 + 1

            junks = [hn[:].rearrange("p a b -> p (a b)")[:, c * D:(c + 1) * D] for c in range(G)]

            def dots(n, slot_count, g):
                s = g % GS
                dve.wait_ge(rows_ready[s], slot_count)
                sync()
                for c in range(G):
                    steps(ttr(junks[c], rows[:, s, c, 0:D], h_cur[:], ALU.mult, ALU.add, pre[:, s, c:c + 1]))
                tell(dve, steps, pre_done)

            def weights(n, h, g):
                s = g % GS
                dve.wait_ge(gelu_done.sem, gelu_done.ready(n))
                hold()
                steps(V.tensor_tensor(coef[:, s, :], pre[:, s, :], wgt[:, 0, bass.ds(h * PK + g * G, G)], ALU.mult))
                tell(dve, steps, coef_done)
            GROUP = G + 1

            def experts_of_head(j, h, also_next):
                base = j * (PH * GROUPS) + h * GROUPS
                parts = choose(j + 1, h, j * PH + h + PH) if also_next else iter(())
                for g in range(GROUPS):
                    dots(base + g, j * (PH * GROUPS // GS * 16 * G) + h * (GROUPS // GS * 16 * G)
                         + (g // GS + 1) * 16 * G, g)
                    weights(base + g, h, g)
                    next(parts, None)

            def begin_tile(j):
                sync()
                steps(V.tensor_copy(eidx[:, 0, :], eidx[:, 1, :]))
                steps(V.tensor_copy(wgt[:, 0, :], wgt[:, 1, :]))
                steps(V.tensor_copy(h_cur[:], h_tok[:, j, :]))
                tell(dve, steps, idx_ready)

            def tile_of_tokens(j, also_next):
                with steps.loop(PH, GROUPS * GROUP + (CHOOSE if also_next else 0)) as h:
                    experts_of_head(j, h, also_next)
                if also_next:
                    begin_tile(j + 1)
                dve.wait_ge(f_done.sem, f_done.ready(j))
                hold()
                for k in range(KT):
                    xs = x[:, k, bass.ds(j * P + META, P)]
                    steps(stt(xs, bank(4, P, k * P), mod[:, 40 + k:41 + k], xs, ALU.mult, ALU.add))

            dve.wait_ge(key_taken.sem, key_taken.ready(15))
            dve.wait_ge(htok_taken.sem, htok_taken.ready(TT - 1))
            with steps.loop(PH, CHOOSE) as h:
                for _ in choose(0, h, h):
                    pass
            begin_tile(0)
            with steps.loop(TT - 1, 3 + PH * (GROUPS * GROUP + CHOOSE) + KT) as j:
                tile_of_tokens(j, True)
            tile_of_tokens(TT - 1, False)
            tell(dve, steps, x_ready)
            norm(2, META, vec[:, GF:GF + KT], None, dst=x)
            tell(dve, steps, x_ready)
            norm(3, 0, vec[:, N1:N1 + KT], 2)

            with steps.loop(3, 4) as q:
                for j in range(4):
                    dve.wait_ge(tile_done.sem, tile_done.ready(S_IN2 + q * 4 + j))
                    steps(V.tensor_scalar(big[:, q * 4 + j, :], seam(4 + 2 * (j % 2)), 1.0, None, ALU.mult))
                    tell(dve, steps, dense_dve)
            steps(V.memset(v2[:, TT, :], 0.0))
            steps.wait()
            for c in range(2):
                columns = slice(2 * c * P, 2 * (c + 1) * P)
                dve.wait_ge(tile_done.sem, tile_done.ready(S_V2 + 2 * c + 1))
                steps(V.tensor_copy(v2[:, 0:TT, columns], bank(2 * c, 1024).rearrange("p (a b) -> p a b", b=2 * P)))
                steps(V.tensor_copy(v2[0:META, TT, columns], bank(4 + c, 2 * P)[0:META, :]))
                tell(dve, steps, dense_dve)
            dve.wait_ge(tile_done.sem, tile_done.ready(S_FG))
            steps(V.tensor_scalar(lf[0:NH, :], seam(6)[0:NH, :], vec[0:NH, BF:BF + 1], None, ALU.add))
            steps.wait()
            steps(stt(lf2[0:NH, :], lf[0:NH, :], -1.0, lf[0:NH, :], ALU.mult, ALU.max))
            tell(dve, steps, fg_done)
            for n in range(8):
                dve.wait_ge(sq_used.sem, sq_used.ready(4 * KT + n))
                steps.wait()
                steps(V.tensor_scalar(rstd[:], seam(2), 1.0 / DH, EPS, ALU.mult, ALU.add))
                tell(dve, steps, ms_ready)
                dve.wait_ge(root_ready.sem, root_ready.ready(4 + n))
                steps(V.reciprocal(rstd[:], rstd[:]))
                steps.wait()
                c = QN + n // 4
                steps(stt(big[:, n, :], big[:, n, :], vec[:, c:c + 1], rstd[:], ALU.mult, ALU.mult))
            steps.wait()
            steps(V.tensor_scalar(big[:, 0:4, :], big[:, 0:4, :], 0.125, None, ALU.mult))
            dve.wait_ge(fg_exp.sem, fg_exp.ready(0))
            steps(stt(lf[0:NH, :], lf[0:NH, :], 0.0, lf2[0:NH, :], ALU.min, ALU.subtract))
            steps.wait()
            steps(V.tensor_tensor_scan(cum[0:NH, :], ones[0:NH, 0:1].to_broadcast([NH, L2]), lf[0:NH, :], 0.0,
                                       ALU.mult, ALU.add))
            tell(dve, steps, cum_done)
            dve.wait_ge(cumt_done.sem, cumt_done.ready(0))
            steps(V.tensor_copy(cum_tok[:], bank(0, TT * NH).rearrange("p (a b) -> p a b", b=NH)))
            for g in range(4):
                u = big[:, 8 + g, :]
                src, lo = u, 0
                for a in range(g + 1):
                    dst = (pool_a, pool_b)[a % 2]
                    lo += 1 << a
                    steps.wait()
                    steps(V.tensor_tensor(dst[:, lo:], src[:, lo:], src[:, lo - (1 << a):L2 - (1 << a)], ALU.add))
                    src = dst
                steps.wait()
                steps(stt(pooled[:, g, :], src[:, META:], 1.0 / (2 << g), u[:, META:], ALU.mult, ALU.subtract))
                steps.wait()
                low_part(pooled_low[:, g, :], pooled[:, g, :], pooled_high[:, g, :])
            tell(dve, steps, pooled_done)
            dve.wait_ge(cumr_taken.sem, cumr_taken.ready(NH - 1))
            with steps.loop(HP, 3 + 5 * U + 2) as q:
                base = q * U + HP * U
                dve.wait_ge(s_done.sem, s_done.free(base, 1))
                dve.wait_ge(pv_done.sem, pv_done.free(base, 1))
                hold()
                steps(V.tensor_copy(stage2[0], big[:, q, :]))
                steps(V.tensor_copy(stage2[1], big[:, q + 4, :]))
                steps(V.tensor_copy(stage2_v[:], v2[:, :, bass.ds(q * P, P)]))
                tell(dve, steps, staged)
                for u in range(U + 1):
                    if u < U:
                        e, i = units[u]
                        w = META + P * (i + 1)
                        lg = logit2[u % 2][:, 0:w]
                        dve.wait_ge(s_done.sem, s_done.ready(base + u))
                        dve.wait_ge(t_done.sem, t_done.free(base + u, 2))
                        hold()
                        steps(stt(lg, seam(2 + 2 * (u % 2), w), cum_tok[:, i, bass.ds(q * 2 + e, 1)],
                                  cum_row[:, q * 2 + e, 0:w], ALU.add, ALU.add))
                        steps.wait()
                        steps(V.tensor_tensor(lg[:, w - P:w], lg[:, w - P:w], causal[:], ALU.add))
                        sync()
                        steps(V.tensor_reduce(col[:, 2 + u % 2:3 + u % 2], lg, AX, ALU.max, negate=True))
                        tell(dve, steps, s_taken)
                    if u >= 1:
                        finish_unit(base, u - 1, logit2, META + P * (units[u - 1][1] + 1))
                dve.wait_ge(pv_done.sem, pv_done.ready(base + U - 1))
                hold()
                low_part(mix_low[:, q, :], bank(1), mix_high[:, q, :])
                tell(dve, steps, y_taken)
            dve.wait_ge(tile_done.sem, tile_done.ready(S_POOL))
            for g in range(4):
                steps(V.tensor_scalar(mix[:, 4 + g, :], bank(2 + g), vec[:, PS + g:PS + g + 1], None, ALU.mult))
                steps.wait()
                low_part(mix_low[:, 4 + g, :], mix[:, 4 + g, :], mix_high[:, 4 + g, :])
            tell(dve, steps, dense_dve)
            with steps.loop(2, 4) as q:
                for j in range(4):
                    m = q * 4 + j
                    dve.wait_ge(tile_done.sem, tile_done.ready(S_OUT2 + m))
                    steps(V.tensor_tensor(x[:, m, META:], bank(j % 2), x[:, m, META:], ALU.add))
                    tell(dve, steps, dense_dve)
            tell(dve, steps, x_ready)
            norm(4, META, vec[:, N2:N2 + KT], 3)
            with steps.loop(FF // 2, 6) as q:
                for j in range(2):
                    dve.wait_ge(tile_done.sem, tile_done.ready(S_UP + q * 4 + 2 * j + 1))
                    dve.wait_ge(up_silu.sem, up_silu.ready(q * 2 + j))
                    steps(V.tensor_tensor(act_ff[:, q * 2 + j, :], silu[j][:], bank(2 * j + 1), ALU.mult))
                    steps.wait()
                    low_part(act_low[:, q * 2 + j, :], act_ff[:, q * 2 + j, :], act_high[:, q * 2 + j, :])
                    tell(dve, steps, dense_dve)
            with steps.loop(2, 4) as q:
                for m in range(4):
                    dve.wait_ge(tile_done.sem, tile_done.ready(S_DOWN + q * 12 + 3 * m + 2))
                    steps(V.tensor_tensor(outb[:, q * 4 + m, :], bank(m % 2), x[:, q * 4 + m, META:], ALU.add))
                    tell(dve, steps, o_ready)


def tiles(w):
    k, m = w.shape
    return w.reshape(k // P, P, m // P, P).transpose(2, 1, 0, 3).reshape(m // P, P, k)


def columns(vector):
    return vector.reshape(-1, P).T


def kernel(**inputs):
    import numpy as np
    import concourse.bacc as bacc
    from concourse.bass_utils import run_bass_kernel_spmd

    a = {n: np.asarray(v) for n, v in inputs.items()}
    w_in = a["w_in"][0]
    cut = np.split(w_in, np.cumsum([512, 512, 512, 512, 64, 8, 512, 512, 512, 1024]), axis=1)
    qa, ka, va, qi, ki, wi, qb, kb, vb, ga, gb = cut
    w_in2 = a["w_in_2"][0]
    q2, k2, v2, fg, u2 = np.split(w_in2, np.cumsum([512, 512, 512, 8]), axis=1)
    pad = lambda w, m: np.concatenate([w, np.zeros((w.shape[0], m - w.shape[1]), w.dtype)], axis=1)
    both = np.concatenate([a["w_proj_a"][0], a["w_proj_b"][0]], axis=0)
    gate, up = tiles(a["w_gate_2"][0]), tiles(a["w_up_2"][0])
    down = tiles(a["w_down_2"][0])
    down = np.concatenate([down, np.zeros((KT, P, (24 - FF) * P), down.dtype)], axis=2)
    down = down.reshape(KT, P, 3, D).transpose(0, 2, 1, 3).reshape(3 * KT, P, D)
    pools = pad(a["w_pool_2"][0].transpose(1, 0, 2).reshape(P, 4 * P), D)[None]
    stream = np.concatenate([
        tiles(np.concatenate([qi, ka, qa, kb, qb], axis=1)), tiles(np.concatenate([ki, ki], axis=1)),
        tiles(pad(wi, P)), tiles(np.concatenate([va, vb, ga, gb], axis=1)), tiles(both),
        tiles(a["w_out"][0]), tiles(a["peer_wq"][0]), tiles(np.concatenate([q2, k2, u2, v2], axis=1)),
        tiles(pad(fg, P)), pools, tiles(a["w_out_2"][0]),
        np.stack([gate, up], axis=1).reshape(2 * FF, P, D), down], axis=0)
    assert stream.shape[0] == TILES, stream.shape
    twice = lambda w: np.concatenate([w, w])
    small = np.concatenate([
        columns(a["b_ada"][0]), columns(a["norm1_g"][0]), columns(a["norm2_g"][0]), columns(a["final_g"]),
        columns(a["norm1_w_2"][0]), columns(a["norm2_w_2"][0]), columns(twice(a["q_norm_w_2"][0])),
        columns(twice(a["k_norm_w_2"][0])), columns(a["pool_scale_2"][0]),
        np.concatenate([a["b_fgate_2"][0], np.zeros(P - NH, w_in.dtype)])[:, None],
        np.zeros((P, 1), w_in.dtype)], axis=1)
    dist = np.arange(REL) - (P - 1)
    far = BUCKETS // 2 + (np.log(np.maximum(dist, 1).astype(np.float32) / (BUCKETS // 2))
                          / np.float32(np.log(128 / (BUCKETS // 2))) * (BUCKETS // 2)).astype(np.int32)
    bucket = np.where(dist < BUCKETS // 2, np.maximum(dist, 0), np.minimum(far, BUCKETS - 1))
    onehot = (np.arange(BUCKETS)[:, None] == bucket[None]).astype(np.float32)
    arrays = {
        "xT": a["x"][0].T, "metaT": a["meta_tokens_2"].T, "cond": a["c"],
        "w_ada": a["w_ada"][0].T.reshape(ADA, P, D), "small": small, "onehot": onehot,
        "rel_bias": a["rel_bias"], "w_stream": stream,
        "sub_keys": a["peer_sub_keys"][0].reshape(2 * PH, NK, P).transpose(2, 0, 1),
        "experts": np.concatenate([a["peer_u"][0], a["peer_v"][0]], axis=1),
    }
    arrays = {n: np.ascontiguousarray(v) for n, v in arrays.items()}
    nc = bacc.Bacc("TRN2", target_bir_lowering=False, num_devices=1)
    args = [nc.dram_tensor(n, v.shape, mybir.dt.from_np(v.dtype), kind="ExternalInput").ap()
            for n, v in arrays.items()]
    out = nc.dram_tensor("outT", (D, T), mybir.dt.float32, kind="ExternalOutput").ap()
    program(nc, *args, out)
    r = run_bass_kernel_spmd(nc, [arrays], core_ids=[0])
    return np.ascontiguousarray(r.results[0]["outT"].T)[None]
```

```python
import concourse.bass as bass
from concourse import mybir
from contextlib import ExitStack, contextmanager

P = 128
D = 1024
KT = D // P
T = 512
TT = T // P
META = 16
L2 = META + T
NH, DH = 8, 64
HP = NH // 2
TOPK = 128
BUCKETS = 32
REL = T + P - 1
PH, NK, PK = 8, 128, 16
ADA = 6 * D // P
FF = 2816 // P
EPS = 1e-6
GATED, TAKEN = -1e30, -3e38
SLOTS = 4
HIGHS = 2
G, GS = 2, 4
GROUPS = PK // G
BEST_AFTER = 2
IDX_SCALE = 64 ** -0.5 * 8 ** -0.5

B_ADA, G1, G2, GF, N1, N2, QN, PS, BF = 0, 48, 56, 64, 72, 80, 88, 90, 94
SMALL = 96

S_QK, S_KI, S_WI, S_V, S_GATE = 0, 20, 21, 22, 30
S_PROJ, S_OUT, S_WQ = 46, 54, 62
S_IN2, S_V2, S_FG, S_POOL, S_OUT2, S_UP, S_DOWN = 78, 90, 94, 95, 96, 104, 148
TILES = 172


V_QK, V_KI, V_WI, V_PROJ, V_OUT, V_IN2, V_V2, V_POOL, V_OUT2, V_UP = 0, 20, 21, 22, 30, 38, 50, 52, 53, 61
A_V, A_GATE, A_WQ = 0, 4, 20

SQ0, MS = [0, 8, 16, 24, 40], [0, 1, 2, 3, 12]


class Signal:
    CREDIT = 4

    def __init__(self, sem):
        self.sem = sem

    def ready(self, n):
        return n + 1 + self.CREDIT

    def free(self, n, depth):
        return n + 1 + self.CREDIT - depth


class Steps:

    def __init__(self, eng, sem):
        self.eng, self.sem, self.n, self.shift = eng, sem, 0, 0

    def __call__(self, instruction):
        instruction.then_inc(self.sem, 1)
        self.n += 1

    def wait(self):
        self.eng.wait_ge(self.sem, self.shift + self.n)

    @contextmanager
    def loop(self, count, per):
        with self.eng.Fori(0, count) as i:
            base, shift = self.n, self.shift
            self.shift = shift + i * per
            yield i
            assert self.n - base == per, (self.n - base, per)
        self.n, self.shift = base + per * count, shift


def program(nc, xT, metaT, cond, w_ada, small, onehot, rel_bias, w_stream, sub_keys, experts, outT):
    f32, u32, f32r = mybir.dt.float32, mybir.dt.uint32, mybir.dt.float32r
    ALU, ACT, AX = mybir.AluOpType, mybir.ActivationFunctionType, mybir.AxisListType.X
    rel_dram = nc.dram_tensor("rel_rows", (NH, REL + 1), f32, kind="Internal").ap()

    ctx = ExitStack()
    with ctx:
        def sb(name, shape, dtype=f32):
            return ctx.enter_context(nc.sbuf_tensor(name, shape, dtype))

        place = {}

        def sb_placed(name, shape, dtype=f32):
            place[name] = -(-nc.sbuf_base // 32) * 32
            return sb(name, shape, dtype)

        def over(name, shape, other, dtype=f32r, start=0):
            return nc.alloc_sbuf_tensor_at(name, shape, dtype, offset=place[other] + 4 * start)

        def sem(name):
            return ctx.enter_context(nc.semaphore(name))

        x = sb("x", [P, KT, L2])
        hn = sb_placed("hn", [P, KT, L2])
        hn_low = over("hn_low", [P, KT, L2], "hn")
        hn_high = sb_placed("hn_high", [P, KT, L2], f32r)
        ring = sb_placed("ring", [P, SLOTS, D])
        ring_low = over("ring_low", [P, SLOTS, D], "ring")
        w_high = sb("w_high", [P, HIGHS, D], f32r)
        vec = sb("vec", [P, SMALL])
        mod = sb("mod", [P, ADA])
        gain1 = sb("gain1", [P, KT])
        gain2 = sb("gain2", [P, KT])
        ident = sb("ident", [P, P])
        ones = sb("ones", [P, P])
        neg_ones = sb("neg_ones", [P, P])
        neg_tri = sb("neg_tri", [P, P])
        ident_r = sb("ident_r", [P, P], f32r)
        half_ones = sb("half_ones", [P, P])
        causal = sb("causal", [P, P])
        strict = sb("strict", [P, P])
        sq = sb("sq", [P, 2, L2])
        rstd = sb("rstd", [P, L2])
        col = sb("col", [P, 16])
        rel_sb = sb("rel_sb", [BUCKETS, NH])

        ARENA = 31100
        arena = sb_placed("arena", [P, ARENA])
        used = [0]

        def take(*shape):
            n = 1
            for s in shape:
                n *= s
            a = arena[:, used[0]:used[0] + n]
            used[0] += n
            assert used[0] <= ARENA, used[0]
            if len(shape) == 2:
                a = a.rearrange("p (a b) -> p a b", b=shape[1])
            if len(shape) == 3:
                a = a.rearrange("p (a b c) -> p a b c", b=shape[1], c=shape[2])
            return a

        def take_rounded(name, *shape):
            a = over(name, [P, *shape], "arena", start=used[0])
            take(*shape)
            return a

        qk = take(20, T)
        QI, KA, QA, KB, QB = 0, 4, 8, 12, 16
        ki = take(T)
        wi = take(TT, NH)
        v = take(TT, 2 * NH * DH)
        gates_at = used[0]
        gates = take(16, T)
        masks_at = used[0]
        mask = [take(P * (i + 1)) for i in range(TT)]
        probT = [take(TT, P) for _ in range(2)]
        stage = [take(T) for _ in range(2)]
        stage_v = take(TT, P)
        work = used[0]
        bias = take(NH, T)
        y = bias
        y_low = over("y_low", [P, NH, T], "arena", start=work)
        logit = [sq[:, c, 0:T] for c in range(2)]
        used[0] = work
        relu_all = take(2 * T)
        relu = [relu_all[:, 0:T], relu_all[:, T:2 * T]]
        score = take(T)
        onehot_sb = take(1024)[0:BUCKETS, 0:REL]
        rel_row = relu_all[0:NH, 0:REL]
        used[0] = work + 3 * T
        v_high = take_rounded("v_high", 2, D)
        used[0] = 0
        y_high = [take_rounded("ya_high", HP, T)]
        stage_h = logit
        sp = [take(T - P * i) for i in range(TT)]
        az = [[take(T - P * i) for i in range(TT)] for _ in range(2)]
        assert used[0] <= 12 * T
        used[0] = 4 * T
        merged_high = take_rounded("merged_high", KT, T)
        merged_low = over("merged_low", [P, KT, T], "arena", start=gates_at)
        used[0] = masks_at
        y_high.append(take_rounded("yb_high", HP, T))
        used[0] = gates_at
        ada = take(SLOTS, D)
        cvec = take(D)
        junk_ada = take(D)
        bias_rows = gates[:, 0:NH, :]
        used[0] = 0
        sc = take(TT, 16, NK)
        h_tok = take(TT, D)
        keys = take(16, NK)
        qh = [take(T) for _ in range(2)]
        used[0] -= 16 * NK + 2 * T
        rows = take(GS, G, 2 * D)
        spare = over("spare", [P, 3 * D], "hn_high", f32)
        h_cur = spare[:, 0:D]
        acc = spare[:, D:2 * D]
        diag = spare[:, 2 * D:3 * D].rearrange("p (a b) -> p a b", b=G * P)
        eidx = sb("eidx", [P, 2, P], u32)
        eslot = sb("eslot", [P, GS, G], u32)
        wgt = take(2, P)
        pre = take(GS, G)
        coef = take(GS, G)
        half = take(2, NK)
        top = take(2, PK)
        topf = take(2, PK)
        cand = take(PK, PK)
        best = take(PK)
        posf = take(2, PK)
        hot = take(2, PK * PK)
        iota16 = sb("iota16", [P, PK])
        epart = take(2, PK)
        topi = sb("topi", [P, 2, PK], u32)
        pos = sb("pos", [P, PK], u32)
        pos2 = sb("pos2", [P, 2, PK], u32)
        used[0] = 0
        big = take(12, L2)
        v2 = take(TT + 1, NH * DH)
        lf = take(L2)
        lf2 = take(L2)
        cum = take(L2)
        cum_tok = take(TT, NH)
        cum_row = take(NH, L2)
        mix_low = over("mix_low", [P, 8, T], "arena", start=used[0])
        mix = take(8, T)
        v2_high = over("v2_high", [P, 2, D], "arena", start=used[0])
        mix_high = take_rounded("mix_high", 8, T)
        stage2 = [take(L2) for _ in range(2)]
        stage2_v = take(TT + 1, P)
        logit2 = [take(L2) for _ in range(2)]
        probT2 = [take(TT + 1, P) for _ in range(2)]
        pool_a = take(L2)
        pool_b = take(L2)
        pooled_low = over("pooled_low", [P, 4, T], "arena", start=used[0])
        pooled = take(4, T)
        meta_parts = take_rounded("meta_parts", KT, 2 * META)
        pooled_high = mix_high[:, 4:8, :]
        used[0] = 0
        act_low = over("act_low", [P, FF, T], "arena", start=used[0])
        act_ff = take(FF, T)
        act_high = take_rounded("act_high", FF, T)
        silu = [take(T) for _ in range(2)]
        outb = take(KT, T)

        psum = ctx.enter_context(nc.psum_tensor("psum", [P, 8 * 512], f32))

        def bank(b, width=512, start=0):
            return psum[:, b * 512 + start:b * 512 + start + width]

        def seam(b, width=L2):
            return psum[:, (b + 1) * 512 - META:(b + 1) * 512 - META + width]

        zs_all = [bank(2), bank(3, 384), bank(4, 256), bank(3, 128, 384)]
        us_all = [bank(5), bank(7), bank(5), bank(7)]

        ring_ready = [sem(f"ring_ready{i}") for i in range(SLOTS)]
        x_loaded, vec_loaded, meta_loaded, cond_loaded = (sem(n) for n in (
            "x_loaded", "vec_loaded", "meta_loaded", "cond_loaded"))
        onehot_loaded, rel_stored, bias_loaded, keys_loaded = (sem(n) for n in (
            "onehot_loaded", "rel_stored", "bias_loaded", "keys_loaded"))
        ada_ready = [sem(f"ada_ready{i}") for i in range(SLOTS)]
        rows_ready = [sem(f"rows_ready{i}") for i in range(GS)]
        out_stored = sem("out_stored")
        consts_done = sem("consts_done")

        signals = {"pe": [], "act": [], "dve": [], "pool": []}

        def signal(engine, name):
            s = Signal(sem(name))
            signals[engine].append(s)
            return s

        tile_done = signal("pe", "tile_done")
        ada_used = signal("dve", "ada_used")
        cond_done = signal("act", "cond_done")
        w_split = signal("pool", "w_split")
        normed = signal("dve", "normed")
        high_ready = signal("act", "high_ready")
        sq_ready = signal("act", "sq_ready")
        sq_used = signal("pe", "sq_used")
        root_ready = signal("act", "root_ready")
        ms_ready = signal("dve", "ms_ready")
        hn_ready = signal("dve", "hn_ready")
        x_ready = signal("dve", "x_ready")
        dense_dve = signal("dve", "dense_dve")
        dense_act = signal("act", "dense_act")
        rel_done = signal("pe", "rel_done")
        rel_copied = signal("dve", "rel_copied")
        idx_done = signal("pe", "idx_done")
        relu_done = signal("act", "relu_done")
        relu_used = signal("dve", "relu_used")
        staged = signal("dve", "staged")
        s_done = signal("pe", "s_done")
        s_taken = signal("dve", "s_taken")
        exp_done = signal("act", "exp_done")
        p_done = signal("dve", "p_done")
        t_done = signal("pe", "t_done")
        t_taken = signal("act", "t_taken")
        pv_done = signal("pe", "pv_done")
        y_taken = signal("dve", "y_taken")
        z_done = signal("pe", "z_done")
        values_staged = signal("dve", "values_staged")
        soft_done = signal("act", "soft_done")
        sp_done = signal("dve", "sp_done")
        sp_gated = signal("pool", "sp_gated")
        u_done = signal("pe", "u_done")
        half_zeroed = signal("pool", "half_zeroed")
        a_done = signal("act", "a_done")
        yb_done = signal("pe", "yb_done")
        yb_taken = signal("dve", "yb_taken")
        gates_done = signal("act", "gates_done")
        key_done = signal("pe", "key_done")
        key_taken = signal("act", "key_taken")
        htok_done = signal("pe", "htok_done")
        htok_taken = signal("act", "htok_taken")
        chosen = signal("dve", "chosen")
        eidx_taken = signal("pool", "eidx_taken")
        best_done = signal("dve", "best_done")
        best_exp = signal("act", "best_exp")
        pre_done = signal("dve", "pre_done")
        gelu_done = signal("act", "gelu_done")
        coef_done = signal("dve", "coef_done")
        diag_done = signal("act", "diag_done")
        rows_used = signal("pe", "rows_used")
        acc_done = signal("act", "acc_done")
        f_done = signal("pe", "f_done")
        fg_done = signal("dve", "fg_done")
        fg_exp = signal("act", "fg_exp")
        meta_ready = signal("dve", "meta_ready")
        cum_done = signal("dve", "cum_done")
        cumt_done = signal("pe", "cumt_done")
        cumr_done = signal("pe", "cumr_done")
        cumr_taken = signal("act", "cumr_taken")
        pooled_done = signal("dve", "pooled_done")
        up_silu = signal("act", "up_silu")
        o_ready = signal("dve", "o_ready")
        cum_pick = [ident[0:NH, h:h + 1].to_broadcast([NH, P]) for h in range(NH)]
        own = {e: sem(f"{e}_step") for e in ("act", "dve", "pool")}
        held = {e: sem(f"{e}_held") for e in ("act", "dve", "pool", "pe")}

        def start(eng, name):
            for s in signals[name]:
                eng.sem_inc(s.sem, Signal.CREDIT)

        def tell(eng, steps, s):
            steps.wait()
            eng.sem_inc(s.sem, 1)

        block = ctx.enter_context(nc.Block())

        @block.sync
        def _(sp_eng):
            eng = sp_eng
            def ada_load(j, n0, q=0, per=0):
                if n0 >= SLOTS:
                    eng.wait_ge(ada_used.sem, ada_used.free(n0 + q * per, SLOTS))
                eng.dma_start(ada[:, j, :], w_ada[n0 + q * per]).then_inc(ada_ready[j], 16)

            def refill(q, j):
                eng.wait_ge(tile_done.sem, tile_done.ready(q * SLOTS + j))
                eng.dma_start(ring[:, j, :], w_stream[(q + 1) * SLOTS + j]).then_inc(ring_ready[j], 16)

            for j in range(SLOTS):
                ada_load(j, j)
            eng.dma_start(x[:, :, META:], xT.rearrange("(k p) t -> p k t", p=P)).then_inc(x_loaded, 16)
            eng.dma_start(vec[:], small).then_inc(vec_loaded, 16)
            with eng.Fori(0, 2) as q:
                for j in range(SLOTS):
                    ada_load(j, SLOTS + j, q, SLOTS)
            for j in range(SLOTS):
                eng.dma_start(ring[:, j, :], w_stream[j]).then_inc(ring_ready[j], 16)
            for n in range(3 * SLOTS, 5 * SLOTS):
                ada_load(n % SLOTS, n)
            eng.dma_start(x[:, :, 0:META], metaT.rearrange("(k p) t -> p k t", p=P))\
               .then_inc(meta_loaded, 16)
            with eng.Fori(0, 3) as q:
                for j in range(SLOTS):
                    refill(q, j)
                    for c in range(2):
                        ada_load((2 * j + c) % SLOTS, 5 * SLOTS + 2 * j + c, q, 2 * SLOTS)
            for j in range(SLOTS):
                refill(3, j)
                for n in range(11 * SLOTS + 2 * j, min(11 * SLOTS + 2 * j + 2, ADA)):
                    ada_load(n % SLOTS, n)
            with eng.Fori(4, TILES // SLOTS - 1) as q:
                for j in range(SLOTS):
                    refill(q, j)
            for m in range(KT):
                eng.wait_ge(o_ready.sem, o_ready.ready(m))
                eng.dma_start(outT[m * P:(m + 1) * P, :], outb[:, m, :]).then_inc(out_stored, 16)
            eng.wait_ge(out_stored, 16 * KT)

        @block.tensor
        def _(pe):
            mm = nc.tensor.matmul
            start(pe, "pe")

            def tile(t0, j, q=0, per=0):
                n = t0 + j
                pe.wait_ge(w_split.sem, w_split.ready(n + q * per))
                return (w_high[:, n % HIGHS, :].rearrange("p (k m) -> p k m", m=P),
                        ring_low[:, n % SLOTS, :].rearrange("p (k m) -> p k m", m=P))

            def part(a, *index):
                return tuple(half[index] for half in a)

            def product(out, a, b, start, stop):
                mm(out, a[0], b[0], start=start, stop=False)
                mm(out, a[0], b[1], start=False, stop=False)
                return mm(out, a[1], b[0], start=False, stop=stop)

            def norm(c, with_meta):
                for k in range(KT):
                    pe.wait_ge(sq_ready.sem, sq_ready.ready(SQ0[c] + k))
                    if k == 0 and c:
                        pe.wait_ge(ms_ready.sem, ms_ready.ready(MS[c] - 1))
                    if with_meta:
                        mm(seam(2, META), ones[:], sq[:, k % 2, 0:META], start=k == 0, stop=k == KT - 1)
                    mm(bank(3), ones[:], sq[:, k % 2, META:], start=k == 0, stop=k == KT - 1)\
                        .then_inc(sq_used.sem, 1)

            def dense(out, w, rhs, norm_part=None):
                for k in range(KT):
                    if norm_part is not None:
                        pe.wait_ge(hn_ready.sem, hn_ready.ready(norm_part * KT + k))
                    last = product(out, part(w, ALL, k), part(rhs, ALL, k), k == 0, k == KT - 1)
                return last

            def by_token(out, w, tokens):
                for k in range(KT):
                    last = product(out, part(hn_parts, ALL, k, tokens), part(w, ALL, k), k == 0, k == KT - 1)
                return last

            def tile_pair(t0, high):
                pe.wait_ge(w_split.sem, w_split.ready(t0 + 1))
                low = ring_low[:, t0 % SLOTS:t0 % SLOTS + 2, :]
                return tuple(a.rearrange("p c (k m) -> p k c m", m=P) for a in (high[:], low))

            def pair_by_token(b, w):
                for i in range(TT):
                    last = by_token(bank(b + i // 2, 2 * P, i % 2 * 2 * P), w, slice(META + i * P, META + (i + 1) * P))
                last.then_inc(tile_done.sem, 2)

            ALL = slice(None)
            hn_parts = (hn_high, hn_low)

            pe.wait_ge(consts_done, 1)
            pe.wait_ge(onehot_loaded, 32)
            for a in range(2):
                w = min(512, REL - a * 512)
                last = mm(bank(4 + a, w)[0:NH, :], rel_sb[:], onehot_sb[:, a * 512:a * 512 + w], start=True, stop=True)
            last.then_inc(rel_done.sem, 1)
            norm(0, False)
            rhs = part(hn_parts, ALL, ALL, slice(META, L2))
            with pe.Fori(0, 5) as q:
                for j in range(4):
                    w = tile(S_QK, j, q, 4)
                    pe.wait_ge(dense_dve.sem, dense_dve.free(q * 4 + j, 2))
                    dense(bank(j % 2), w, rhs, 0 if j == 0 else None).then_inc(tile_done.sem, 1)
            w = tile(S_KI, 0)
            pe.wait_ge(dense_dve.sem, dense_dve.free(V_KI, 2))
            dense(bank(0), w, rhs).then_inc(tile_done.sem, 1)
            w = tile(S_WI, 0)
            pe.wait_ge(dense_dve.sem, dense_dve.free(V_WI, 2))
            w = part(w, ALL, ALL, slice(0, NH))
            for i in range(TT):
                last = by_token(bank(1, NH, i * NH), w, slice(META + i * P, META + (i + 1) * P))
            last.then_inc(tile_done.sem, 1)
            def v_pair(p):
                w = tile_pair(S_V + 2 * p, (w_high, v_high)[p % 2])
                pe.wait_ge(dense_act.sem, dense_act.free(A_V + p, 2))
                pair_by_token(2 * (p % 2), w)

            pe.wait_ge(dense_dve.sem, dense_dve.ready(V_WI))
            n = 0
            for i in range(1, TT):
                for h in range(NH):
                    pe.wait_ge(relu_done.sem, relu_done.free(n, 2))
                    r = slice(64 * (h % 2), 64 * (h % 2) + 64)
                    mm(bank(4 + n % 2, P * (i + 1)), qk[r, QI + h // 2, i * P:(i + 1) * P],
                       ki[r, 0:P * (i + 1)], start=True, stop=True).then_inc(idx_done.sem, 1)
                    n += 1
                v_pair(i - 1)
            v_pair(TT - 1)

            units = [(e, i) for e in range(2) for i in range(TT)]
            U = len(units)

            pe.wait_ge(relu_done.sem, relu_done.ready(23))
            with pe.Fori(0, HP) as q:
                pe.wait_ge(staged.sem, staged.ready(q))

                def scores(u):
                    e, i = units[u]
                    r = slice(64 * e, 64 * e + 64)
                    pe.wait_ge(s_taken.sem, s_taken.free(q * U + u, 2))
                    mm(bank(2 + u % 2, P * (i + 1)), stage[0][r, i * P:(i + 1) * P],
                       stage[1][r, 0:P * (i + 1)], start=True, stop=True).then_inc(s_done.sem, 1)

                def transposes(u):
                    pe.wait_ge(p_done.sem, p_done.ready(q * U + u))
                    pe.wait_ge(t_taken.sem, t_taken.free(q * U + u, 2))
                    for j in range(units[u][1] + 1):
                        last = nc.tensor.transpose(bank(4 + u % 2, P, j * P),
                                                   logit[u % 2][:, j * P:(j + 1) * P], ident[:])
                    last.then_inc(t_done.sem, 1)

                def values(u):
                    e, i = units[u]
                    if u == 0:
                        pe.wait_ge(y_taken.sem, y_taken.free(q, 1))
                    pe.wait_ge(t_taken.sem, t_taken.ready(q * U + u))
                    for j in range(i + 1):
                        last = mm(bank(6, P, i * P)[64 * e:64 * e + 64, :], stage_v[:, j, 64 * e:64 * e + 64],
                                  probT[u % 2][:, j, :], start=j == 0, stop=j == i)
                    last.then_inc(pv_done.sem, 1)

                scores(0)
                for u in range(U + 2):
                    if u + 1 < U:
                        scores(u + 1)
                    if u % 2 == 1 and u < U:
                        w = tile(S_GATE, u // 2, q, 4)
                        pe.wait_ge(dense_act.sem, dense_act.free(A_GATE + q * 4 + u // 2, 2))
                        dense(bank(u // 2 % 2), w, rhs).then_inc(tile_done.sem, 1)
                    if 1 <= u <= U:
                        transposes(u - 1)
                    if u >= 2:
                        values(u - 2)

            pe.wait_ge(y_taken.sem, y_taken.ready(HP - 1))
            def z_products(q, e):
                if e == 0:
                    pe.wait_ge(staged.sem, staged.ready(HP + q))
                pe.wait_ge(sp_done.sem, sp_done.free((q * 2 + e) * TT, 1))
                for i in reversed(range(TT)):
                    mm(zs_all[i], stage[0][:, i * P:(i + 1) * P], stage_h[e][:, i * P:T],
                       start=True, stop=True).then_inc(z_done.sem, 1)

            def sums(q, e):
                for n, i in enumerate(reversed(range(TT))):
                    item = (q * 2 + e) * TT + n
                    pe.wait_ge(sp_gated.sem, sp_gated.ready(item))
                    pe.wait_ge(a_done.sem, a_done.free(item, 2))
                    mm(us_all[n][:, 0:T - i * P], stage[0][:, i * P:(i + 1) * P], stage_h[e][:, i * P:T],
                       start=True, stop=False)
                    mm(us_all[n][:, 0:P], ident[:], strict[:], start=False, stop=False)
                    for j in range(i, TT):
                        last = mm(us_all[n][:, (j - i) * P:T - i * P], neg_tri[:] if j == i else neg_ones[:],
                                  sp[j], start=False, stop=j == TT - 1)
                    last.then_inc(u_done.sem, 1)

            def weighted(q, e):
                pe.wait_ge(a_done.sem, a_done.ready((q * 2 + e) * TT + TT - 1))
                if e == 0:
                    pe.wait_ge(values_staged.sem, values_staged.ready(q))
                    pe.wait_ge(yb_taken.sem, yb_taken.free(q, 1))
                for i in range(TT):
                    last = mm(bank(6, T - i * P, i * P)[64 * e:64 * e + 64, :],
                              stage_v[:, i, 64 * e:64 * e + 64], az[e][i], start=i == 0, stop=i == TT - 1)
                last.then_inc(yb_done.sem, 1)

            z_products(0, 0)
            with pe.Fori(0, HP - 1) as q:
                sums(q, 0)
                z_products(q, 1)
                weighted(q, 0)
                sums(q, 1)
                z_products(q + 1, 0)
                weighted(q, 1)
            sums(HP - 1, 0)
            z_products(HP - 1, 1)
            weighted(HP - 1, 0)
            sums(HP - 1, 1)
            weighted(HP - 1, 1)

            pe.wait_ge(yb_taken.sem, yb_taken.ready(HP - 1))
            pe.wait_ge(dense_act.sem, dense_act.ready(A_WQ - 1))
            with pe.Fori(0, 2) as q:
                for j in range(4):
                    w = tile(S_PROJ, j, q, 4)
                    pe.wait_ge(dense_dve.sem, dense_dve.free(V_PROJ + q * 4 + j, 2))
                    for e in range(2):
                        for k in range(HP):
                            last = product(bank(2 * (j % 2) + e), part(w, ALL, HP * e + k),
                                           (y_high[e][:, k, :], y_low[:, HP * e + k, :]), k == 0, k == HP - 1)
                    last.then_inc(tile_done.sem, 1)
            pe.wait_ge(dense_dve.sem, dense_dve.ready(V_OUT - 1))
            with pe.Fori(0, 2) as q:
                for j in range(4):
                    w = tile(S_OUT, j, q, 4)
                    pe.wait_ge(dense_dve.sem, dense_dve.free(V_OUT + q * 4 + j, 2))
                    dense(bank(j % 2), w, (merged_high, merged_low)).then_inc(tile_done.sem, 1)

            norm(1, False)
            pe.wait_ge(keys_loaded, 16)

            def query(j, q=0, per=0):
                w = tile(S_WQ, j, q, per)
                pe.wait_ge(dense_act.sem, dense_act.free(A_WQ + q * per + j, 2))
                dense(bank(j % 2), w, rhs, 1 if j == 0 else None).then_inc(tile_done.sem, 1)

            def key_scores(j, q=0, per=0):
                pe.wait_ge(dense_act.sem, dense_act.ready(A_WQ + q * per + j))
                pe.wait_ge(key_taken.sem, key_taken.free(q * per + j, 2))
                for i in range(TT):
                    last = mm(bank(2 + j % 2, P, i * P), qh[j % 2][:, i * P:(i + 1) * P],
                              keys[:, q * per + j, :], start=True, stop=True)
                last.then_inc(key_done.sem, 1)

            query(0)
            with pe.Fori(0, 3) as q:
                for j in range(4):
                    query(j + 1, q, 4)
                    key_scores(j, q, 4)
            for j in range(12, 15):
                query(j + 1)
                key_scores(j)
            key_scores(15)
            for n in range(TT):
                pe.wait_ge(htok_taken.sem, htok_taken.free(n, 2))
                tokens = slice(META + n * P, META + (n + 1) * P)
                for k in range(KT):
                    out = bank(4 + 2 * (n % 2), P, k * P)
                    mm(out, hn_high[:, k, tokens], ident_r[:], start=True, stop=False)
                    last = mm(out, hn_low[:, k, tokens], ident_r[:], start=False, stop=True)
                last.then_inc(htok_done.sem, 1)
            def v_rows(n, g, first, last_one):
                s = g % GS
                pe.wait_ge(diag_done.sem, diag_done.ready(n + g))
                for c in range(G):
                    for a in range(2):
                        last = mm(bank(2 + a), diag[:, s, c * P:(c + 1) * P], rows[:, s, c, D + a * 512:D + (a + 1) * 512],
                                  start=first and c == 0, stop=last_one and c == G - 1)
                last.then_inc(rows_used.sem, 1)

            with pe.Fori(0, TT) as n:
                tile_groups = n * (PH * GROUPS)
                pe.wait_ge(acc_done.sem, acc_done.free(n, 1))
                for g in range(GROUPS):
                    v_rows(tile_groups, g, g == 0, False)
                with pe.Fori(1, PH - 1) as h:
                    for g in range(GROUPS):
                        v_rows(tile_groups + h * GROUPS, g, False, False)
                for g in range(GROUPS):
                    v_rows(tile_groups + (PH - 1) * GROUPS, g, False, g == GROUPS - 1)
                pe.wait_ge(acc_done.sem, acc_done.ready(n))
                for k in range(KT):
                    last = nc.tensor.transpose(bank(4, P, k * P), acc[:, k * P:(k + 1) * P], ident[:])
                last.then_inc(f_done.sem, 1)
            norm(2, False)
            norm(3, True)

            meta = part(hn_parts, ALL, ALL, slice(0, META))

            def in2(j, q=0, per=0):
                w = tile(S_IN2, j, q, per)
                pe.wait_ge(dense_dve.sem, dense_dve.free(V_IN2 + q * per + j, 2))
                first_user = not per and j == 0
                dense(bank(5 + 2 * (j % 2)), w, rhs, 2 if first_user else None)
                if first_user:
                    pe.wait_ge(meta_ready.sem, meta_ready.ready(0))
                out = bank(4 + 2 * (j % 2), 2 * META, 512 - 2 * META)
                for k in range(KT):
                    for c in range(2):
                        last = mm(out, w[c][:, k, :], meta_parts[:, k, :], start=k + c == 0, stop=k + c == KT)
                last.then_inc(tile_done.sem, 1)

            for j in range(4):
                in2(j)
            with pe.Fori(0, 2) as q:
                for j in range(4):
                    in2(4 + j, q, 4)
                    pe.wait_ge(sq_ready.sem, sq_ready.ready(q * 4 + (4 * KT + j)))
                    pe.wait_ge(ms_ready.sem, ms_ready.ready(q * 4 + (3 + j)))
                    mm(seam(2, META), half_ones[:], sq[:, j % 2, 0:META], start=True, stop=True)
                    mm(bank(3), half_ones[:], sq[:, j % 2, META:], start=True, stop=True).then_inc(sq_used.sem, 1)
            pe.wait_ge(dense_dve.sem, dense_dve.ready(V_V2 - 1))
            for c, high in enumerate((w_high, v2_high)):
                w = tile_pair(S_V2 + 2 * c, high)
                if c:
                    pe.wait_ge(ms_ready.sem, ms_ready.ready(11))
                by_token(bank(4 + c, 2 * P)[0:META, :], w, slice(0, META))
                pair_by_token(2 * c, w)
            w = tile(S_FG, 0)
            w = part(w, ALL, ALL, slice(0, NH))
            dense(seam(6, META)[0:NH, :], w, meta)
            last = dense(bank(7)[0:NH, :], w, rhs)
            last.then_inc(tile_done.sem, 1)
            pe.wait_ge(cum_done.sem, cum_done.ready(0))
            for i in range(TT):
                last = nc.tensor.transpose(bank(0, NH, i * NH), cum[0:NH, META + i * P:META + (i + 1) * P],
                                           ident[0:NH, 0:NH])
            last.then_inc(cumt_done.sem, 1)
            for h in range(NH):
                pe.wait_ge(cumr_taken.sem, cumr_taken.free(h, 2))
                mm(seam(4 + 2 * (h % 2), META), cum_pick[h], cum[0:NH, 0:META], start=True, stop=True)
                mm(bank(5 + 2 * (h % 2)), cum_pick[h], cum[0:NH, META:], start=True, stop=True).then_inc(cumr_done.sem, 1)
            pe.wait_ge(cumr_taken.sem, cumr_taken.ready(NH - 1))
            with pe.Fori(0, HP) as q:
                pe.wait_ge(staged.sem, staged.ready(2 * HP + q))

                def scores(u):
                    e, i = units[u]
                    r = slice(64 * e, 64 * e + 64)
                    pe.wait_ge(s_taken.sem, s_taken.free(HP * U + q * U + u, 2))
                    lhsT = stage2[0][r, META + i * P:META + (i + 1) * P]
                    mm(seam(2 + 2 * (u % 2), META), lhsT, stage2[1][r, 0:META], start=True, stop=True)
                    mm(bank(3 + 2 * (u % 2), P * (i + 1)), lhsT, stage2[1][r, META:META + P * (i + 1)],
                       start=True, stop=True).then_inc(s_done.sem, 1)

                def transposes(u):
                    item = HP * U + q * U + u
                    pe.wait_ge(p_done.sem, p_done.ready(item))
                    pe.wait_ge(t_taken.sem, t_taken.free(item, 2))
                    for j in range(units[u][1] + 1):
                        nc.tensor.transpose(bank(6 + u % 2, P, j * P),
                                            logit2[u % 2][:, META + j * P:META + (j + 1) * P], ident[:])
                    pe.wait_ge(t_taken.sem, t_taken.free(item, 1))
                    nc.tensor.transpose(bank(0, P), logit2[u % 2][:, 0:P], ident[:]).then_inc(t_done.sem, 1)

                def values(u):
                    e, i = units[u]
                    if u == 0:
                        pe.wait_ge(y_taken.sem, y_taken.free(HP + q, 1))
                    pe.wait_ge(t_taken.sem, t_taken.ready(HP * U + q * U + u))
                    out = bank(1, P, i * P)[64 * e:64 * e + 64, :]
                    mm(out, stage2_v[:, TT, 64 * e:64 * e + 64], probT2[u % 2][:, TT, :],
                       start=True, stop=False)
                    for j in range(i + 1):
                        last = mm(out, stage2_v[:, j, 64 * e:64 * e + 64],
                                  probT2[u % 2][:, j, :], start=False, stop=j == i)
                    last.then_inc(pv_done.sem, 1)

                scores(0)
                for u in range(U + 2):
                    if u + 1 < U:
                        scores(u + 1)
                    if 1 <= u <= U:
                        transposes(u - 1)
                    if u >= 2:
                        values(u - 2)
            w = tile(S_POOL, 0)
            pe.wait_ge(pooled_done.sem, pooled_done.ready(0))
            pe.wait_ge(y_taken.sem, y_taken.ready(2 * HP - 1))
            for g in range(4):
                last = product(bank(2 + g), part(w, ALL, g), (pooled_high[:, g, :], pooled_low[:, g, :]), True, True)
            last.then_inc(tile_done.sem, 1)
            pe.wait_ge(dense_dve.sem, dense_dve.ready(V_POOL))
            with pe.Fori(0, 2) as q:
                for j in range(4):
                    w = tile(S_OUT2, j, q, 4)
                    pe.wait_ge(dense_dve.sem, dense_dve.free(V_OUT2 + q * 4 + j, 2))
                    dense(bank(j % 2), w, (mix_high, mix_low)).then_inc(tile_done.sem, 1)
            norm(4, False)
            with pe.Fori(0, FF // 2) as q:
                for j in range(4):
                    w = tile(S_UP, j, q, 4)
                    if j % 2 == 0:
                        pe.wait_ge(dense_dve.sem, dense_dve.free(V_UP + q * 2 + j // 2, 2))
                    dense(bank(j), w, rhs, 3 if j == 0 else None).then_inc(tile_done.sem, 1)
            pe.wait_ge(dense_dve.sem, dense_dve.ready(V_UP + FF - 1))
            with pe.Fori(0, 2) as q:
                for m in range(4):
                    pe.wait_ge(o_ready.sem, o_ready.free(q * 4 + m, 2))
                    for c in range(3):
                        w = tile(S_DOWN, 3 * m + c, q, 12)
                        for k in range(min(8, FF - 8 * c)):
                            kk = 8 * c + k
                            last = product(bank(m % 2), part(w, ALL, k), (act_high[:, kk, :], act_low[:, kk, :]),
                                           kk == 0, kk == FF - 1)
                        last.then_inc(tile_done.sem, 1)

        @block.scalar
        def _(act):
            op = nc.scalar.activation
            start(act, "act")
            steps = Steps(act, own["act"])

            def hold():
                act.sem_inc(held["act"], 1)

            act.dma_start(cvec[:], cond.to_broadcast([P, D])).then_inc(cond_loaded, 16)
            act.dma_start(rel_sb[:], rel_bias).then_inc(onehot_loaded, 16)
            act.dma_start(onehot_sb, onehot).then_inc(onehot_loaded, 16)
            act.wait_ge(cond_loaded, 16)
            op(cvec[:], cvec[:], ACT.Silu).then_inc(cond_done.sem, 1)

            def high_parts(c, first, shift=None):
                for k in range(KT):
                    act.wait_ge(normed.sem, normed.ready(c * KT + k))
                    if shift is None:
                        ins = op(hn_high[:, k, first:], hn[:, k, first:], ACT.Copy)
                    else:
                        ins = op(hn_high[:, k, first:], hn[:, k, first:], ACT.Identity, bias=shift[:, k:k + 1])
                    ins.then_inc(high_ready.sem, 1)

            def norm(c, first):
                for k in range(KT):
                    act.wait_ge(sq_used.sem, sq_used.free(SQ0[c] + k, 2))
                    op(sq[:, k % 2, first:], x[:, k, first:], ACT.Square).then_inc(sq_ready.sem, 1)
                act.wait_ge(ms_ready.sem, ms_ready.ready(MS[c]))
                op(rstd[:, first:], rstd[:, first:], ACT.Sqrt).then_inc(root_ready.sem, 1)

            act.wait_ge(x_loaded, 16)
            norm(0, META)
            high_parts(0, META, mod[:, 0:KT])
            act.wait_ge(rel_stored, 16)
            def v_out(p):
                act.wait_ge(tile_done.sem, tile_done.ready(S_V + 2 * p + 1))
                op(v[:, :, 2 * P * p:2 * P * (p + 1)],
                   bank(2 * (p % 2), 1024).rearrange("p (a b) -> p a b", b=2 * P), ACT.Copy)\
                    .then_inc(dense_act.sem, 1)

            n = 0
            for i in range(1, TT):
                for h in range(NH):
                    act.wait_ge(idx_done.sem, idx_done.ready(n))
                    act.wait_ge(relu_used.sem, relu_used.free(n, 2))
                    op(relu[n % 2][:, 0:P * (i + 1)], bank(4 + n % 2, P * (i + 1)), ACT.Relu)\
                        .then_inc(relu_done.sem, 1)
                    n += 1
                v_out(i - 1)
            v_out(TT - 1)

            units = [(e, i) for e in range(2) for i in range(TT)]
            U = len(units)

            def gate(q, j):
                act.wait_ge(tile_done.sem, tile_done.ready(S_GATE + q * 4 + j))
                hold()
                op(gates[:, q * 4 + j, :], bank(j % 2), ACT.Copy).then_inc(dense_act.sem, 1)

            def softmax_pair(base, lg, width, copy, between=None):
                for u in range(U + 1):
                    if u < U:
                        w = width(units[u][1])
                        act.wait_ge(s_taken.sem, s_taken.ready(base + u))
                        op(lg[u % 2][:, 0:w], lg[u % 2][:, 0:w], ACT.Exp, bias=col[:, 2 + u % 2:3 + u % 2],
                           accum_out=col[:, 4 + u % 2:5 + u % 2]).then_inc(exp_done.sem, 1)
                    if between and u % 2 == 1:
                        between(u // 2)
                    if u >= 1:
                        act.wait_ge(t_done.sem, t_done.ready(base + u - 1))
                        act.wait_ge(pv_done.sem, pv_done.free(base + u - 1, 2))
                        copy(u - 1, units[u - 1][1])

            def copy_a(u, i):
                op(probT[u % 2][:, 0:i + 1, :], bank(4 + u % 2, P * (i + 1)).rearrange("p (a b) -> p a b", b=P),
                   ACT.Copy).then_inc(t_taken.sem, 1)

            with act.Fori(0, HP) as q:
                softmax_pair(q * U, logit, lambda i: P * (i + 1), copy_a, lambda j: gate(q, j))
            with steps.loop(HP, 16) as q:
                for e in range(2):
                    act.wait_ge(yb_done.sem, yb_done.free(q * 2 + e, 2))
                    item = (q * 2 + e) * TT
                    act.wait_ge(z_done.sem, z_done.ready(item + TT - 1))
                    for i in reversed(range(TT)):
                        steps(op(az[e][i], zs_all[i], ACT.Abs))
                    steps.wait()
                    for i in reversed(range(TT)):
                        steps(op(az[e][i], az[e][i], ACT.Exp, scale=-1.0))
                    steps.wait()
                    for i in reversed(range(TT)):
                        op(az[e][i], az[e][i], ACT.Ln, bias=1.0).then_inc(soft_done.sem, 1)
                    for n, i in enumerate(reversed(range(TT))):
                        act.wait_ge(u_done.sem, u_done.ready(item + n))
                        op(az[e][i], us_all[n][:, 0:T - i * P], ACT.Exp).then_inc(a_done.sem, 1)
            for m in (0, 8, 4, 12):
                op(gates[:, m:m + 4, :], gates[:, m:m + 4, :], ACT.Sigmoid).then_inc(gates_done.sem, 1)
            act.wait_ge(x_ready.sem, x_ready.ready(0))
            norm(1, META)
            high_parts(1, META, mod[:, 24:32])
            def best_weights(n):
                act.wait_ge(best_done.sem, best_done.ready(n))
                op(best[:], best[:], ACT.Exp, bias=col[:, 8:9], accum_out=col[:, 9:10])\
                    .then_inc(best_exp.sem, 1)

            def query(n, j):
                act.wait_ge(tile_done.sem, tile_done.ready(S_WQ + n + j))
                act.wait_ge(key_done.sem, key_done.free(n + j, 2))
                op(qh[j % 2][:], bank(j % 2), ACT.Copy).then_inc(dense_act.sem, 1)

            def key_scores(n, j):
                act.wait_ge(key_done.sem, key_done.ready(n + j))
                hold()
                scores = sc[:, :, j, :] if isinstance(n, int) else sc[:, :, bass.ds(n + j, 1), :]
                src = bank(2 + j % 2).rearrange("p (a b) -> p a b", b=P)
                op(scores, src if isinstance(n, int) else src.unsqueeze(2), ACT.Copy).then_inc(key_taken.sem, 1)

            def token_rows(n):
                act.wait_ge(htok_done.sem, htok_done.ready(n))
                op(h_tok[:, n, :], psum[:, (4 + 2 * (n % 2)) * 512:(6 + 2 * (n % 2)) * 512], ACT.Copy)\
                    .then_inc(htok_taken.sem, 1)

            query(0, 0)
            query(0, 1)
            key_scores(0, 0)
            with act.Fori(0, PH - 1) as h:
                query(h * 2, 2)
                key_scores(h * 2, 1)
                best_weights(h)
                query(h * 2, 3)
                key_scores(h * 2, 2)
            key_scores(0, 2 * PH - 1)
            token_rows(0)
            best_weights(PH - 1)
            for n in range(1, TT):
                token_rows(n)

            def diagonals(n, g):
                s = g % GS
                act.wait_ge(coef_done.sem, coef_done.ready(n + g))
                for c in range(G):
                    ins = op(diag[:, s, c * P:(c + 1) * P], ident[:], ACT.Copy, scale=coef[:, s, c:c + 1])
                    if c == G - 1:
                        steps.wait()
                        ins.then_inc(diag_done.sem, 1)
                    else:
                        steps(ins)

            def gelus(n, best_n=None):
                for g in range(GROUPS):
                    act.wait_ge(pre_done.sem, pre_done.ready(n + g))
                    op(pre[:, g % GS, :], pre[:, g % GS, :], ACT.Gelu).then_inc(gelu_done.sem, 1)
                    diagonals(n, g)
                    if g == BEST_AFTER and best_n is not None:
                        best_weights(best_n)

            def sum_out(j):
                act.wait_ge(rows_used.sem, rows_used.ready(j * (PH * GROUPS) + (PH * GROUPS - 1)))
                act.wait_ge(f_done.sem, f_done.free(j, 1))
                op(acc[:], psum[:, 2 * 512:4 * 512], ACT.Copy).then_inc(acc_done.sem, 1)

            with steps.loop(TT - 1, PH * GROUPS * (G - 1)) as j:
                with steps.loop(PH, GROUPS * (G - 1)) as h:
                    n = j * (PH * GROUPS) + h * GROUPS
                    gelus(n, j * PH + h + PH)
                sum_out(j)
            with steps.loop(PH, GROUPS * (G - 1)) as h:
                gelus(h * GROUPS + (TT - 1) * PH * GROUPS)
            sum_out(TT - 1)
            act.wait_ge(x_ready.sem, x_ready.ready(1))
            norm(2, META)
            act.wait_ge(x_ready.sem, x_ready.ready(2))
            act.wait_ge(meta_loaded, 16)
            norm(3, 0)
            high_parts(2, 0)
            with act.Fori(0, 2) as q:
                for j in range(4):
                    act.wait_ge(dense_dve.sem, dense_dve.ready(q * 4 + (V_IN2 + j)))
                    act.wait_ge(sq_used.sem, sq_used.free(q * 4 + (4 * KT + j), 2))
                    hold()
                    op(sq[:, j % 2, :], big[:, q * 4 + j, :], ACT.Square).then_inc(sq_ready.sem, 1)
                    act.wait_ge(ms_ready.sem, ms_ready.ready(q * 4 + (4 + j)))
                    hold()
                    op(rstd[:], rstd[:], ACT.Sqrt).then_inc(root_ready.sem, 1)
            act.wait_ge(fg_done.sem, fg_done.ready(0))
            steps(op(lf2[0:NH, :], lf2[0:NH, :], ACT.Exp, scale=-1.0))
            steps.wait()
            op(lf2[0:NH, :], lf2[0:NH, :], ACT.Ln, bias=1.0).then_inc(fg_exp.sem, 1)
            for h in range(NH):
                act.wait_ge(cumr_done.sem, cumr_done.ready(h))
                op(cum_row[:, h, :], seam(4 + 2 * (h % 2)), ACT.Copy, scale=-1.0).then_inc(cumr_taken.sem, 1)

            def copy_2(u, i):
                steps(op(probT2[u % 2][:, TT, :], bank(0, P), ACT.Copy))
                steps(op(probT2[u % 2][:, 0:i + 1, :],
                         bank(6 + u % 2, P * (i + 1)).rearrange("p (a b) -> p a b", b=P), ACT.Copy))
                steps.wait()
                act.sem_inc(t_taken.sem, 1)

            with steps.loop(HP, 2 * U) as q:
                softmax_pair(HP * U + q * U, logit2, lambda i: META + P * (i + 1), copy_2)
            act.wait_ge(x_ready.sem, x_ready.ready(3))
            norm(4, META)
            high_parts(3, META)
            with act.Fori(0, FF // 2) as q:
                for j in range(2):
                    act.wait_ge(tile_done.sem, tile_done.ready(S_UP + q * 4 + 2 * j))
                    act.wait_ge(dense_dve.sem, dense_dve.free(V_UP + q * 2 + j, 2))
                    op(silu[j][:], bank(2 * j), ACT.Silu).then_inc(up_silu.sem, 1)

        @block.gpsimd
        def _(pool):
            start(pool, "pool")
            steps = Steps(pool, own["pool"])
            select = nc.gpsimd.affine_select

            for a, value in ((ident, 0.0), (ones, 1.0), (neg_ones, -1.0), (neg_tri, -1.0),
                             (half_ones, 0.0), (causal, 0.0), (strict, 0.0)):
                steps(nc.gpsimd.memset(a[:], value))
            steps(nc.gpsimd.iota(iota16[:], pattern=[[1, PK]], base=0, channel_multiplier=0,
                                 allow_small_or_imprecise_dtypes=True))
            steps.wait()
            steps(select(out=ident[:], in_=ident[:], compare_op=ALU.not_equal, fill=1.0, base=0,
                         pattern=[[-1, P]], channel_multiplier=1))
            steps(select(out=neg_tri[:], in_=neg_tri[:], compare_op=ALU.is_ge, fill=0.0, base=0,
                         pattern=[[-1, P]], channel_multiplier=1))
            steps(select(out=causal[:], in_=causal[:], compare_op=ALU.is_ge, fill=GATED, base=0,
                         pattern=[[-1, P]], channel_multiplier=1))
            steps(select(out=strict[:], in_=strict[:], compare_op=ALU.is_gt, fill=GATED, base=0,
                         pattern=[[1, P]], channel_multiplier=-1))
            steps.wait()
            steps(nc.gpsimd.tensor_tensor(ident_r[:], ident[:], ones[:], ALU.mult))
            for e in range(2):
                steps.wait()
                steps(nc.gpsimd.memset(half_ones[64 * e:64 * e + 64, 64 * e:64 * e + 64], 1.0))
            steps.wait()
            pool.sem_inc(consts_done, 1)

            def split_tile(n, q=0, per=0, high=None, depth=HIGHS):
                pool.wait_ge(ring_ready[n % SLOTS], 16 * (n // SLOTS + 1) + q * (16 * per // SLOTS))
                pool.wait_ge(tile_done.sem, tile_done.free(n + q * per, depth))
                pool.sem_inc(held["pool"], 1)
                if high is None:
                    high = w_high[:, n % HIGHS, :]
                raw, low = ring[:, n % SLOTS, :], ring_low[:, n % SLOTS, :]
                steps(nc.gpsimd.tensor_tensor(high.rearrange("p (a b) -> p a b", b=P),
                                              raw.rearrange("p (a b) -> p a b", b=P),
                                              ones[:].unsqueeze(1).to_broadcast([P, KT, P]), ALU.mult))
                steps.wait()
                steps(nc.gpsimd.tensor_tensor(low, raw, high.bitcast(f32), ALU.subtract))
                tell(pool, steps, w_split)

            def split(first, last):
                with steps.loop((last - first) // SLOTS, 2 * SLOTS) as q:
                    for j in range(SLOTS):
                        split_tile(first + j, q, SLOTS)

            def split_pairs(first, rounds, second_high):
                pool.wait_ge(tile_done.sem, tile_done.ready(first - 1))
                with steps.loop(rounds, 2 * SLOTS) as q:
                    for j in range(SLOTS):
                        split_tile(first + j, q, SLOTS, second_high[:, j - 2, :] if j >= 2 else None, SLOTS)
                for n in range(first + rounds * SLOTS, first + rounds * SLOTS + 2):
                    split_tile(n, depth=SLOTS)

            pool.wait_ge(rel_copied.sem, rel_copied.ready(0))
            nc.gpsimd.dma_start(rel_dram[:, 0:REL], rel_row).then_inc(rel_stored, 16)
            pool.wait_ge(rel_stored, 16)
            split(S_QK, S_KI)
            pool.wait_ge(ada_used.sem, ada_used.ready(ADA - 1))
            nc.gpsimd.dma_start(bias_rows, bass.AP(tensor=rel_dram.tensor, offset=rel_dram.offset,
                                                 ap=[[1, P], [REL + 1, NH], [1, T]])).then_inc(bias_loaded, 16)
            for n in range(S_KI, S_V):
                split_tile(n)
            split_pairs(S_V, 2, v_high)
            split(S_GATE + 2, 48)
            pool.wait_ge(y_taken.sem, y_taken.ready(HP - 1))
            for e in range(2):
                steps.wait()
                steps(nc.gpsimd.memset(stage_h[e][64 * (1 - e):64 * (1 - e) + 64, :], 0.0))
            tell(pool, steps, half_zeroed)
            with pool.Fori(0, HP) as q:
                for e in range(2):
                    for n, i in enumerate(reversed(range(TT))):
                        pool.wait_ge(sp_done.sem, sp_done.ready((q * 2 + e) * TT + n))
                        pool.sem_inc(held["pool"], 1)
                        d = sp[i][:, 0:P]
                        select(out=d, in_=d, compare_op=ALU.is_gt, fill=0.0, base=0, pattern=[[1, P]],
                               channel_multiplier=-1).then_inc(sp_gated.sem, 1)
            pool.wait_ge(yb_taken.sem, yb_taken.ready(HP - 1))
            nc.gpsimd.dma_start(keys[:], sub_keys).then_inc(keys_loaded, 16)
            split(48, 80)
            def gathers(n, h):
                for g in range(GROUPS):
                    s = g % GS
                    pool.wait_ge(rows_used.sem, rows_used.free(n + g, GS))
                    pool.sem_inc(held["pool"], 1)
                    steps(nc.gpsimd.tensor_copy(eslot[:, s, :], eidx[:, 0, bass.ds(h * PK + g * G, G)]))
                    steps.wait()
                    pool.sem_inc(held["pool"], 1)
                    for c in range(G):
                        nc.gpsimd.indirect_dma_start(
                            rows[:, s, c, :], None, experts,
                            bass.IndirectOffsetOnAxis(ap=eslot[:, s, c:c + 1], axis=0)).then_inc(rows_ready[s], 16)

            with steps.loop(TT, PH * GROUPS + 1) as j:
                pool.wait_ge(chosen.sem, chosen.ready(j * PH + (PH - 1)))
                pool.sem_inc(held["pool"], 1)
                steps(nc.gpsimd.tensor_copy(eidx[:, 0, :], eidx[:, 1, :]))
                tell(pool, steps, eidx_taken)
                with steps.loop(PH, GROUPS) as h:
                    gathers(j * PH * GROUPS + h * GROUPS, h)
            split(80, S_V2 - 2)
            for n in range(S_V2 - 2, S_V2):
                split_tile(n)
            split_pairs(S_V2, 1, v2_high)
            split(S_OUT2, TILES)

        @block.vector
        def _(dve):
            V = nc.vector
            start(dve, "dve")
            steps = Steps(dve, own["dve"])

            def hold():
                dve.sem_inc(held["dve"], 1)

            def sync():
                steps.wait()
                hold()

            def stt(out, a, s, b, op0, op1):
                return V.scalar_tensor_tensor(out=out, in0=a, scalar=s, in1=b, op0=op0, op1=op1)

            def ttr(out, a, b, op0, op1, accum):
                return V.tensor_tensor_reduce(out=out, in0=a, in1=b, scale=1.0,
                                              scalar=0.0 if op1 == ALU.add else TAKEN,
                                              op0=op0, op1=op1, accum_out=accum)

            def ada_tiles(q, js, n0, per=SLOTS):
                for j in js:
                    dve.wait_ge(ada_ready[j], 16 * (n0 // SLOTS + 1) + q * (16 * per // SLOTS))
                    sync()
                    steps(ttr(junk_ada, ada[:, j, :],
                              cvec[:], ALU.mult, ALU.add, col[:, j:j + 1]))
                    steps.wait()
                    dve.sem_inc(ada_used.sem, 1)

            def ada_store(q, n0, per=SLOTS):
                sync()
                steps(V.tensor_tensor(mod[:, bass.ds(q * per + n0, SLOTS)], col[:, 0:SLOTS],
                                      vec[:, bass.ds(q * per + (B_ADA + n0), SLOTS)], ALU.add))

            dve.wait_ge(rel_done.sem, rel_done.ready(0))
            steps(V.tensor_copy(rel_row, bank(4, REL)[0:NH, :]))
            tell(dve, steps, rel_copied)

            def root(c, first):
                dve.wait_ge(sq_used.sem, sq_used.ready(SQ0[c] + KT - 1))
                sums = seam(2) if first == 0 else bank(3)
                steps(V.tensor_scalar(rstd[:, first:], sums, 1.0 / D, EPS, ALU.mult, ALU.add))
                tell(dve, steps, ms_ready)
                dve.wait_ge(root_ready.sem, root_ready.ready(MS[c]))
                steps(V.reciprocal(rstd[:, first:], rstd[:, first:]))
                steps.wait()

            dve.wait_ge(cond_done.sem, cond_done.ready(0))
            dve.wait_ge(vec_loaded, 16)
            with steps.loop(2, SLOTS + 1) as q:
                ada_tiles(q, range(SLOTS), 0)
                ada_store(q, 0)
            root(0, META)
            with steps.loop(2, SLOTS + 1) as q:
                ada_tiles(q, range(SLOTS), 2 * SLOTS)
                ada_store(q, 2 * SLOTS)
            steps.wait()
            steps(stt(gain1[:], mod[:, 8:16], 1.0, vec[:, G1:G1 + KT], ALU.add, ALU.mult))
            steps.wait()

            def norm(c, first, gain, parts, shift=None, dst=hn):
                if c:
                    root(c, first)
                for k in range(KT):
                    steps(stt(dst[:, k, first:], x[:, k, first:], gain[:, k:k + 1], rstd[:, first:],
                              ALU.mult, ALU.mult))
                    if parts is not None:
                        tell(dve, steps, normed)
                if parts is None:
                    return
                for k in range(KT):
                    dve.wait_ge(high_ready.sem, high_ready.ready(parts * KT + k))
                    high = hn_high[:, k, first:].bitcast(f32)
                    if shift is None:
                        ins = V.tensor_tensor(hn_low[:, k, first:], hn[:, k, first:], high, ALU.subtract)
                    else:
                        ins = stt(hn_low[:, k, first:], hn[:, k, first:], shift[:, k:k + 1], high,
                                  ALU.add, ALU.subtract)
                    ins.then_inc(hn_ready.sem, 1)

            def low_part(low, raw, high):
                steps(V.tensor_copy(high, raw))
                steps.wait()
                steps(V.tensor_tensor(low, raw, high.bitcast(f32), ALU.subtract))

            norm(0, META, gain1, 0, mod[:, 0:KT])
            def qk_out(q, j):
                dve.wait_ge(tile_done.sem, tile_done.ready(S_QK + q * 4 + j))
                steps(V.tensor_scalar(qk[:, q * 4 + j, :], bank(j % 2), 1.0, None, ALU.mult))
                tell(dve, steps, dense_dve)

            with steps.loop(4, 4 + 2 * (SLOTS + 1)) as q:
                for half_q in range(2):
                    for j in range(2):
                        qk_out(q, 2 * half_q + j)
                        ada_tiles(q, [2 * j, 2 * j + 1], 16 + 4 * half_q, 8)
                    ada_store(q, 16 + 4 * half_q, 8)
            for j in range(4):
                qk_out(4, j)
            dve.wait_ge(tile_done.sem, tile_done.ready(S_KI))
            steps(V.tensor_copy(ki[:], bank(0)))
            tell(dve, steps, dense_dve)
            dve.wait_ge(tile_done.sem, tile_done.ready(S_WI))
            steps(V.tensor_copy(wi[:], bank(1, TT * NH).rearrange("p (a b) -> p a b", b=NH)))
            tell(dve, steps, dense_dve)
            steps(V.tensor_scalar(qk[:, QB:QB + 4, :], qk[:, QB:QB + 4, :], 0.125, None, ALU.mult))
            steps.wait()
            steps(stt(gain2[:], mod[:, 32:40], 1.0, vec[:, G2:G2 + KT], ALU.add, ALU.mult))

            steps(V.tensor_copy(mask[0], causal[:]))
            n = 0
            for i in range(1, TT):
                w = P * (i + 1)
                for h in range(NH):
                    dve.wait_ge(relu_done.sem, relu_done.ready(n))
                    if h == 0:
                        steps(V.tensor_scalar(score[:, 0:w], relu[n % 2][:, 0:w], wi[:, i, h:h + 1], None, ALU.mult))
                    else:
                        steps(stt(score[:, 0:w], relu[n % 2][:, 0:w], wi[:, i, h:h + 1], score[:, 0:w],
                                  ALU.mult, ALU.add))
                    tell(dve, steps, relu_used)
                    n += 1
                steps(V.tensor_scalar(score[:, 0:w], score[:, 0:w], IDX_SCALE, None, ALU.mult))
                steps.wait()
                steps(V.tensor_tensor(score[:, w - P:w], score[:, w - P:w], causal[:], ALU.add))
                steps.wait()
                for r in range(TOPK // 8):
                    steps(V.max(col[:, 0:8], score[:, 0:w]))
                    steps.wait()
                    steps(V.match_replace(score[:, 0:w], col[:, 0:8], score[:, 0:w], TAKEN))
                    steps.wait()
                steps(V.tensor_scalar(mask[i], score[:, 0:w], 0.5 * TAKEN, GATED, ALU.is_gt, ALU.mult))
                steps.wait()

            units = [(e, i) for e in range(2) for i in range(TT)]
            U = len(units)

            def finish_unit(base, u, lg, w):
                dve.wait_ge(exp_done.sem, exp_done.ready(base + u))
                steps(V.reciprocal(col[:, 6 + u % 2:7 + u % 2], col[:, 4 + u % 2:5 + u % 2]))
                steps.wait()
                steps(V.tensor_scalar(lg[u % 2][:, 0:w], lg[u % 2][:, 0:w], col[:, 6 + u % 2:7 + u % 2],
                                      None, ALU.mult))
                tell(dve, steps, p_done)

            dve.wait_ge(dense_act.sem, dense_act.ready(A_GATE - 1))
            dve.wait_ge(bias_loaded, 16)
            steps(V.tensor_copy(bias[:], bias_rows[:, :, ::-1]))
            with steps.loop(HP, 3 + 5 * U + 2) as q:
                dve.wait_ge(s_done.sem, s_done.free(q * U, 1))
                dve.wait_ge(pv_done.sem, pv_done.free(q * U, 1))
                hold()
                steps(V.tensor_copy(stage[0], qk[:, q + QA, :]))
                steps(V.tensor_copy(stage[1], qk[:, q + KA, :]))
                steps(V.tensor_copy(stage_v[:], v[:, :, bass.ds(q * P, P)]))
                tell(dve, steps, staged)
                for u in range(U + 1):
                    if u < U:
                        e, i = units[u]
                        w = P * (i + 1)
                        lg = logit[u % 2][:, 0:w]
                        dve.wait_ge(s_done.sem, s_done.ready(q * U + u))
                        dve.wait_ge(t_done.sem, t_done.free(q * U + u, 2))
                        hold()
                        steps(stt(lg, bank(2 + u % 2, w), 0.125, bias[:, q * 2 + e, T - w:T], ALU.mult, ALU.add))
                        sync()
                        steps(ttr(lg, lg, mask[i], ALU.add, ALU.max, col[:, u % 2:u % 2 + 1]))
                        steps.wait()
                        steps(V.tensor_scalar(col[:, 2 + u % 2:3 + u % 2], col[:, u % 2:u % 2 + 1], -1.0, None, ALU.mult))
                        tell(dve, steps, s_taken)
                    if u >= 1:
                        finish_unit(q * U, u - 1, logit, P * (units[u - 1][1] + 1))
                dve.wait_ge(pv_done.sem, pv_done.ready(q * U + U - 1))
                hold()
                low_part(y_low[:, q, :], bank(6), y_high[0][:, q, :])
                tell(dve, steps, y_taken)

            dve.wait_ge(half_zeroed.sem, half_zeroed.ready(0))

            def stage_pair(q):
                steps(V.tensor_copy(stage[0], qk[:, q + KB, :]))
                for e in range(2):
                    steps(V.tensor_copy(stage_h[e][64 * e:64 * e + 64, :], qk[64 * e:64 * e + 64, q + QB, :]))
                tell(dve, steps, staged)

            def stage_values(q):
                steps(V.tensor_copy(stage_v[:], v[:, :, bass.ds(q * P + NH * DH, P)]))
                tell(dve, steps, values_staged)

            def softplus(q):
                for e in range(2):
                    item = (q * 2 + e) * TT
                    dve.wait_ge(u_done.sem, u_done.free(item, 1))
                    for n, i in enumerate(reversed(range(TT))):
                        dve.wait_ge(soft_done.sem, soft_done.ready(item + n))
                        steps(stt(sp[i], zs_all[i], 0.0, az[e][i], ALU.max, ALU.add))
                        tell(dve, steps, sp_done)

            def take_pair(q):
                dve.wait_ge(yb_done.sem, yb_done.ready(q * 2 + 1))
                hold()
                low_part(y_low[:, q + HP, :], bank(6), y_high[1][:, q, :])
                tell(dve, steps, yb_taken)

            stage_pair(0)
            stage_values(0)
            with steps.loop(HP - 1, 2 * TT + 3 + 2 + 1) as q:
                softplus(q)
                dve.wait_ge(u_done.sem, u_done.ready((q * 2 + 1) * TT + (TT - 1)))
                hold()
                stage_pair(q + 1)
                take_pair(q)
                stage_values(q + 1)
            softplus(HP - 1)
            take_pair(HP - 1)

            with steps.loop(2, 4 * 5) as q:
                for j in range(4):
                    m = q * 4 + j
                    b = 2 * (j % 2)
                    dve.wait_ge(gates_done.sem, gates_done.ready(q * 2 + 1))
                    dve.wait_ge(tile_done.sem, tile_done.ready(S_PROJ + m))
                    steps(V.tensor_tensor(gates[:, m, :], gates[:, m, :], bank(b), ALU.mult))
                    steps(V.tensor_tensor(gates[:, m + 8, :], gates[:, m + 8, :], bank(b + 1), ALU.mult))
                    steps.wait()
                    steps(V.tensor_tensor(gates[:, m, :], gates[:, m, :], gates[:, m + 8, :], ALU.add))
                    steps.wait()
                    low_part(merged_low[:, m, :], gates[:, m, :], merged_high[:, m, :])
                    tell(dve, steps, dense_dve)
            with steps.loop(2, 4) as q:
                for j in range(4):
                    m = q * 4 + j
                    dve.wait_ge(tile_done.sem, tile_done.ready(S_OUT + m))
                    steps(stt(x[:, m, META:], bank(j % 2), mod[:, bass.ds(q * 4 + (16 + j), 1)], x[:, m, META:],
                              ALU.mult, ALU.add))
                    tell(dve, steps, dense_dve)
            tell(dve, steps, x_ready)
            norm(1, META, gain2, 1, mod[:, 24:32])

            def bc(a, dims, axis):
                return a.unsqueeze(axis).to_broadcast(dims)

            def choose(j, h, n):
                steps(V.tensor_copy(half[:], sc[:, j, bass.ds(h * 2, 2), :]))
                sync()
                for c in range(2):
                    steps(V.max(top[:, c, 0:8], half[:, c, :]))
                sync()
                for c in range(2):
                    steps(V.max_index(topi[:, c, 0:8], top[:, c, 0:8], half[:, c, :]))
                sync()
                for c in range(2):
                    steps(V.match_replace(half[:, c, :], top[:, c, 0:8], half[:, c, :], TAKEN))
                sync()
                for c in range(2):
                    steps(V.max(top[:, c, 8:16], half[:, c, :]))
                sync()
                for c in range(2):
                    steps(V.max_index(topi[:, c, 8:16], top[:, c, 8:16], half[:, c, :]))
                yield
                steps(V.tensor_tensor(cand[:], bc(top[:, 0, :], [P, PK, PK], 2), bc(top[:, 1, :], [P, PK, PK], 1), ALU.add))
                sync()
                steps(V.tensor_copy(topf[:], topi[:]))
                flat = cand[:].rearrange("p a b -> p (a b)")
                steps(V.max(best[:, 0:8], flat))
                sync()
                steps(V.max_index(pos[:, 0:8], best[:, 0:8], flat))
                steps(V.tensor_scalar(col[:, 8:9], best[:, 0:1], -1.0, None, ALU.mult))
                sync()
                yield
                steps(V.match_replace(flat, best[:, 0:8], flat, TAKEN))
                sync()
                steps(V.max(best[:, 8:16], flat))
                sync()
                steps(V.max_index(pos[:, 8:16], best[:, 8:16], flat))
                tell(dve, steps, best_done)
                yield
                steps(V.tensor_single_scalar(pos2[:, 0, :], pos[:], 4, ALU.logical_shift_right))
                steps(V.tensor_single_scalar(pos2[:, 1, :], pos[:], 15, ALU.bitwise_and))
                sync()
                steps(V.tensor_copy(posf[:], pos2[:]))
                sync()
                for c in range(2):
                    hc = hot[:, c, :].rearrange("p (a b) -> p a b", b=PK)
                    steps(V.tensor_tensor(hc, bc(posf[:, c, :], [P, PK, PK], 2), bc(iota16[:], [P, PK, PK], 1), ALU.is_equal))
                sync()
                yield
                for c in range(2):
                    hc = hot[:, c, :].rearrange("p (a b) -> p a b", b=PK)
                    steps(V.tensor_tensor(hc, hc, bc(topf[:, c, :], [P, PK, PK], 1), ALU.mult))
                sync()
                for c in range(2):
                    hc = hot[:, c, :].rearrange("p (a b) -> p a b", b=PK)
                    steps(V.tensor_reduce(epart[:, c, :], hc, AX, ALU.add))
                sync()
                steps(stt(eidx[:, 1, bass.ds(h * PK, PK)], epart[:, 0, :], float(NK), epart[:, 1, :], ALU.mult, ALU.add))
                dve.wait_ge(best_exp.sem, best_exp.ready(n))
                hold()
                steps(V.reciprocal(col[:, 10:11], col[:, 9:10]))
                sync()
                steps(V.tensor_scalar(wgt[:, 1, bass.ds(h * PK, PK)], best[:], col[:, 10:11], None, ALU.mult))
                tell(dve, steps, chosen)
            CHOOSE = 1 + 2 + 4 + 2 + 3 + 2 + 3 + 1 + 1 + 2 + 1 + 6 + 1 + 1 + 1

            junks = [hn[:].rearrange("p a b -> p (a b)")[:, c * D:(c + 1) * D] for c in range(G)]

            def dots(n, slot_count, g):
                s = g % GS
                dve.wait_ge(rows_ready[s], slot_count)
                sync()
                for c in range(G):
                    steps(ttr(junks[c], rows[:, s, c, 0:D], h_cur[:], ALU.mult, ALU.add, pre[:, s, c:c + 1]))
                tell(dve, steps, pre_done)

            def weights(n, h, g):
                s = g % GS
                dve.wait_ge(gelu_done.sem, gelu_done.ready(n))
                hold()
                steps(V.tensor_tensor(coef[:, s, :], pre[:, s, :], wgt[:, 0, bass.ds(h * PK + g * G, G)], ALU.mult))
                tell(dve, steps, coef_done)
            GROUP = G + 1

            def experts_of_head(j, h, also_next):
                base = j * (PH * GROUPS) + h * GROUPS
                parts = choose(j + 1, h, j * PH + h + PH) if also_next else iter(())
                for g in range(GROUPS):
                    dots(base + g, j * (PH * GROUPS // GS * 16 * G) + h * (GROUPS // GS * 16 * G)
                         + (g // GS + 1) * 16 * G, g)
                    weights(base + g, h, g)
                    next(parts, None)

            def begin_tile(j):
                sync()
                dve.wait_ge(eidx_taken.sem, eidx_taken.ready(j))
                hold()
                steps(V.tensor_copy(wgt[:, 0, :], wgt[:, 1, :]))
                steps(V.tensor_copy(h_cur[:], h_tok[:, j, :]))
                steps.wait()

            def tile_of_tokens(j, also_next):
                with steps.loop(PH, GROUPS * GROUP + (CHOOSE if also_next else 0)) as h:
                    experts_of_head(j, h, also_next)
                if also_next:
                    begin_tile(j + 1)
                dve.wait_ge(f_done.sem, f_done.ready(j))
                hold()
                for k in range(KT):
                    xs = x[:, k, bass.ds(j * P + META, P)]
                    steps(stt(xs, bank(4, P, k * P), mod[:, 40 + k:41 + k], xs, ALU.mult, ALU.add))

            with steps.loop(PH, CHOOSE) as h:
                dve.wait_ge(key_taken.sem, key_taken.ready(h * 2 + 1))
                hold()
                for _ in choose(0, h, h):
                    pass
            dve.wait_ge(htok_taken.sem, htok_taken.ready(TT - 1))
            begin_tile(0)
            with steps.loop(TT - 1, 2 + PH * (GROUPS * GROUP + CHOOSE) + KT) as j:
                tile_of_tokens(j, True)
            tile_of_tokens(TT - 1, False)
            tell(dve, steps, x_ready)
            norm(2, META, vec[:, GF:GF + KT], None, dst=x)
            tell(dve, steps, x_ready)
            norm(3, 0, vec[:, N1:N1 + KT], 2)

            dve.wait_ge(hn_ready.sem, hn_ready.ready(3 * KT - 1))
            for c, a in enumerate((hn_low, hn_high)):
                steps(V.tensor_copy(meta_parts[:, :, c * META:(c + 1) * META], a[:, :, 0:META].bitcast(f32)))
            tell(dve, steps, meta_ready)

            def in2_out(j, q=0, per=0):
                dve.wait_ge(tile_done.sem, tile_done.ready(S_IN2 + q * per + j))
                steps(V.tensor_scalar(big[:, q * per + j, :], seam(4 + 2 * (j % 2)), 1.0, None, ALU.mult))
                sync()
                of_low = bank(4 + 2 * (j % 2), META, 512 - 2 * META)
                steps(V.tensor_tensor(big[:, q * per + j, 0:META], big[:, q * per + j, 0:META], of_low, ALU.add))
                tell(dve, steps, dense_dve)

            for j in range(4):
                in2_out(j)
            with steps.loop(2, 4 * 5) as q:
                for j in range(4):
                    in2_out(4 + j, q, 4)
                    dve.wait_ge(sq_used.sem, sq_used.ready(q * 4 + (4 * KT + j)))
                    sync()
                    steps(V.tensor_scalar(rstd[:], seam(2), 1.0 / DH, EPS, ALU.mult, ALU.add))
                    tell(dve, steps, ms_ready)
                    dve.wait_ge(root_ready.sem, root_ready.ready(q * 4 + (4 + j)))
                    hold()
                    steps(V.reciprocal(rstd[:], rstd[:]))
                    sync()
                    steps(stt(big[:, q * 4 + j, :], big[:, q * 4 + j, :], vec[:, bass.ds(q + QN, 1)], rstd[:],
                              ALU.mult, ALU.mult))
            steps(V.memset(v2[:, TT, :], 0.0))
            steps.wait()
            for c in range(2):
                columns = slice(2 * c * P, 2 * (c + 1) * P)
                dve.wait_ge(tile_done.sem, tile_done.ready(S_V2 + 2 * c + 1))
                steps(V.tensor_copy(v2[:, 0:TT, columns], bank(2 * c, 1024).rearrange("p (a b) -> p a b", b=2 * P)))
                steps(V.tensor_copy(v2[0:META, TT, columns], bank(4 + c, 2 * P)[0:META, :]))
                tell(dve, steps, dense_dve)
            dve.wait_ge(tile_done.sem, tile_done.ready(S_FG))
            steps(V.tensor_scalar(lf[0:NH, :], seam(6)[0:NH, :], vec[0:NH, BF:BF + 1], None, ALU.add))
            steps.wait()
            steps(stt(lf2[0:NH, :], lf[0:NH, :], -1.0, lf[0:NH, :], ALU.mult, ALU.max))
            tell(dve, steps, fg_done)
            steps(V.tensor_scalar(big[:, 0:4, :], big[:, 0:4, :], 0.125, None, ALU.mult))
            dve.wait_ge(fg_exp.sem, fg_exp.ready(0))
            steps(stt(lf[0:NH, :], lf[0:NH, :], 0.0, lf2[0:NH, :], ALU.min, ALU.subtract))
            steps.wait()
            steps(V.tensor_tensor_scan(cum[0:NH, :], ones[0:NH, 0:1].to_broadcast([NH, L2]), lf[0:NH, :], 0.0,
                                       ALU.mult, ALU.add))
            tell(dve, steps, cum_done)
            dve.wait_ge(cumt_done.sem, cumt_done.ready(0))
            steps(V.tensor_copy(cum_tok[:], bank(0, TT * NH).rearrange("p (a b) -> p a b", b=NH)))
            for g in range(4):
                u = big[:, 8 + g, :]
                src, lo = u, 0
                for a in range(g + 1):
                    dst = (pool_a, pool_b)[a % 2]
                    lo += 1 << a
                    steps.wait()
                    steps(V.tensor_tensor(dst[:, lo:], src[:, lo:], src[:, lo - (1 << a):L2 - (1 << a)], ALU.add))
                    src = dst
                steps.wait()
                steps(stt(pooled[:, g, :], src[:, META:], 1.0 / (2 << g), u[:, META:], ALU.mult, ALU.subtract))
                steps.wait()
                low_part(pooled_low[:, g, :], pooled[:, g, :], pooled_high[:, g, :])
            tell(dve, steps, pooled_done)
            dve.wait_ge(cumr_taken.sem, cumr_taken.ready(NH - 1))
            with steps.loop(HP, 3 + 5 * U + 2) as q:
                base = q * U + HP * U
                dve.wait_ge(s_done.sem, s_done.free(base, 1))
                dve.wait_ge(pv_done.sem, pv_done.free(base, 1))
                hold()
                steps(V.tensor_copy(stage2[0], big[:, q, :]))
                steps(V.tensor_copy(stage2[1], big[:, q + 4, :]))
                steps(V.tensor_copy(stage2_v[:], v2[:, :, bass.ds(q * P, P)]))
                tell(dve, steps, staged)
                for u in range(U + 1):
                    if u < U:
                        e, i = units[u]
                        w = META + P * (i + 1)
                        lg = logit2[u % 2][:, 0:w]
                        dve.wait_ge(s_done.sem, s_done.ready(base + u))
                        dve.wait_ge(t_done.sem, t_done.free(base + u, 2))
                        hold()
                        steps(stt(lg, seam(2 + 2 * (u % 2), w), cum_tok[:, i, bass.ds(q * 2 + e, 1)],
                                  cum_row[:, q * 2 + e, 0:w], ALU.add, ALU.add))
                        steps.wait()
                        steps(V.tensor_tensor(lg[:, w - P:w], lg[:, w - P:w], causal[:], ALU.add))
                        sync()
                        steps(V.tensor_reduce(col[:, 2 + u % 2:3 + u % 2], lg, AX, ALU.max, negate=True))
                        tell(dve, steps, s_taken)
                    if u >= 1:
                        finish_unit(base, u - 1, logit2, META + P * (units[u - 1][1] + 1))
                dve.wait_ge(pv_done.sem, pv_done.ready(base + U - 1))
                hold()
                low_part(mix_low[:, q, :], bank(1), mix_high[:, q, :])
                tell(dve, steps, y_taken)
            dve.wait_ge(tile_done.sem, tile_done.ready(S_POOL))
            for g in range(4):
                steps(V.tensor_scalar(mix[:, 4 + g, :], bank(2 + g), vec[:, PS + g:PS + g + 1], None, ALU.mult))
                steps.wait()
                low_part(mix_low[:, 4 + g, :], mix[:, 4 + g, :], mix_high[:, 4 + g, :])
            tell(dve, steps, dense_dve)
            with steps.loop(2, 4) as q:
                for j in range(4):
                    m = q * 4 + j
                    dve.wait_ge(tile_done.sem, tile_done.ready(S_OUT2 + m))
                    steps(V.tensor_tensor(x[:, m, META:], bank(j % 2), x[:, m, META:], ALU.add))
                    tell(dve, steps, dense_dve)
            tell(dve, steps, x_ready)
            norm(4, META, vec[:, N2:N2 + KT], 3)
            with steps.loop(FF // 2, 6) as q:
                for j in range(2):
                    dve.wait_ge(tile_done.sem, tile_done.ready(S_UP + q * 4 + 2 * j + 1))
                    dve.wait_ge(up_silu.sem, up_silu.ready(q * 2 + j))
                    steps(V.tensor_tensor(act_ff[:, q * 2 + j, :], silu[j][:], bank(2 * j + 1), ALU.mult))
                    steps.wait()
                    low_part(act_low[:, q * 2 + j, :], act_ff[:, q * 2 + j, :], act_high[:, q * 2 + j, :])
                    tell(dve, steps, dense_dve)
            with steps.loop(2, 4) as q:
                for m in range(4):
                    dve.wait_ge(tile_done.sem, tile_done.ready(S_DOWN + q * 12 + 3 * m + 2))
                    steps(V.tensor_tensor(outb[:, q * 4 + m, :], bank(m % 2), x[:, q * 4 + m, META:], ALU.add))
                    tell(dve, steps, o_ready)


def tiles(w):
    k, m = w.shape
    return w.reshape(k // P, P, m // P, P).transpose(2, 1, 0, 3).reshape(m // P, P, k)


def columns(vector):
    return vector.reshape(-1, P).T


def kernel(**inputs):
    import numpy as np
    import concourse.bacc as bacc
    from concourse.bass_utils import run_bass_kernel_spmd

    a = {n: np.asarray(v) for n, v in inputs.items()}
    w_in = a["w_in"][0]
    cut = np.split(w_in, np.cumsum([512, 512, 512, 512, 64, 8, 512, 512, 512, 1024]), axis=1)
    qa, ka, va, qi, ki, wi, qb, kb, vb, ga, gb = cut
    w_in2 = a["w_in_2"][0]
    q2, k2, v2, fg, u2 = np.split(w_in2, np.cumsum([512, 512, 512, 8]), axis=1)
    pad = lambda w, m: np.concatenate([w, np.zeros((w.shape[0], m - w.shape[1]), w.dtype)], axis=1)
    both = np.concatenate([a["w_proj_a"][0], a["w_proj_b"][0]], axis=0)
    gate, up = tiles(a["w_gate_2"][0]), tiles(a["w_up_2"][0])
    down = tiles(a["w_down_2"][0])
    down = np.concatenate([down, np.zeros((KT, P, (24 - FF) * P), down.dtype)], axis=2)
    down = down.reshape(KT, P, 3, D).transpose(0, 2, 1, 3).reshape(3 * KT, P, D)
    pools = pad(a["w_pool_2"][0].transpose(1, 0, 2).reshape(P, 4 * P), D)[None]
    stream = np.concatenate([
        tiles(np.concatenate([qi, ka, qa, kb, qb], axis=1)), tiles(np.concatenate([ki, ki], axis=1)),
        tiles(pad(wi, P)), tiles(np.concatenate([va, vb, ga, gb], axis=1)), tiles(both),
        tiles(a["w_out"][0]), tiles(a["peer_wq"][0]), tiles(np.concatenate([q2, k2, u2, v2], axis=1)),
        tiles(pad(fg, P)), pools, tiles(a["w_out_2"][0]),
        np.stack([gate, up], axis=1).reshape(2 * FF, P, D), down], axis=0)
    assert stream.shape[0] == TILES, stream.shape
    twice = lambda w: np.concatenate([w, w])
    small = np.concatenate([
        columns(a["b_ada"][0]), columns(a["norm1_g"][0]), columns(a["norm2_g"][0]), columns(a["final_g"]),
        columns(a["norm1_w_2"][0]), columns(a["norm2_w_2"][0]), columns(twice(a["q_norm_w_2"][0])),
        columns(twice(a["k_norm_w_2"][0])), columns(a["pool_scale_2"][0]),
        np.concatenate([a["b_fgate_2"][0], np.zeros(P - NH, w_in.dtype)])[:, None],
        np.zeros((P, 1), w_in.dtype)], axis=1)
    dist = np.arange(REL) - (P - 1)
    far = BUCKETS // 2 + (np.log(np.maximum(dist, 1).astype(np.float32) / (BUCKETS // 2))
                          / np.float32(np.log(128 / (BUCKETS // 2))) * (BUCKETS // 2)).astype(np.int32)
    bucket = np.where(dist < BUCKETS // 2, np.maximum(dist, 0), np.minimum(far, BUCKETS - 1))
    onehot = (np.arange(BUCKETS)[:, None] == bucket[None]).astype(np.float32)
    arrays = {
        "xT": a["x"][0].T, "metaT": a["meta_tokens_2"].T, "cond": a["c"],
        "w_ada": a["w_ada"][0].T.reshape(ADA, P, D), "small": small, "onehot": onehot,
        "rel_bias": a["rel_bias"], "w_stream": stream,
        "sub_keys": a["peer_sub_keys"][0].reshape(2 * PH, NK, P).transpose(2, 0, 1),
        "experts": np.concatenate([a["peer_u"][0], a["peer_v"][0]], axis=1),
    }
    arrays = {n: np.ascontiguousarray(v) for n, v in arrays.items()}
    nc = bacc.Bacc("TRN2", target_bir_lowering=False, num_devices=1)
    args = [nc.dram_tensor(n, v.shape, mybir.dt.from_np(v.dtype), kind="ExternalInput").ap()
            for n, v in arrays.items()]
    out = nc.dram_tensor("outT", (D, T), mybir.dt.float32, kind="ExternalOutput").ap()
    program(nc, *args, out)
    r = run_bass_kernel_spmd(nc, [arrays], core_ids=[0])
    return np.ascontiguousarray(r.results[0]["outT"].T)[None]
```
